# Optimizing a Trainium2 kernel written in Bass

```python
import jax, jax.numpy as jnp
from jax import lax
import numpy as np

D_MODEL = 1024
BATCH = 1
SEQ = 512
DEPTH = 1
DEC_BATCH = 1
DEC_SEQ = 1024
PAST_LEN = 128

D_MIX = D_MODEL
A_WIDTH = D_MIX // 2
B_WIDTH = D_MIX - A_WIDTH
CHUNK = 128
A_HEADS = 4
A_HEAD_DIM = A_WIDTH // A_HEADS
POOL_WINDOWS = (2, 4, 8, 16)
B_GROUPS = len(POOL_WINDOWS)
B_GROUP_DIM = B_WIDTH // B_GROUPS
N_GROUPS = 4
EXPERTS_PER_GROUP = 8
N_EXPERTS = N_GROUPS * EXPERTS_PER_GROUP
TOP_K = 2
D_EXPERT = D_MODEL // 2
ROW_BLOCK = 128
N_MOD = 6
LN_EPS = 1e-5
ALPHA = (2.0 * DEPTH) ** 0.25
BETA = (8.0 * DEPTH) ** -0.25

kernel_name = "hybrid_sgu_pool_hmoe_encoder"

def layer_norm(x, g, b):
    xf = x.astype(jnp.float32)
    mu = jnp.mean(xf, axis=-1, keepdims=True)
    xc = xf - mu
    var = jnp.mean(xc * xc, axis=-1, keepdims=True)
    return (xc * lax.rsqrt(var + LN_EPS) * g + b).astype(x.dtype)

def multiscale_pool(p):
    bsz, s, _ = p.shape
    pg = p.reshape(bsz, s, B_GROUPS, B_GROUP_DIM).astype(jnp.float32)
    cs = jnp.concatenate([jnp.zeros((bsz, 1, B_GROUPS, B_GROUP_DIM), jnp.float32),
                          jnp.cumsum(pg, axis=1)], axis=1)
    t = jnp.arange(s)
    outs = []
    for g, w in enumerate(POOL_WINDOWS):
        lo = jnp.clip(t - w // 2, 0, s)
        hi = jnp.clip(t + w // 2, 0, s)
        win_sum = cs[:, hi, g] - cs[:, lo, g]
        cnt = (hi - lo).astype(jnp.float32)[None, :, None]
        outs.append(win_sum / cnt - pg[:, :, g])
    return jnp.stack(outs, axis=2).astype(p.dtype)

def token_mixer(h, w_in, v_norm_g, v_norm_b, w_spatial, b_spatial, w_pool, pool_scale, w_out):
    bsz, s, _ = h.shape
    z = h @ w_in
    za = jax.nn.gelu(z[..., :2 * A_WIDTH])
    u = za[..., :A_WIDTH]
    v = layer_norm(za[..., A_WIDTH:], v_norm_g, v_norm_b)
    v = v.reshape(bsz, s // CHUNK, CHUNK, A_HEADS, A_HEAD_DIM)
    v = jnp.einsum('hqp,bnphc->bnqhc', w_spatial, v) + b_spatial.T[:, :, None]
    a_out = u * v.reshape(bsz, s, A_WIDTH)
    pooled = multiscale_pool(z[..., 2 * A_WIDTH:])
    b_out = jnp.einsum('bsgc,gcd->bsgd', pooled, w_pool).reshape(bsz, s, B_WIDTH) * pool_scale
    return jnp.concatenate([a_out, b_out], axis=-1) @ w_out

def grouped_experts(h, e_id, e_w, w_gate_up, w_down):
    t_tok, d = h.shape
    tk = t_tok * TOP_K
    flat_e = e_id.reshape(-1)
    flat_w = e_w.reshape(-1)
    order = jnp.argsort(flat_e)
    sorted_e = flat_e[order]
    sorted_tok = (order // TOP_K).astype(jnp.int32)
    sorted_w = flat_w[order].astype(h.dtype)
    counts = jnp.bincount(flat_e, length=N_EXPERTS)
    padded = (counts + ROW_BLOCK - 1) // ROW_BLOCK * ROW_BLOCK
    seg_start = jnp.cumsum(counts) - counts
    pad_end = jnp.cumsum(padded)
    pad_start = pad_end - padded
    dest = pad_start[sorted_e] + jnp.arange(tk) - seg_start[sorted_e]
    n_blocks = -(-(tk + N_EXPERTS * (ROW_BLOCK - 1)) // ROW_BLOCK)
    rows = n_blocks * ROW_BLOCK
    buf_tok = jnp.full((rows,), t_tok, jnp.int32).at[dest].set(sorted_tok)
    buf_w = jnp.zeros((rows,), h.dtype).at[dest].set(sorted_w)
    block_e = jnp.minimum(jnp.searchsorted(pad_end, jnp.arange(n_blocks) * ROW_BLOCK, side='right'),
                          N_EXPERTS - 1)
    h_pad = jnp.concatenate([h, jnp.zeros((1, d), h.dtype)], axis=0)

    def block_fn(args):
        tok, w, e = args
        xb = h_pad[tok]
        gu = xb @ w_gate_up[e]
        y = (jax.nn.silu(gu[:, :D_EXPERT]) * gu[:, D_EXPERT:]) @ w_down[e]
        return y * w[:, None]

    yb = lax.map(block_fn, (buf_tok.reshape(n_blocks, ROW_BLOCK),
                            buf_w.reshape(n_blocks, ROW_BLOCK), block_e))
    out = jnp.zeros((t_tok + 1, d), h.dtype).at[buf_tok].add(yb.reshape(rows, d))
    return out[:t_tok]

def hierarchical_moe(h, w_route_group, b_route_group, w_route_expert, b_route_expert, w_gate_up, w_down):
    t_tok = h.shape[0]
    g_logits = (h @ w_route_group).astype(jnp.float32) + b_route_group
    g_prob = jax.nn.softmax(g_logits, axis=-1)
    g_idx = jnp.argmax(g_logits, axis=-1)
    g_w = jnp.take_along_axis(g_prob, g_idx[:, None], axis=-1)[:, 0]
    e_logits = (h @ w_route_expert).astype(jnp.float32).reshape(t_tok, N_GROUPS, EXPERTS_PER_GROUP) + b_route_expert
    e_logits = jnp.take_along_axis(e_logits, g_idx[:, None, None], axis=1)[:, 0]
    top_v, top_j = lax.top_k(e_logits, TOP_K)
    e_w = jax.nn.softmax(top_v, axis=-1) * g_w[:, None]
    e_id = g_idx[:, None].astype(jnp.int32) * EXPERTS_PER_GROUP + top_j.astype(jnp.int32)
    return grouped_experts(h, e_id, e_w, w_gate_up, w_down)

def encoder_layer(x, c, w_ada, b_ada, w_in, v_norm_g, v_norm_b, w_spatial, b_spatial, w_pool, pool_scale,
                  w_out, ln1_g, ln1_b, w_route_group, b_route_group, w_route_expert, b_route_expert,
                  w_gate_up, w_down, ln2_g, ln2_b):
    bsz, s, d = x.shape
    mod = (jax.nn.silu(c) @ w_ada + b_ada).reshape(bsz, 1, N_MOD, d)
    sh1, sc1, g1, sh2, sc2, g2 = (mod[:, :, i] for i in range(N_MOD))
    h = x * (1 + sc1) + sh1
    mix = token_mixer(h, w_in, v_norm_g, v_norm_b, w_spatial, b_spatial, w_pool, pool_scale, w_out)
    x = layer_norm(ALPHA * x + g1 * mix, ln1_g, ln1_b)
    h = x * (1 + sc2) + sh2
    y = hierarchical_moe(h.reshape(bsz * s, d), w_route_group, b_route_group, w_route_expert,
                         b_route_expert, w_gate_up, w_down).reshape(bsz, s, d)
    return layer_norm(ALPHA * x + g2 * y, ln2_g, ln2_b)

def trunk(x, c, w_ada, b_ada, w_in, v_norm_g, v_norm_b, w_spatial, b_spatial, w_pool, pool_scale,
          w_out, ln1_g, ln1_b, w_route_group, b_route_group, w_route_expert, b_route_expert,
          w_gate_up, w_down, ln2_g, ln2_b):
    for l in range(DEPTH):
        x = encoder_layer(x, c, w_ada[l], b_ada[l], w_in[l], v_norm_g[l], v_norm_b[l], w_spatial[l],
                          b_spatial[l], w_pool[l], pool_scale[l], w_out[l], ln1_g[l], ln1_b[l],
                          w_route_group[l], b_route_group[l], w_route_expert[l], b_route_expert[l],
                          w_gate_up[l], w_down[l], ln2_g[l], ln2_b[l])
    return x

def setup_inputs(seed: int = 0) -> dict:
    key = jax.random.key(seed)
    ks = jax.random.split(key, 26)
    L = DEPTH

    def nrm(k, shape, s):
        return jax.random.normal(k, shape, jnp.float32) * s

    return {
        "x_prompt": nrm(ks[0], (BATCH, SEQ, D_MODEL), 1.0),
        "x_sample": nrm(ks[1], (DEC_BATCH, DEC_SEQ, D_MODEL), 1.0),
        "c_prompt": nrm(ks[2], (BATCH, D_MODEL), 1.0),
        "c_sample": nrm(ks[3], (DEC_BATCH, D_MODEL), 1.0),
        "w_ada": nrm(ks[4], (L, D_MODEL, N_MOD * D_MODEL), D_MODEL ** -0.5),
        "b_ada": nrm(ks[5], (L, N_MOD * D_MODEL), 0.02),
        "w_in": nrm(ks[6], (L, D_MODEL, 2 * A_WIDTH + B_WIDTH), D_MODEL ** -0.5),
        "v_norm_g": 1.0 + nrm(ks[7], (L, A_WIDTH), 0.02),
        "v_norm_b": nrm(ks[8], (L, A_WIDTH), 0.02),
        "w_spatial": nrm(ks[9], (L, A_HEADS, CHUNK, CHUNK), CHUNK ** -0.5),
        "b_spatial": 1.0 + nrm(ks[10], (L, A_HEADS, CHUNK), 0.1),
        "w_pool": nrm(ks[11], (L, B_GROUPS, B_GROUP_DIM, B_GROUP_DIM), B_GROUP_DIM ** -0.5),
        "pool_scale": 1.0 + nrm(ks[12], (L, B_WIDTH), 0.1),
        "w_out": nrm(ks[13], (L, D_MIX, D_MODEL), BETA * D_MIX ** -0.5),
        "ln1_g": 1.0 + nrm(ks[14], (L, D_MODEL), 0.02),
        "ln1_b": nrm(ks[15], (L, D_MODEL), 0.02),
        "w_route_group": nrm(ks[16], (L, D_MODEL, N_GROUPS), D_MODEL ** -0.5),
        "b_route_group": nrm(ks[17], (L, N_GROUPS), 0.01),
        "w_route_expert": nrm(ks[18], (L, D_MODEL, N_EXPERTS), D_MODEL ** -0.5),
        "b_route_expert": nrm(ks[19], (L, N_GROUPS, EXPERTS_PER_GROUP), 0.01),
        "w_gate_up": nrm(ks[20], (L, N_EXPERTS, D_MODEL, 2 * D_EXPERT), D_MODEL ** -0.5),
        "w_down": nrm(ks[21], (L, N_EXPERTS, D_EXPERT, D_MODEL), BETA * D_EXPERT ** -0.5),
        "ln2_g": 1.0 + nrm(ks[22], (L, D_MODEL), 0.02),
        "ln2_b": nrm(ks[23], (L, D_MODEL), 0.02),
    }

def reference(x_prompt, x_sample, c_prompt, c_sample, w_ada, b_ada, w_in, v_norm_g, v_norm_b, w_spatial,
              b_spatial, w_pool, pool_scale, w_out, ln1_g, ln1_b, w_route_group, b_route_group,
              w_route_expert, b_route_expert, w_gate_up, w_down, ln2_g, ln2_b):
    y_prompt = trunk(x_prompt, c_prompt, w_ada, b_ada, w_in, v_norm_g, v_norm_b, w_spatial, b_spatial,
                     w_pool, pool_scale, w_out, ln1_g, ln1_b, w_route_group, b_route_group,
                     w_route_expert, b_route_expert, w_gate_up, w_down, ln2_g, ln2_b)
    y_sample = trunk(x_sample, c_sample, w_ada, b_ada, w_in, v_norm_g, v_norm_b, w_spatial, b_spatial,
                     w_pool, pool_scale, w_out, ln1_g, ln1_b, w_route_group, b_route_group,
                     w_route_expert, b_route_expert, w_gate_up, w_down, ln2_g, ln2_b)
    return (y_prompt, y_sample)


_drawn_inputs = setup_inputs


def setup_inputs(seed=0):
    import zlib

    import numpy as np

    out = dict(_drawn_inputs(seed))
    spreads = {}
    factors = {'v_norm_g': 5.944,
     'v_norm_b': 8.0,
     'b_route_group': 20.694,
     'b_route_expert': 13.566,
     'ln2_g': 7.961,
     'ln2_b': 8.214,
     'b_spatial': 3.036,
     'pool_scale': 2.76}
    for name, (base, spread) in spreads.items():
        noise = np.random.default_rng([zlib.crc32(name.encode()), seed]).standard_normal(out[name].shape)
        drawn = base * np.exp(spread * noise) if base else spread * noise
        out[name] = __import__('jax').numpy.asarray(drawn.astype(out[name].dtype))
    for name, factor in factors.items():
        out[name] = (out[name] * factor).astype(out[name].dtype)
    return out
```

```python
from contextlib import ExitStack

import concourse.bass as bass
from concourse import mybir

F32 = mybir.dt.float32
F32R = mybir.dt.float32r
I32 = mybir.dt.int32
ACT = mybir.ActivationFunctionType
ALU = mybir.AluOpType
AX = mybir.AxisListType

P = 128
D = 1024
KD = D // P
SEQS = (512, 1024)
T = sum(SEQS)
NT = T // P
SEQ_TILES = ((0, SEQS[0] // P), (SEQS[0] // P, NT))
AW = D // 2
HEADS = 4
WINDOWS = (2, 4, 8, 16)
NG = 4
EPG = 8
NE = NG * EPG
DE = D // 2
KE = DE // P
NMOD = 6
EPS = 1e-5
ALPHA = 2.0 ** 0.25
PAIRS = 2 * T
MAXBLK = (PAIRS + NE * P) // P
TAB = MAXBLK + 2
NO_ROW = 4096.0
FAR = 1e30
SILU_N = 512
CH = 4
N_ADA = NMOD * D // SILU_N


class Steps:

    def __init__(self, eng, sem, carrier):
        self.eng, self.sem, self.carrier, self.base, self.n = eng, sem, carrier, 0, 0

    def done(self, ins):
        ins.then_inc(self.sem, 1)
        self.n += 1

    def sync(self):
        self.eng.wait_ge(self.sem, self.base + self.n)

    def sync_apart(self):
        self.sync()
        self.eng.sem_inc(self.carrier, 1)

    def enter(self, i, per):
        self.start = self.base + self.n
        self.per = per
        self.base, self.n = self.start + i * per, 0

    def leave(self, count):
        assert self.n == self.per, (self.n, self.per)
        self.base, self.n = self.start + count * self.per, 0


def encoder(nc, ins, outs):
    ctx = ExitStack()
    with ctx:
        names = []

        def sem(name):
            names.append(name)
            return ctx.enter_context(nc.semaphore(name))

        base = (nc.sbuf_base + 63) // 64 * 64
        top = nc.sbuf_usable_end

        class Region:
            def __init__(self, start):
                self.at = start

            def take(self, name, shape, dt=F32):
                n = 4
                for s in shape[1:]:
                    n *= s
                t = nc.alloc_sbuf_tensor_at(name, list(shape), dt, offset=self.at)
                self.at += (n + 31) // 32 * 32
                assert self.at <= top, (name, self.at - top)
                return t

        KB = 1024
        W0 = base
        Z0 = W0 + 96 * KB
        C0 = Z0 + 48 * KB

        r = Region(W0)
        win_h = r.take("win_h", [P, KD, 3 * AW], F32R)
        win_l = r.take("win_l", [P, KD, 3 * AW], F32R)
        r = Region(W0)
        wout_h = r.take("wout_h", [P, KD, D], F32R)
        wout_l = r.take("wout_l", [P, KD, D], F32R)
        wout_raw = [r.take(f"wout_raw{s}", [P, D]) for s in range(4)]
        r = Region(W0)
        ring_h = [r.take(f"ring_h{s}", [P, 2048], F32R) for s in range(3)]
        ring_l = [r.take(f"ring_l{s}", [P, 2048], F32R) for s in range(3)]
        raw_hi = [r.take(f"raw{s}", [P, 2048]) for s in (4, 5)]
        raw = [r.take(f"raw{s}", [P, 2048]) for s in (0, 1, 2, 3)] + raw_hi
        assert r.at <= Z0

        r = Region(Z0)
        ada = [r.take(f"ada{s}", [P, CH, SILU_N]) for s in range(3)]
        b_ada_sb = r.take("b_ada_sb", [2, NMOD * D])
        r = Region(Z0)
        z2T = r.take("z2T", [P, NT, KD, P])
        r = Region(Z0)
        x1 = r.take("x1", [P, NT, D])

        r = Region(C0)
        ident = r.take("ident", [P, P])
        router_w = r.take("router_w", [P, KD, NG + NE])
        router_b = r.take("router_b", [P, NG + NE])
        half_neg = r.take("half_neg", [P, 1])
        C1 = r.at
        TOP0 = top // 32 * 32 - 3328
        r = Region(TOP0)
        logits = r.take("logits", [P, NT, NG + NE])
        table = r.take("table", [P, 3, TAB])
        table_i = r.take("table_i", [P, 2, TAB], I32)
        block_e = r.take("block_e", [1, TAB], I32)
        block_n = r.take("block_n", [1, 1], I32)
        r = Region(C1)
        bands = r.take("bands", [P, 3, len(WINDOWS), P])
        band_prev = r.take("band_prev", [P, len(WINDOWS), P])
        band_next = r.take("band_next", [P, len(WINDOWS), P])
        w_spT = r.take("w_spT", [P, HEADS, P])
        b_sp = r.take("b_sp", [P, HEADS])
        w_pool = r.take("w_pool", [P, len(WINDOWS), P])
        pool_s = r.take("pool_s", [P, len(WINDOWS)])
        vg = r.take("vg", [P, AW])
        vb = r.take("vb", [P, AW])
        B0 = r.at
        sc1 = r.take("sc1", [P, D])
        sh1 = r.take("sh1", [P, D])
        xs = r.take("xs", [P, D])
        hT_h = [r.take(f"hT_h{s}", [P, KD, P], F32R) for s in range(2)]
        hT_l = [r.take(f"hT_l{s}", [P, KD, P], F32R) for s in range(2)]
        u_sb = r.take("u_sb", [P, AW])
        v_sb = r.take("v_sb", [P, AW])
        a_sb = r.take("a_sb", [P, AW])
        p_sb = [r.take(f"p_sb{s}", [P, AW]) for s in range(2)]
        p_old = r.take("p_old", [P, AW])
        pooledT = r.take("pooledT", [P, len(WINDOWS), P])
        v_stat = r.take("v_stat", [P, 6])
        v_mv = r.take("v_mv", [P, 2])
        v_rstd = r.take("v_rstd", [P, 1])
        r = Region(B0)
        mod = r.take("mod", [2, NMOD * D])
        win_raw = [r.take(f"win_raw{s}", [P, 3 * AW]) for s in range(2)]
        c_in = r.take("c_in", [2 * KD, P])
        c_act = r.take("c_act", [2 * KD, P])
        cT = r.take("cT", [P, 2 * KD])
        r = Region(C1)
        z2_h = [r.take(f"z2_h{s}", [P, KD, P], F32R) for s in range(2)]
        z2_l = [r.take(f"z2_l{s}", [P, KD, P], F32R) for s in range(2)]
        xr = r.take("xr", [P, D])
        res = r.take("res", [P, D])
        h2 = r.take("h2", [P, D])
        h2T = r.take("h2T", [P, KD, P])
        g1b = r.take("g1b", [P, D])
        sc2b = r.take("sc2b", [P, D])
        sh2b = r.take("sh2b", [P, D])
        ln_g = r.take("ln_g", [P, D])
        ln_b = r.take("ln_b", [P, D])
        stat = r.take("stat", [P, 2, 6])
        mv = r.take("mv", [P, 2])
        rstd = r.take("rstd", [P, 1])
        nmr = r.take("nmr", [P, 1])
        r = Region(C1)
        tri = r.take("tri", [P, P])
        ones = r.take("ones", [P, P])
        iota_p = r.take("iota_p", [P, 1])
        iota_r = r.take("iota_r", [P, P])
        rev = r.take("rev", [P, NE])
        tok = r.take("tok", [P, 2, NT])
        gmax = r.take("gmax", [P, NT])
        gw = r.take("gw", [P, NT])
        g_a = r.take("g_a", [P, NT, NG])
        g_b = r.take("g_b", [P, NT, NG])
        gm = r.take("gm", [P, NT])
        e2 = r.take("e2", [P, NT, NE])
        e_t = r.take("e_t", [P, NT, NE])
        oh = [r.take(f"oh{k}", [P, NT, NE]) for k in range(2)]
        both = r.take("both", [P, NT, NE])
        v1 = r.take("v1", [P, NT])
        v2 = r.take("v2", [P, NT])
        em = r.take("em", [P, NT])
        ex = r.take("ex", [P, NT])
        den = r.take("den", [P, NT])
        vals = r.take("vals", [P, 3, 2, NT])
        before = r.take("before", [P, NT + 1, NE])
        pos = r.take("pos", [P, NT, NE])
        cmp = r.take("cmp", [P, NE, NT])
        nblk = r.take("nblk", [P, NE])
        cum = [r.take(f"cum{k}", [P, NE]) for k in range(2)]
        cmp_e = r.take("cmp_e", [1, TAB, NE])
        eid_f = r.take("eid_f", [1, TAB])
        slot_f = r.take("slot_f", [P, 2, NT])
        slot_i = r.take("slot_i", [P, 2, NT], I32)
        blk_i = r.take("blk_i", [P, 2, NT], I32)
        in_i = r.take("in_i", [P, 2, NT], I32)
        blk_f = r.take("blk_f", [P, 2, NT])
        in_f = r.take("in_f", [P, 2, NT])
        pick_r = [r.take(f"pick_r{s}", [P, P]) for s in range(2)]
        pick_b = [r.take(f"pick_b{s}", [P, 3, TAB]) for s in range(2)]
        r = Region(C1)
        xg = r.take("xg", [P, D])
        xT_h = r.take("xT_h", [P, KD, P], F32R)
        xT_l = r.take("xT_l", [P, KD, P], F32R)
        act_s = r.take("act_s", [P, DE // 2])
        act_a = r.take("act_a", [P, DE])
        aT_h = r.take("aT_h", [P, KE, P], F32R)
        aT_l = r.take("aT_l", [P, KE, P], F32R)
        y_sb = r.take("y_sb", [P, D])
        g_idx = r.take("g_idx", [P, 1], I32)
        s_idx = r.take("s_idx", [P, 1], I32)
        s_w = r.take("s_w", [P, 1])
        r = Region(W0)
        y0 = [r.take(f"y0_{s}", [P, D]) for s in range(2)]
        y1 = [r.take(f"y1_{s}", [P, D]) for s in range(2)]
        fin = [r.take(f"fin{s}", [P, D]) for s in range(2)]
        g2b = [r.take(f"g2b{q}", [P, D]) for q in range(2)]
        ln2_g = r.take("ln2_gb", [P, D])
        ln2_b = r.take("ln2_bb", [P, D])
        stat2 = r.take("stat2", [P, 2, 6])
        mv2 = r.take("mv2", [P, 2])
        rstd2 = r.take("rstd2", [P, 1])
        nmr2 = r.take("nmr2", [P, 1])

        ps = [ctx.enter_context(nc.psum_tensor(f"bank{b}", [P, 512], F32)) for b in range(8)]

        mod_d = nc.dram_tensor("mod_rows", (2, NMOD * D), F32).ap()
        h2_d = nc.dram_tensor("h2_rows", (T, D), F32).ap()
        y_d = nc.dram_tensor("y_rows", (PAIRS, D), F32).ap()

        x_in = (ins["x_prompt"][0], ins["x_sample"][0])
        y_out = (outs[0][0], outs[1][0])

        def x_rows(q, t):
            return x_in[q][bass.ds((t - SEQ_TILES[q][0]) * P, P), :]

        def bcast(row, n):
            return row.to_broadcast([P, n])

        w_ada = ins["w_ada"][0].rearrange("(k p) n -> p k n", p=P)
        w_in = ins["w_in"][0].rearrange("(k p) n -> p k n", p=P)
        w_out = ins["w_out"][0].rearrange("(k p) n -> p k n", p=P)
        w_gu = ins["w_gate_up"][0].rearrange("e (k p) (s n) -> e p k s n", p=P, s=2)
        w_dn = ins["w_down"][0].rearrange("e (k p) n -> e p k n", p=P)

        S = {n: sem(n) for n in (
            "c_loaded small_loaded ada_bias c_silu cT_made cT_copied ident_made ident_zero"
            " consts_made mod_row mod_stored wsp_loaded wspT_made wspT_copied band_edge"
            " band_made bands_ready win_h_made win_l_made"
            " mod1_loaded x_loaded h_ready xT_made hT_h_made hT_l_made v_made v_gelu v_stats v_rs"
            " v_normed u_made u_gelu p_made p_kept p_copied s_made a_ready aT_made aT_copied pooled"
            " pooled_copied b_made b_copied"
            " mod2_loaded xr_loaded wout_h_made wout_l_made z2_h_made z2_l_made mix_made res_normed"
            " res_ready var_ready rstd_ready shift_ready x1_ready h2_ready h2_stored h2T_made h2T_copied"
            " logit_made logit_read mod2_used"
            " rt_consts g_shifted g_exp top_diff top_exp sel_ready ranks_made pick_ready pick_used"
            " tab_made tab_ready eid_ready"
            " idx_ready gathered xgT_made xT_h_made xT_l_made chunk_h chunk_l chunk_used"
            " silu_made act_ready aT_e_made aT_h_made aT_l_made y_ready y_idx"
            " y_scattered"
            " last_loaded y0_loaded_0 y0_loaded_1 f_var f_rstd f_normed f_ready f_stored_0 f_stored_1"
            " f_scaled dve_steps pool_steps dve_carrier pool_carrier"
        ).split()}
        ada_loaded = [sem(f"ada_loaded{s}") for s in range(3)]
        ada_used = sem("ada_used")
        win_loaded = [sem(f"win_loaded{k}") for k in range(KD)]
        wout_loaded = [sem(f"wout_loaded{k}") for k in range(KD)]
        raw_loaded = [sem(f"raw_loaded{s}") for s in range(6)]

        block = ctx.enter_context(nc.Block())

        HC = DE // 2

        def chunk_src(e, c):
            if c < 4:
                half, kk = c // 2, c % 2
                return [(w_gu[e, :, bass.ds(4 * kk, 4), s, bass.ds(HC * half, HC)], s) for s in range(2)]
            return [(w_dn[e, :, bass.ds(2 * (c - 4), 2), :], None)]

        @block.sync
        def _(sp):
            sp.dma_start(c_in[0:KD, :], ins["c_prompt"].rearrange("a (k p) -> (a k) p", p=P)).then_inc(S["c_loaded"], 16)
            sp.dma_start(c_in[KD:2 * KD, :], ins["c_sample"].rearrange("a (k p) -> (a k) p", p=P)).then_inc(S["c_loaded"], 16)
            sp.dma_start(b_ada_sb[:], ins["b_ada"].to_broadcast([2, NMOD * D])).then_inc(S["ada_bias"], 16)
            n = 0
            for j in range(N_ADA):
                for kk in range(KD // CH):
                    if n >= 3:
                        sp.wait_ge(ada_used, n - 2)
                    sp.dma_start(ada[n % 3][:], w_ada[:, kk * CH:(kk + 1) * CH, j * SILU_N:(j + 1) * SILU_N]).then_inc(ada_loaded[n % 3], 16)
                    n += 1
                if j == 0:
                    for dst, src in ((vg[:], bcast(ins["v_norm_g"], AW)), (vb[:], bcast(ins["v_norm_b"], AW)),
                                     (w_pool[:], ins["w_pool"][0].rearrange("g c d -> c g d")),
                                     (router_w[:, :, 0:NG], ins["w_route_group"][0].rearrange("(k p) n -> p k n", p=P)),
                                     (router_w[:, :, NG:NG + NE], ins["w_route_expert"][0].rearrange("(k p) n -> p k n", p=P)),
                                     (router_b[:, 0:NG], bcast(ins["b_route_group"], NG)),
                                     (router_b[:, NG:NG + NE], bcast(ins["b_route_expert"].rearrange("a g e -> a (g e)"), NE))):
                        sp.dma_start(dst, src).then_inc(S["small_loaded"], 16)
                    with nc.allow_non_contiguous_dma(reason="1024 words in all"):
                        sp.dma_start(b_sp[:], ins["b_spatial"][0].rearrange("h q -> q h")).then_inc(S["small_loaded"], 16)
                        sp.dma_start(pool_s[:], ins["pool_scale"][0].rearrange("(g c) -> c g", c=P)).then_inc(S["small_loaded"], 16)
                    sp.dma_start(w_spT[:], ins["w_spatial"][0].rearrange("h q p -> q h p")).then_inc(S["wsp_loaded"], 16)
            for k in range(KD):
                if k >= 2:
                    sp.wait_ge(S["win_l_made"], k - 1)
                sp.dma_start(win_raw[k % 2][:], w_in[:, k, :]).then_inc(win_loaded[k], 16)
            sp.wait_ge(S["mod_row"], N_ADA)
            sp.dma_start(mod_d, mod[:]).then_inc(S["mod_stored"], 16)
            sp.wait_ge(S["mod_stored"], 16)

            def load_mod1(q):
                sp.dma_start(sc1[:], bcast(mod_d[q:q + 1, D:2 * D], D)).then_inc(S["mod1_loaded"], 16)
                sp.dma_start(sh1[:], bcast(mod_d[q:q + 1, 0:D], D)).then_inc(S["mod1_loaded"], 16)

            def load_x(t, q):
                sp.wait_ge(S["xT_made"], t)
                sp.dma_start(xs[:], x_rows(q, t)).then_inc(S["x_loaded"], 16)

            load_mod1(0)
            sp.dma_start(xs[:], x_rows(0, 0)).then_inc(S["x_loaded"], 16)
            for t in range(1, 4):
                load_x(t, 0)
            sp.wait_ge(S["h_ready"], 4)
            load_mod1(1)
            with sp.Fori(4, NT) as t:
                load_x(t, 1)
            for k in range(KD):
                if k >= 4:
                    sp.wait_ge(S["wout_l_made"], k - 3)
                elif k == 0:
                    sp.wait_ge(S["p_made"], NT)
                sp.dma_start(wout_raw[k % 4][:], w_out[:, k, :]).then_inc(wout_loaded[k], 16)
            sp.wait_ge(S["b_copied"], NT)
            sp.wait_ge(S["aT_copied"], NT)

            def load_mod2(q):
                for dst, m in ((g1b, 2), (sc2b, 4), (sh2b, 3)):
                    sp.dma_start(dst[:], bcast(mod_d[q:q + 1, m * D:(m + 1) * D], D)).then_inc(S["mod2_loaded"], 16)

            sp.dma_start(ln_g[:], bcast(ins["ln1_g"], D)).then_inc(S["mod2_loaded"], 16)
            sp.dma_start(ln_b[:], bcast(ins["ln1_b"], D)).then_inc(S["mod2_loaded"], 16)
            load_mod2(0)

            def second(t, q, first=False):
                if not first:
                    sp.wait_ge(S["res_ready"], t)
                sp.dma_start(xr[:], x_rows(q, t)).then_inc(S["xr_loaded"], 16)

            def store_h2(t):
                sp.wait_ge(S["h2_ready"], t + 1)
                sp.dma_start(h2_d[bass.ds(t * P, P), :], h2[:]).then_inc(S["h2_stored"], 16)

            second(0, 0, first=True)
            with sp.Fori(1, 4) as t:
                second(t, 0)
                store_h2(t - 1)
            store_h2(3)
            load_mod2(1)
            second(4, 1)
            with sp.Fori(5, NT) as t:
                second(t, 1)
                store_h2(t - 1)
            store_h2(NT - 1)

            def load_chunk(e, i, c, wait=True):
                s = c
                if wait:
                    sp.wait_ge(S["chunk_l"], 6 * i + c - 5)
                for src, part in chunk_src(e, c):
                    dst = raw[s][:].rearrange("p (k s n) -> p k s n", k=4, s=2)[:, :, part, :] if part is not None \
                        else raw[s][:].rearrange("p (k n) -> p k n", k=2)
                    sp.dma_start(dst, src).then_inc(raw_loaded[s], 16)

            sp.wait_ge(S["wout_l_made"], KD)
            for c in range(4):
                load_chunk(0, 0, c, wait=False)
            sp.wait_ge(S["mix_made"], NT)
            for c in (4, 5):
                load_chunk(0, 0, c, wait=False)
            sp.wait_ge(S["eid_ready"], 1)
            n_blocks = sp.value_load(block_n[0:1, 0:1], min_val=NE, max_val=MAXBLK)

            def expert_of(i):
                return sp.value_load(block_e[0:1, bass.ds(i, 1)], min_val=0, max_val=NE - 1)

            e = expert_of(1)
            for c in range(2):
                load_chunk(e, 1, c)
            with sp.Fori(1, n_blocks) as i:
                e = expert_of(i)
                for c in range(2, 6):
                    load_chunk(e, i, c)
                e = expert_of(i + 1)
                for c in range(2):
                    load_chunk(e, i + 1, c)

            sp.wait_ge(S["y_ready"], n_blocks)
            sp.wait_ge(S["chunk_l"], 6 * n_blocks + 2)
            for dst, src in ((g2b[0], mod_d[0:1, 5 * D:6 * D]), (g2b[1], mod_d[1:2, 5 * D:6 * D]),
                             (ln2_g, ins["ln2_g"]), (ln2_b, ins["ln2_b"])):
                sp.dma_start(dst[:], bcast(src, D)).then_inc(S["last_loaded"], 16)
            sp.wait_ge(S["y_scattered"], n_blocks * 16)
            yl = [S["y0_loaded_0"], S["y0_loaded_1"]]

            def load_y(t, s):
                sp.dma_start(y0[s][:], y_d[bass.ds(t * P, P), :]).then_inc(yl[s], 16)
                sp.dma_start(y1[s][:], y_d[bass.ds(T + t * P, P), :]).then_inc(yl[s], 16)

            def store_y(t, s, q):
                sp.wait_ge(S["f_ready"], t + 1)
                sp.dma_start(y_out[q][bass.ds((t - SEQ_TILES[q][0]) * P, P), :], fin[s][:]).then_inc(S[f"f_stored_{s}"], 16)

            load_y(0, 0)
            load_y(1, 1)
            for q, (lo, hi) in enumerate(SEQ_TILES):
                last = hi if hi < NT else NT - 2
                with sp.Fori(lo // 2, last // 2) as i:
                    for s in range(2):
                        store_y(2 * i + s, s, q)
                        load_y(2 * i + s + 2, s)
            for s in range(2):
                store_y(NT - 2 + s, s, 1)
            for s in range(2):
                sp.wait_ge(S[f"f_stored_{s}"], 16 * NT // 2)

        @block.gpsimd
        def _(pool):
            st = Steps(pool, S["pool_steps"], S["pool_carrier"])
            st.done(pool.memset(ident[:], 0.0))
            st.sync()
            nc.gpsimd.affine_select(out=ident[:], in_=ident[:], compare_op=ALU.not_equal, fill=1.0, base=0,
                                    pattern=[[-1, P]], channel_multiplier=1).then_inc(S["ident_made"], 1)
            st.done(pool.memset(half_neg[:], -0.5))
            nc.gpsimd.iota(band_prev[:, 0, :], pattern=[[1, P]], base=0, channel_multiplier=0,
                           allow_small_or_imprecise_dtypes=True).then_inc(S["consts_made"], 1)
            pool.wait_ge(S["band_edge"], 1)
            for g, w in enumerate(WINDOWS):
                h = w // 2
                for b, shift in [(bands[:, v, g, :], 0) for v in range(3)] + [(band_prev[:, g, :], -P), (band_next[:, g, :], P)]:
                    st.done(nc.gpsimd.affine_select(out=b, in_=b, compare_op=ALU.is_ge, fill=0.0, base=shift + h,
                                                    pattern=[[-1, P]], channel_multiplier=1))
                    st.sync()
                    nc.gpsimd.affine_select(out=b, in_=b, compare_op=ALU.is_gt, fill=0.0, base=h - shift,
                                            pattern=[[1, P]], channel_multiplier=-1).then_inc(S["band_made"], 1)

            def modulate(t):
                if isinstance(t, int) and t == 0:
                    pool.wait_ge(S["mod1_loaded"], 32)
                    st.done(nc.gpsimd.tensor_scalar(sc1[:], sc1[:], 1.0, None, ALU.add))
                    st.sync()
                if isinstance(t, int) and t == 4:
                    pool.wait_ge(S["mod1_loaded"], 64)
                    st.done(nc.gpsimd.tensor_scalar(sc1[:], sc1[:], 1.0, None, ALU.add))
                    st.sync()
                pool.wait_ge(S["x_loaded"], 16 * (t + 1))
                st.done(nc.gpsimd.tensor_tensor(xs[:], xs[:], sc1[:], ALU.mult))
                st.sync()
                nc.gpsimd.tensor_tensor(xs[:], xs[:], sh1[:], ALU.add).then_inc(S["h_ready"], 1)

            def v_power(t):
                pool.wait_ge(S["v_stats"], t + 1)
                nc.gpsimd.tensor_tensor(v_rstd[:], v_mv[:, 1:2], half_neg[:], ALU.pow).then_inc(S["v_rs"], 1)

            modulate(0)
            modulate(1)
            for t in (0, 1, 2):
                v_power(t)
                modulate(t + 2)
            with pool.Fori(3, NT - 2) as t:
                st.enter(t - 3, 1)
                v_power(t)
                modulate(t + 2)
            st.leave(NT - 5)
            v_power(NT - 2)
            v_power(NT - 1)

            def second(t):
                pool.wait_ge(S["var_ready"], t + 1)
                nc.gpsimd.tensor_tensor(rstd[:], mv[:, 1:2], half_neg[:], ALU.pow).then_inc(S["rstd_ready"], 1)
                pool.wait_ge(S["x1_ready"], t + 1)
                if not (isinstance(t, int) and t == 0):
                    pool.wait_ge(S["h2_stored"], 16 * t)
                    pool.wait_ge(S["h2T_made"], t)
                st.done(nc.gpsimd.tensor_tensor(h2[:], x1[:, t, :] if isinstance(t, int) else x1[:, bass.ds(t, 1), :].rearrange("p a n -> p (a n)"), sc2b[:], ALU.mult))
                st.sync()
                nc.gpsimd.tensor_tensor(h2[:], h2[:], sh2b[:], ALU.add).then_inc(S["h2_ready"], 1)

            def plus_one(n):
                pool.wait_ge(S["mod2_loaded"], 16 * n)
                st.done(nc.gpsimd.tensor_scalar(sc2b[:], sc2b[:], 1.0, None, ALU.add))
                st.sync()

            plus_one(5)
            second(0)
            with pool.Fori(1, 4) as t:
                st.enter(t - 1, 1)
                second(t)
            st.leave(3)
            plus_one(8)
            with pool.Fori(4, NT) as t:
                st.enter(t - 4, 1)
                second(t)
            st.leave(NT - 4)

            pool.wait_ge(S["logit_read"], NT)
            pool.wait_ge(S["h2_stored"], 16 * NT)
            st.done(pool.memset(ones[:], 1.0))
            st.done(pool.memset(tri[:], 1.0))
            st.sync()
            nc.gpsimd.affine_select(out=tri[:], in_=tri[:], compare_op=ALU.is_gt, fill=0.0, base=0,
                                    pattern=[[1, P]], channel_multiplier=-1).then_inc(S["rt_consts"], 1)
            nc.gpsimd.iota(iota_r[:], pattern=[[1, P]], base=0, channel_multiplier=0,
                           allow_small_or_imprecise_dtypes=True).then_inc(S["rt_consts"], 1)
            nc.gpsimd.iota(rev[:], pattern=[[-1, NE]], base=NE, channel_multiplier=0,
                           allow_small_or_imprecise_dtypes=True).then_inc(S["rt_consts"], 1)
            nc.gpsimd.iota(tok[:], pattern=[[T, 2], [P, NT]], base=0, channel_multiplier=1,
                           allow_small_or_imprecise_dtypes=True).then_inc(S["rt_consts"], 1)
            nc.gpsimd.iota(cmp_e[:], pattern=[[1, TAB], [0, NE]], base=0, channel_multiplier=0,
                           allow_small_or_imprecise_dtypes=True).then_inc(S["rt_consts"], 1)
            nc.gpsimd.iota(cmp[:], pattern=[[0, NE], [P, NT]], base=0, channel_multiplier=0,
                           allow_small_or_imprecise_dtypes=True).then_inc(S["rt_consts"], 1)

            pool.wait_ge(S["tab_ready"], 1)
            pool.wait_ge(S["eid_ready"], 1)
            n_blocks = pool.value_load(block_n[0:1, 0:1], min_val=NE, max_val=MAXBLK)

            def gather(i, first=False):
                if not first:
                    pool.wait_ge(S["gathered"], 16 * i)
                    pool.wait_ge(S["xgT_made"], i)
                nc.gpsimd.tensor_copy(g_idx[:], table_i[:, 0, bass.ds(i, 1)]).then_inc(S["idx_ready"], 1)
                pool.wait_ge(S["idx_ready"], i + 1)
                pool.sem_inc(S["pool_carrier"], 1)
                nc.gpsimd.indirect_dma_start(out=xg[:], out_offset=None, in_=h2_d,
                                             in_offset=bass.IndirectOffsetOnAxis(ap=g_idx[:, 0:1], axis=0)).then_inc(S["gathered"], 16)

            def scatter(i, first=False):
                if not first:
                    pool.wait_ge(S["y_scattered"], 16 * i)
                    pool.wait_ge(S["y_ready"], i)
                nc.gpsimd.tensor_copy(s_idx[:], table_i[:, 1, bass.ds(i, 1)]).then_inc(S["y_idx"], 1)
                nc.gpsimd.tensor_copy(s_w[:], table[:, 2, bass.ds(i, 1)]).then_inc(S["y_idx"], 1)
                pool.wait_ge(S["y_idx"], 2 * (i + 1))
                pool.wait_ge(S["y_ready"], i + 1)
                pool.sem_inc(S["pool_carrier"], 1)
                nc.gpsimd.indirect_dma_start(out=y_d, out_offset=bass.IndirectOffsetOnAxis(ap=s_idx[:, 0:1], axis=0),
                                             in_=y_sb[:], in_offset=None, bounds_check=PAIRS - 1,
                                             oob_is_err=False).then_inc(S["y_scattered"], 16)

            gather(0, first=True)
            gather(1)
            gather(2)
            scatter(0, first=True)
            with pool.Fori(1, n_blocks) as i:
                gather(i + 2)
                scatter(i)
            pool.wait_ge(S["gathered"], 16 * (n_blocks + 2))
            pool.sem_inc(S["pool_carrier"], 1)

            with pool.Fori(0, NT) as t:
                pool.wait_ge(S["f_var"], t + 1)
                nc.gpsimd.tensor_tensor(rstd2[:], mv2[:, 1:2], half_neg[:], ALU.pow).then_inc(S["f_rstd"], 1)

        @block.scalar
        def _(act):
            act.wait_ge(S["c_loaded"], 32)
            nc.scalar.activation(c_act[:], c_in[:], ACT.Silu).then_inc(S["c_silu"], 1)
            act.wait_ge(S["cT_made"], 1)
            nc.scalar.activation(cT[:], ps[0][:, 0:2 * KD], ACT.Copy).then_inc(S["cT_copied"], 1)
            act.wait_ge(S["wspT_made"], 1)
            nc.scalar.activation(w_spT[:], ps[1][:].rearrange("p (h q) -> p h q", h=HEADS), ACT.Copy).then_inc(S["wspT_copied"], 1)
            for k in range(KD):
                act.wait_ge(win_loaded[k], 16)
                nc.scalar.activation(win_h[:, k, :], win_raw[k % 2][:], ACT.Copy).then_inc(S["win_h_made"], 1)

            def high_x(t, s):
                act.wait_ge(S["xT_made"], t + 1)
                if not (isinstance(t, int) and t < 2):
                    act.wait_ge(S["p_made"], t - 1)
                for b in range(2):
                    last = nc.scalar.activation(hT_h[s][:, 4 * b:4 * b + 4, :], ps[b][:].rearrange("p (k m) -> p k m", k=4), ACT.Copy)
                last.then_inc(S["hT_h_made"], 1)

            def z_tile(t, s, nxt, prev):
                act.wait_ge(S["v_made"], t + 1)
                if not (isinstance(t, int) and t == 0):
                    act.wait_ge(S["s_made"], t)
                nc.scalar.activation(v_sb[:], ps[2][:], ACT.Gelu_apprx_tanh).then_inc(S["v_gelu"], 1)
                if nxt:
                    high_x(t + 1, 1 - s)
                act.wait_ge(S["u_made"], t + 1)
                if not (isinstance(t, int) and t == 0):
                    act.wait_ge(S["a_ready"], t)
                nc.scalar.activation(u_sb[:], ps[3][:], ACT.Gelu_apprx_tanh).then_inc(S["u_gelu"], 1)
                if prev:
                    copy_aT(t - 1)
                act.wait_ge(S["p_made"], t + 1)
                if not (isinstance(t, int) and t < 2):
                    act.wait_ge(S["p_kept"], t - 1)
                nc.scalar.activation(p_sb[s][:], ps[4][:], ACT.Copy).then_inc(S["p_copied"], 1)

            def copy_aT(t):
                act.wait_ge(S["aT_made"], t + 1)
                dst = z2T[:, t, 0:4, :] if isinstance(t, int) else z2T[:, bass.ds(t, 1), 0:4, :].rearrange("p a k m -> p (a k) m")
                nc.scalar.activation(dst, ps[6][:].rearrange("p (k m) -> p k m", k=4), ACT.Copy).then_inc(S["aT_copied"], 1)

            high_x(0, 0)
            z_tile(0, 0, True, False)
            z_tile(1, 1, True, True)
            with act.Fori(1, NT // 2 - 1) as i:
                for s in range(2):
                    z_tile(2 * i + s, s, True, True)
            z_tile(NT - 2, 0, True, True)
            z_tile(NT - 1, 1, False, True)
            copy_aT(NT - 1)

            for k in range(KD):
                act.wait_ge(wout_loaded[k], 16)
                nc.scalar.activation(wout_h[:, k, :], wout_raw[k % 4][:], ACT.Copy).then_inc(S["wout_h_made"], 1)
            act.wait_ge(S["b_copied"], NT)

            def high_z(t, s):
                if not (isinstance(t, int) and t < 2):
                    act.wait_ge(S["mix_made"], t - 1)
                src = z2T[:, t, :, :] if isinstance(t, int) else z2T[:, bass.ds(t, 1), :, :].rearrange("p a k m -> p (a k) m")
                nc.scalar.activation(z2_h[s][:], src, ACT.Copy).then_inc(S["z2_h_made"], 1)

            def normalise(t):
                act.wait_ge(S["shift_ready"], t + 1)
                nc.scalar.activation(res[:], res[:], ACT.Identity, scale=rstd[:, 0:1], bias=nmr[:, 0:1]).then_inc(S["res_normed"], 1)

            def copy_h2T(t):
                act.wait_ge(S["h2T_made"], t + 1)
                if not (isinstance(t, int) and t == 0):
                    act.wait_ge(S["logit_made"], t)
                for b in range(2):
                    last = nc.scalar.activation(h2T[:, 4 * b:4 * b + 4, :], ps[4 + b][:].rearrange("p (k m) -> p k m", k=4), ACT.Copy)
                last.then_inc(S["h2T_copied"], 1)

            high_z(0, 0)
            high_z(1, 1)
            for t in range(2):
                normalise(t)
                high_z(t + 2, t)
                copy_h2T(t)
            with act.Fori(1, NT // 2 - 1) as i:
                for s in range(2):
                    normalise(2 * i + s)
                    high_z(2 * i + s + 2, s)
                    copy_h2T(2 * i + s)
            for t in (NT - 2, NT - 1):
                normalise(t)
                copy_h2T(t)

            act.wait_ge(S["g_shifted"], 1)
            nc.scalar.activation(g_a[:], g_a[:], ACT.Exp).then_inc(S["g_exp"], 1)
            act.wait_ge(S["top_diff"], 1)
            nc.scalar.activation(ex[:], v2[:], ACT.Exp).then_inc(S["top_exp"], 1)

            def high_chunk(i, c, first=False):
                act.wait_ge(raw_loaded[c], (32 if c < 4 else 16) * (i + 1))
                if not first:
                    act.wait_ge(S["chunk_used"], 6 * i + c - 2)
                nc.scalar.activation(ring_h[c % 3][:], raw[c][:], ACT.Copy).then_inc(S["chunk_h"], 1)

            def silu(i, half):
                act.wait_ge(S["chunk_used"], 6 * i + 2 * half + 2)
                if not (isinstance(i, int) and i == 0 and half == 0):
                    act.wait_ge(S["act_ready"], 2 * i + half)
                nc.scalar.activation(act_s[:], ps[half][:, 0:HC], ACT.Silu).then_inc(S["silu_made"], 1)

            def high_aT(i, half):
                act.wait_ge(S["aT_e_made"], 2 * i + half + 1)
                nc.scalar.activation(aT_h[:, 2 * half:2 * half + 2, :], ps[4][:, HC * half:HC * (half + 1)].rearrange("p (k m) -> p k m", k=2), ACT.Copy).then_inc(S["aT_h_made"], 1)

            def high_xT(i):
                act.wait_ge(S["xgT_made"], i + 1)
                for b in range(2):
                    last = nc.scalar.activation(xT_h[:, 4 * b:4 * b + 4, :], ps[2 + b][:].rearrange("p (k m) -> p k m", k=4), ACT.Copy)
                last.then_inc(S["xT_h_made"], 1)

            act.wait_ge(S["mix_made"], NT)
            for c in range(2):
                high_chunk(0, c, first=True)
            act.wait_ge(S["eid_ready"], 1)
            n_blocks = act.value_load(block_n[0:1, 0:1], min_val=NE, max_val=MAXBLK)
            high_xT(0)

            def expert_block(i, first=False):
                high_chunk(i, 2, first)
                high_chunk(i, 3)
                silu(i, 0)
                high_chunk(i, 4)
                high_aT(i, 0)
                high_chunk(i, 5)
                silu(i, 1)
                high_xT(i + 1)
                high_aT(i, 1)
                high_chunk(i + 1, 0)
                high_chunk(i + 1, 1)
                act.wait_ge(S["chunk_used"], 6 * i + 6)
                act.wait_ge(S["y_idx"], 2 * (i + 1))
                if not first:
                    act.wait_ge(S["y_scattered"], 16 * i)
                for b in range(2):
                    last = nc.scalar.activation(y_sb[:, 512 * b:512 * (b + 1)], ps[5 + b][:], ACT.Copy, scale=s_w[:, 0:1])
                last.then_inc(S["y_ready"], 1)

            expert_block(0, first=True)
            with act.Fori(1, n_blocks) as i:
                expert_block(i)

            def f_norm(t, s):
                act.wait_ge(S["f_normed"], t + 1)
                nc.scalar.activation(y0[s][:], y0[s][:], ACT.Identity, scale=rstd2[:, 0:1], bias=nmr2[:, 0:1]).then_inc(S["f_scaled"], 1)

            with act.Fori(0, NT // 2) as i:
                for s in range(2):
                    f_norm(2 * i + s, s)

        @block.vector
        def _(dve):
            st = Steps(dve, S["dve_steps"], S["dve_carrier"])
            nv = nc.vector

            dve.wait_ge(S["consts_made"], 1)
            for g, w in enumerate(WINDOWS):
                h = w // 2
                st.done(nv.tensor_scalar(bands[:, 0, g, :], band_prev[:, 0, :], float(h), float(w), ALU.add, ALU.min))
                st.done(nv.tensor_scalar(bands[:, 2, g, :], band_prev[:, 0, :], -1.0, float(P + h), ALU.mult, ALU.add))
                st.done(nv.memset(bands[:, 1, g, :], 1.0 / w))
                st.done(nv.memset(band_next[:, g, :], 1.0 / w))
                st.sync()
                st.done(nv.tensor_scalar(bands[:, 2, g, :], bands[:, 2, g, :], float(w), None, ALU.min))
                st.done(nv.reciprocal(bands[:, 0, g, :], bands[:, 0, g, :]))
                st.sync()
                st.done(nv.reciprocal(bands[:, 2, g, :], bands[:, 2, g, :]))
            st.sync()
            for g, w in enumerate(WINDOWS):
                last = nv.memset(band_prev[:, g, :], 1.0 / w)
            last.then_inc(S["band_edge"], 1)
            dve.wait_ge(S["band_made"], 5 * len(WINDOWS))
            dve.wait_ge(S["ident_made"], 1)
            last = nv.tensor_tensor(bands[:].rearrange("p v g m -> p (v g) m"), bands[:].rearrange("p v g m -> p (v g) m"),
                                    ident[:, None, :].to_broadcast([P, 12, P]), ALU.subtract)
            last.then_inc(S["bands_ready"], 1)

            dve.wait_ge(S["ada_bias"], 16)
            for j in range(N_ADA):
                dve.wait_ge(ada_used, (j + 1) * KD // CH)
                c = slice(j * SILU_N, (j + 1) * SILU_N)
                nv.tensor_tensor(mod[:, c], ps[2 + j % 2][0:2, :], b_ada_sb[:, c], ALU.add).then_inc(S["mod_row"], 1)
            for k in range(KD):
                dve.wait_ge(S["win_h_made"], k + 1)
                nv.tensor_tensor(win_l[:, k, :], win_raw[k % 2][:], win_h[:, k, :].bitcast(F32), ALU.subtract).then_inc(S["win_l_made"], 1)
            dve.wait_ge(S["small_loaded"], 16 * 9)
            dve.wait_ge(S["mod_stored"], 16)

            def low_x(t, s):
                dve.wait_ge(S["hT_h_made"], t + 1)
                for b in range(2):
                    last = nv.tensor_tensor(hT_l[s][:, 4 * b:4 * b + 4, :], ps[b][:].rearrange("p (k m) -> p k m", k=4),
                                            hT_h[s][:, 4 * b:4 * b + 4, :].bitcast(F32), ALU.subtract)
                last.then_inc(S["hT_l_made"], 1)

            def b_out(t):
                dve.wait_ge(S["b_made"], t + 1)
                dst = z2T[:, t, 4:8, :] if isinstance(t, int) else z2T[:, bass.ds(t, 1), 4:8, :].rearrange("p a k m -> p (a k) m")
                nv.tensor_tensor(dst, ps[6][:].rearrange("p (k m) -> p k m", k=4),
                                 pool_s[:, :, None].to_broadcast([P, 4, P]), ALU.mult).then_inc(S["b_copied"], 1)

            def pooled_copy(t):
                dve.wait_ge(S["pooled"], t + 1)
                if not (isinstance(t, int) and t == 0):
                    dve.wait_ge(S["b_made"], t)
                nv.tensor_copy(pooledT[:], ps[7][:].rearrange("p (g m) -> p g m", g=4)).then_inc(S["pooled_copied"], 1)

            def z_tile(t, s, nxt, b2, pl):
                if not (isinstance(t, int) and t < 2):
                    dve.wait_ge(S["pooled"], t - 1)
                    nv.tensor_copy(p_old[:], p_sb[s][:]).then_inc(S["p_kept"], 1)
                dve.wait_ge(S["v_gelu"], t + 1)
                st.done(nv.bn_stats(v_stat[:], v_sb[:]))
                st.sync_apart()
                st.done(nv.bn_aggr(v_mv[:], v_stat[:]))
                st.sync()
                nv.tensor_scalar(v_mv[:, 1:2], v_mv[:, 1:2], EPS, None, ALU.add).then_inc(S["v_stats"], 1)
                dve.wait_ge(S["v_rs"], t + 1)
                st.done(nv.tensor_scalar(v_sb[:], v_sb[:], v_mv[:, 0:1], v_rstd[:, 0:1], ALU.subtract, ALU.mult))
                st.sync()
                st.done(nv.tensor_tensor(v_sb[:], v_sb[:], vg[:], ALU.mult))
                st.sync()
                nv.tensor_tensor(v_sb[:], v_sb[:], vb[:], ALU.add).then_inc(S["v_normed"], 1)
                if nxt:
                    low_x(t + 1, 1 - s)
                if b2:
                    b_out(t - 2)
                dve.wait_ge(S["s_made"], t + 1)
                dve.wait_ge(S["u_gelu"], t + 1)
                if not (isinstance(t, int) and t == 0):
                    dve.wait_ge(S["aT_made"], t)
                for h in range(HEADS):
                    c = slice(h * P, (h + 1) * P)
                    last = nv.scalar_tensor_tensor(a_sb[:, c], ps[5][:, c], b_sp[:, h:h + 1], u_sb[:, c], ALU.add, ALU.mult)
                last.then_inc(S["a_ready"], 1)
                if pl:
                    pooled_copy(t - 1)

            low_x(0, 0)
            z_tile(0, 0, True, False, False)
            z_tile(1, 1, True, False, True)
            with dve.Fori(1, NT // 2 - 1) as i:
                st.enter(i - 1, 8)
                for s in range(2):
                    z_tile(2 * i + s, s, True, True, True)
            st.leave(NT // 2 - 2)
            z_tile(NT - 2, 0, True, True, True)
            z_tile(NT - 1, 1, False, True, True)
            b_out(NT - 2)
            pooled_copy(NT - 1)
            b_out(NT - 1)

            for k in range(KD):
                dve.wait_ge(S["wout_h_made"], k + 1)
                nv.tensor_tensor(wout_l[:, k, :], wout_raw[k % 4][:], wout_h[:, k, :].bitcast(F32), ALU.subtract).then_inc(S["wout_l_made"], 1)

            def low_z(t, s):
                dve.wait_ge(S["z2_h_made"], t + 1)
                src = z2T[:, t, :, :] if isinstance(t, int) else z2T[:, bass.ds(t, 1), :, :].rearrange("p a k m -> p (a k) m")
                nv.tensor_tensor(z2_l[s][:], src, z2_h[s][:].bitcast(F32), ALU.subtract).then_inc(S["z2_l_made"], 1)

            def second(t, s):
                dve.wait_ge(S["mix_made"], t + 1)
                if not (isinstance(t, int) and t == 0):
                    dve.wait_ge(S["x1_ready"], t)
                for b in range(2):
                    c = slice(512 * b, 512 * (b + 1))
                    st.done(nv.tensor_tensor(res[:, c], ps[2 * s + b][:], g1b[:, c], ALU.mult))
                st.sync()
                dve.wait_ge(S["xr_loaded"], 16 * (t + 1))
                nv.scalar_tensor_tensor(res[:], xr[:], ALPHA, res[:], ALU.mult, ALU.add).then_inc(S["res_ready"], 1)
                dve.wait_ge(S["res_ready"], t + 1)
                for b in range(2):
                    st.done(nv.bn_stats(stat[:, b, :], res[:, 512 * b:512 * (b + 1)]))
                st.sync_apart()
                st.done(nv.bn_aggr(mv[:], stat[:].rearrange("p a b -> p (a b)")))
                st.sync()
                nv.tensor_scalar(mv[:, 1:2], mv[:, 1:2], EPS, None, ALU.add).then_inc(S["var_ready"], 1)
                dve.wait_ge(S["rstd_ready"], t + 1)
                nv.scalar_tensor_tensor(nmr[:], mv[:, 0:1], -1.0, rstd[:], ALU.mult, ALU.mult).then_inc(S["shift_ready"], 1)

            def x1_out(t):
                dve.wait_ge(S["res_normed"], t + 1)
                st.done(nv.tensor_tensor(res[:], res[:], ln_g[:], ALU.mult))
                st.sync()
                dst = x1[:, t, :] if isinstance(t, int) else x1[:, bass.ds(t, 1), :].rearrange("p a n -> p (a n)")
                nv.tensor_tensor(dst, res[:], ln_b[:], ALU.add).then_inc(S["x1_ready"], 1)

            def logits_out(t):
                dve.wait_ge(S["logit_made"], t + 1)
                dst = logits[:, t, :] if isinstance(t, int) else logits[:, bass.ds(t, 1), :].rearrange("p a n -> p (a n)")
                nv.tensor_tensor(dst, ps[6][:, 0:NG + NE], router_b[:], ALU.add).then_inc(S["logit_read"], 1)

            low_z(0, 0)
            low_z(1, 1)
            dve.wait_ge(S["mod2_loaded"], 16 * 5)
            def norm_tile(t, s, nxt=True, prev=True):
                second(t, s)
                x1_out(t)
                if nxt:
                    low_z(t + 2, s)
                if prev:
                    logits_out(t - 1)

            norm_tile(0, 0, prev=False)
            norm_tile(1, 1)
            norm_tile(2, 0)
            norm_tile(3, 1)
            dve.wait_ge(S["mod2_loaded"], 16 * 8)
            with dve.Fori(2, NT // 2 - 1) as i:
                st.enter(i - 2, 2 * 6)
                for s in range(2):
                    norm_tile(2 * i + s, s)
            st.leave(NT // 2 - 3)
            norm_tile(NT - 2, 0, nxt=False)
            norm_tile(NT - 1, 1, nxt=False)
            logits_out(NT - 1)

            dve.wait_ge(S["rt_consts"], 6)
            G, E = logits[:, :, 0:NG], logits[:, :, NG:NG + NE]

            def step(ins):
                st.done(ins)
                st.sync()

            def first_max(dst, tmp, mx, src, n):
                step(nv.tensor_tensor(tmp, src, mx[:, :, None].to_broadcast([P, NT, n]), ALU.is_ge))
                step(nv.tensor_tensor(tmp, tmp, rev[:, None, 0:n].to_broadcast([P, NT, n]), ALU.mult))
                step(nv.tensor_reduce(em[:], tmp, AX.X, ALU.max))
                step(nv.tensor_tensor(dst, tmp, em[:, :, None].to_broadcast([P, NT, n]), ALU.is_equal))

            step(nv.tensor_reduce(gmax[:], G, AX.X, ALU.max))
            nv.tensor_tensor(g_a[:], G, gmax[:, :, None].to_broadcast([P, NT, NG]), ALU.subtract).then_inc(S["g_shifted"], 1)
            first_max(g_b[:], g_b[:], gmax, G, NG)
            step(nv.tensor_scalar(g_b[:], g_b[:], -1.0, FAR, ALU.add, ALU.mult))
            step(nv.tensor_tensor(e2[:].rearrange("p t (g e) -> p t g e", g=NG), E.rearrange("p t (g e) -> p t g e", g=NG),
                                  g_b[:, :, :, None].to_broadcast([P, NT, NG, EPG]), ALU.add))
            step(nv.tensor_reduce(v1[:], e2[:], AX.X, ALU.max))
            first_max(oh[0][:], e_t[:], v1, e2[:], NE)
            step(nv.scalar_tensor_tensor(e2[:], oh[0][:], -2 * FAR, e2[:], ALU.mult, ALU.add))
            step(nv.tensor_reduce(v2[:], e2[:], AX.X, ALU.max))
            first_max(oh[1][:], e_t[:], v2, e2[:], NE)
            nv.tensor_tensor(both[:], oh[0][:], oh[1][:], ALU.add).then_inc(S["sel_ready"], 1)
            nv.tensor_tensor(v2[:], v2[:], v1[:], ALU.subtract).then_inc(S["top_diff"], 1)
            dve.wait_ge(S["g_exp"], 1)
            step(nv.tensor_reduce(gw[:], g_a[:], AX.X, ALU.add))
            step(nv.reciprocal(gw[:], gw[:]))
            dve.wait_ge(S["top_exp"], 1)
            step(nv.tensor_scalar(den[:], ex[:], 1.0, None, ALU.add))
            step(nv.reciprocal(den[:], den[:]))
            step(nv.tensor_tensor(vals[:, 2, 0, :], den[:], gw[:], ALU.mult))
            step(nv.tensor_tensor(vals[:, 2, 1, :], vals[:, 2, 0, :], ex[:], ALU.mult))
            st.done(nv.tensor_copy(vals[:, 0, 0, :], tok[:, 0, :]))
            st.done(nv.tensor_copy(vals[:, 0, 1, :], tok[:, 0, :]))
            st.done(nv.tensor_scalar(vals[:, 1, :, :], tok[:], -NO_ROW, None, ALU.add))
            st.done(nv.memset(before[:, 0, :], 0.0))
            dve.wait_ge(S["ranks_made"], 1)
            for t in range(NT):
                st.sync()
                st.done(nv.tensor_tensor(before[:, t + 1, :], before[:, t, :], ps[1][:, NE * t:NE * (t + 1)], ALU.add))
            st.sync()
            step(nv.tensor_tensor(pos[:], before[:, 0:NT, :], ps[0][:, 0:NT * NE].rearrange("p (t e) -> p t e", t=NT), ALU.add))
            step(nv.tensor_tensor(cmp[:], before[:, NT, :, None].to_broadcast([P, NE, NT]), cmp[:], ALU.is_gt))
            step(nv.tensor_reduce(nblk[:], cmp[:], AX.X, ALU.add))
            step(nv.tensor_scalar(nblk[:], nblk[:], 1.0, None, ALU.max))
            step(nv.tensor_copy(cum[0][:], nblk[:]))
            k, d = 0, 1
            while d < NE:
                st.done(nv.tensor_copy(cum[1 - k][:, 0:d], cum[k][:, 0:d]))
                st.done(nv.tensor_tensor(cum[1 - k][:, d:NE], cum[k][:, d:NE], cum[k][:, 0:NE - d], ALU.add))
                st.sync()
                k, d = 1 - k, 2 * d
            end = cum[k]
            st.done(nv.tensor_copy(block_n[:], end[0:1, NE - 1:NE]))
            step(nv.tensor_tensor(cmp_e[:], end[0:1, None, :].to_broadcast([1, TAB, NE]), cmp_e[:], ALU.is_le))
            step(nv.tensor_reduce(eid_f[:], cmp_e[:], AX.X, ALU.add))
            step(nv.tensor_scalar(eid_f[:], eid_f[:], float(NE - 1), None, ALU.min))
            nv.tensor_copy(block_e[:], eid_f[:]).then_inc(S["eid_ready"], 1)
            step(nv.tensor_tensor(cum[1 - k][:], end[:], nblk[:], ALU.subtract))
            step(nv.tensor_scalar(cum[1 - k][:], cum[1 - k][:], float(P), None, ALU.mult))
            step(nv.tensor_tensor(pos[:], pos[:], cum[1 - k][:, None, :].to_broadcast([P, NT, NE]), ALU.add))
            for c in range(2):
                step(nv.tensor_tensor(e_t[:], pos[:], oh[c][:], ALU.mult))
                step(nv.tensor_reduce(slot_f[:, c, :], e_t[:], AX.X, ALU.add))
            step(nv.tensor_copy(slot_i[:], slot_f[:]))
            st.done(nv.tensor_scalar(blk_i[:], slot_i[:], 7, None, ALU.logical_shift_right))
            step(nv.tensor_scalar(in_i[:], slot_i[:], P - 1, None, ALU.bitwise_and))
            st.done(nv.tensor_copy(blk_f[:], blk_i[:]))
            step(nv.tensor_copy(in_f[:], in_i[:]))
            blk_v, in_v = blk_f[:].rearrange("p c t -> p (c t)"), in_f[:].rearrange("p c t -> p (c t)")
            val_v = vals[:].rearrange("p v c t -> p v (c t)")

            def pick(j, s):
                if not (isinstance(j, int) and j < 2):
                    dve.wait_ge(S["pick_used"], j - 1)
                one = bass.ds(j, 1)
                nv.tensor_scalar(pick_r[s][:], iota_r[:], in_v[:, one], None, ALU.is_equal)
                for v in range(3):
                    last = nv.tensor_scalar(pick_b[s][:, v, :], iota_r[:, 0:TAB], blk_v[:, one], val_v[:, v, one], ALU.is_equal, ALU.mult)
                last.then_inc(S["pick_ready"], 1)

            pick(0, 0)
            pick(1, 1)
            with dve.Fori(1, NT) as i:
                pick(2 * i, 0)
                pick(2 * i + 1, 1)
            dve.wait_ge(S["tab_made"], 1)
            step(nv.tensor_copy(table[:], ps[7][:, 0:3 * TAB].rearrange("p (v b) -> p v b", v=3)))
            st.done(nv.tensor_copy(table_i[:, 0, :], table[:, 0, :]))
            step(nv.tensor_scalar(table[:, 1, :], table[:, 1, :], NO_ROW, None, ALU.add))
            nv.tensor_copy(table_i[:, 1, :], table[:, 1, :]).then_inc(S["tab_ready"], 1)

            def low_chunk(i, c):
                dve.wait_ge(S["chunk_h"], 6 * i + c + 1)
                nv.tensor_tensor(ring_l[c % 3][:], raw[c][:], ring_h[c % 3][:].bitcast(F32), ALU.subtract).then_inc(S["chunk_l"], 1)

            def gate(i, half):
                dve.wait_ge(S["silu_made"], 2 * i + half + 1)
                if not (isinstance(i, int) and i == 0):
                    dve.wait_ge(S["aT_e_made"], 2 * i + half - 1)
                nv.tensor_tensor(act_a[:, HC * half:HC * (half + 1)], ps[half][:, HC:2 * HC], act_s[:], ALU.mult).then_inc(S["act_ready"], 1)

            def low_aT(i, half):
                dve.wait_ge(S["aT_h_made"], 2 * i + half + 1)
                nv.tensor_tensor(aT_l[:, 2 * half:2 * half + 2, :], ps[4][:, HC * half:HC * (half + 1)].rearrange("p (k m) -> p k m", k=2),
                                 aT_h[:, 2 * half:2 * half + 2, :].bitcast(F32), ALU.subtract).then_inc(S["aT_l_made"], 1)

            def low_xT(i):
                dve.wait_ge(S["xT_h_made"], i + 1)
                for b in range(2):
                    last = nv.tensor_tensor(xT_l[:, 4 * b:4 * b + 4, :], ps[2 + b][:].rearrange("p (k m) -> p k m", k=4),
                                            xT_h[:, 4 * b:4 * b + 4, :].bitcast(F32), ALU.subtract)
                last.then_inc(S["xT_l_made"], 1)

            n_blocks = dve.value_load(block_n[0:1, 0:1], min_val=NE, max_val=MAXBLK)
            for c in range(2):
                low_chunk(0, c)
            low_xT(0)

            def expert_block(i):
                low_chunk(i, 2)
                low_chunk(i, 3)
                gate(i, 0)
                low_chunk(i, 4)
                low_aT(i, 0)
                low_chunk(i, 5)
                gate(i, 1)
                low_xT(i + 1)
                low_aT(i, 1)
                low_chunk(i + 1, 0)
                low_chunk(i + 1, 1)

            expert_block(0)
            with dve.Fori(1, n_blocks) as i:
                expert_block(i)

            yl = [S["y0_loaded_0"], S["y0_loaded_1"]]
            dve.wait_ge(S["last_loaded"], 64)

            def final(i, s, q):
                t = 2 * i + s
                dve.wait_ge(yl[s], 32 * (i + 1))
                st.done(nv.tensor_tensor(y0[s][:], y0[s][:], y1[s][:], ALU.add))
                st.sync()
                st.done(nv.tensor_tensor(y0[s][:], y0[s][:], g2b[q][:], ALU.mult))
                st.sync()
                xt = x1[:, t, :] if isinstance(t, int) else x1[:, bass.ds(t, 1), :].rearrange("p a n -> p (a n)")
                st.done(nv.scalar_tensor_tensor(y0[s][:], xt, ALPHA, y0[s][:], ALU.mult, ALU.add))
                st.sync()
                for b in range(2):
                    st.done(nv.bn_stats(stat2[:, b, :], y0[s][:, 512 * b:512 * (b + 1)]))
                st.sync_apart()
                st.done(nv.bn_aggr(mv2[:], stat2[:].rearrange("p a b -> p (a b)")))
                st.sync()
                nv.tensor_scalar(mv2[:, 1:2], mv2[:, 1:2], EPS, None, ALU.add).then_inc(S["f_var"], 1)
                dve.wait_ge(S["f_rstd"], t + 1)
                nv.scalar_tensor_tensor(nmr2[:], mv2[:, 0:1], -1.0, rstd2[:], ALU.mult, ALU.mult).then_inc(S["f_normed"], 1)
                dve.wait_ge(S["f_scaled"], t + 1)
                st.done(nv.tensor_tensor(y0[s][:], y0[s][:], ln2_g[:], ALU.mult))
                st.sync()
                if not (isinstance(i, int) and i == 0):
                    dve.wait_ge(S[f"f_stored_{s}"], 16 * i)
                nv.tensor_tensor(fin[s][:], y0[s][:], ln2_b[:], ALU.add).then_inc(S["f_ready"], 1)

            for s in range(2):
                final(0, s, 0)
            for q, (lo, hi) in enumerate(((1, SEQ_TILES[0][1] // 2), (SEQ_TILES[1][0] // 2, NT // 2))):
                with dve.Fori(lo, hi) as i:
                    st.enter(i - lo, 14)
                    for s in range(2):
                        final(i, s, q)
                st.leave(hi - lo)

        @block.tensor
        def _(pe):
            mm = nc.tensor.matmul

            def three(out, lh, ll, rh, rl, start, stop):
                mm(out, lh, rh, start=start, stop=False)
                mm(out, lh, rl, start=False, stop=False)
                return mm(out, ll, rh, start=False, stop=stop)

            pe.wait_ge(S["ident_made"], 1)
            pe.wait_ge(S["c_silu"], 1)
            nc.tensor.transpose(ps[0][:, 0:2 * KD], c_act[:], ident[0:2 * KD, 0:2 * KD]).then_inc(S["cT_made"], 1)
            pe.wait_ge(S["wsp_loaded"], 16)
            for h in range(HEADS):
                last = nc.tensor.transpose(ps[1][:, h * P:(h + 1) * P], w_spT[:, h, :], ident[:])
            last.then_inc(S["wspT_made"], 1)
            pe.wait_ge(S["cT_copied"], 1)
            c_cols = cT[:].rearrange("p (s k) -> p k s", s=2)
            n = 0
            for j in range(N_ADA):
                if j >= 2:
                    pe.wait_ge(S["mod_row"], j - 1)
                out = ps[2 + j % 2][0:2, :]
                for kk in range(KD // CH):
                    pe.wait_ge(ada_loaded[n % 3], 16 * (n // 3 + 1))
                    for k in range(kk * CH, (kk + 1) * CH):
                        last = mm(out, c_cols[:, k, :], ada[n % 3][:, k % CH, :], start=k == 0, stop=k == KD - 1)
                    last.then_inc(ada_used, 1)
                    n += 1

            def transposes(t):
                pe.wait_ge(S["h_ready"], t + 1)
                if not (isinstance(t, int) and t == 0):
                    pe.wait_ge(S["hT_l_made"], t)
                for k in range(KD):
                    last = nc.tensor.transpose(ps[k // 4][:, (k % 4) * P:(k % 4 + 1) * P], xs[:, k * P:(k + 1) * P], ident[:])
                last.then_inc(S["xT_made"], 1)

            def z_part(out, s, part):
                c = slice(part * AW, (part + 1) * AW)
                for k in range(KD):
                    last = three(out, hT_h[s][:, k, :], hT_l[s][:, k, :], win_h[:, k, c], win_l[:, k, c], k == 0, k == KD - 1)
                return last

            def w_pool_mm(t):
                pe.wait_ge(S["pooled_copied"], t + 1)
                if not (isinstance(t, int) and t == 0):
                    pe.wait_ge(S["aT_copied"], t + 1)
                for g in range(4):
                    last = mm(ps[6][:, g * P:(g + 1) * P], w_pool[:, g, :], pooledT[:, g, :], start=True, stop=True)
                last.then_inc(S["b_made"], 1)

            def a_transposes(t):
                pe.wait_ge(S["a_ready"], t + 1)
                if not (isinstance(t, int) and t == 0):
                    pe.wait_ge(S["b_copied"], t)
                for h in range(HEADS):
                    last = nc.tensor.transpose(ps[6][:, h * P:(h + 1) * P], a_sb[:, h * P:(h + 1) * P], ident[:])
                last.then_inc(S["aT_made"], 1)

            def pool_mm(t, s, kind, prev, nxt, prev_src=p_old):
                if nxt:
                    pe.wait_ge(S["p_copied"], t + 2)
                else:
                    pe.wait_ge(S["p_copied"], t + 1)
                if prev and prev_src is p_old:
                    pe.wait_ge(S["p_kept"], t)
                if not (isinstance(t, int) and t == 0):
                    pe.wait_ge(S["pooled_copied"], t)
                for g in range(4):
                    c = slice(g * P, (g + 1) * P)
                    last = mm(ps[7][:, c], p_sb[s][:, c], bands[:, kind, g, :], start=True, stop=not (prev or nxt))
                    if prev:
                        last = mm(ps[7][:, c], prev_src[:, c], band_prev[:, g, :], start=False, stop=not nxt)
                    if nxt:
                        last = mm(ps[7][:, c], p_sb[1 - s][:, c], band_next[:, g, :], start=False, stop=True)
                last.then_inc(S["pooled"], 1)

            def z_tile(t, s, nxt, b2, prev, edge=(1, True, True)):
                pe.wait_ge(S["hT_l_made"], t + 1)
                if not (isinstance(t, int) and t == 0):
                    pe.wait_ge(S["v_gelu"], t)
                z_part(ps[2][:], s, 1).then_inc(S["v_made"], 1)
                if nxt:
                    transposes(t + 1)
                if b2:
                    w_pool_mm(t - 2)
                if not (isinstance(t, int) and t == 0):
                    pe.wait_ge(S["u_gelu"], t)
                z_part(ps[3][:], s, 0).then_inc(S["u_made"], 1)
                if prev:
                    a_transposes(t - 1)
                if not (isinstance(t, int) and t == 0):
                    pe.wait_ge(S["p_copied"], t)
                z_part(ps[4][:], s, 2).then_inc(S["p_made"], 1)
                pe.wait_ge(S["v_normed"], t + 1)
                if not (isinstance(t, int) and t == 0):
                    pe.wait_ge(S["a_ready"], t)
                for h in range(HEADS):
                    last = mm(ps[5][:, h * P:(h + 1) * P], w_spT[:, h, :], v_sb[:, h * P:(h + 1) * P], start=True, stop=True)
                last.then_inc(S["s_made"], 1)
                if prev:
                    pool_mm(t - 1, 1 - s, *edge)

            pe.wait_ge(S["wspT_copied"], 1)
            pe.wait_ge(S["bands_ready"], 1)
            transposes(0)
            pe.wait_ge(S["win_l_made"], KD)
            pe.wait_ge(S["small_loaded"], 16 * 9)
            first_t, last_t = (0, False, True), (2, True, False)
            z_tile(0, 0, True, False, False)
            z_tile(1, 1, True, False, True, first_t)
            z_tile(2, 0, True, True, True)
            z_tile(3, 1, True, True, True)
            z_tile(4, 0, True, True, True, last_t)
            z_tile(5, 1, True, True, True, first_t)
            with pe.Fori(3, NT // 2 - 1) as i:
                for s in range(2):
                    z_tile(2 * i + s, s, True, True, True)
            z_tile(NT - 2, 0, True, True, True)
            z_tile(NT - 1, 1, False, True, True)
            w_pool_mm(NT - 2)
            a_transposes(NT - 1)
            pool_mm(NT - 1, 1, *last_t, prev_src=p_sb[0])
            w_pool_mm(NT - 1)

            def mix(t, s, first=False):
                pe.wait_ge(S["z2_l_made"], t + 1)
                if not (isinstance(t, int) and t < 2):
                    pe.wait_ge(S["res_ready"], t - 1)
                if first:
                    for k in range(KD):
                        pe.wait_ge(S["wout_l_made"], k + 1)
                        for b in range(2):
                            c = slice(512 * b, 512 * (b + 1))
                            last = three(ps[2 * s + b][:], z2_h[s][:, k, :], z2_l[s][:, k, :], wout_h[:, k, c], wout_l[:, k, c], k == 0, k == KD - 1)
                else:
                    for b in range(2):
                        c = slice(512 * b, 512 * (b + 1))
                        for k in range(KD):
                            last = three(ps[2 * s + b][:], z2_h[s][:, k, :], z2_l[s][:, k, :], wout_h[:, k, c], wout_l[:, k, c], k == 0, k == KD - 1)
                last.then_inc(S["mix_made"], 1)

            def h2_transposes(t):
                pe.wait_ge(S["h2_ready"], t + 1)
                if not (isinstance(t, int) and t == 0):
                    pe.wait_ge(S["h2T_copied"], t)
                for k in range(KD):
                    last = nc.tensor.transpose(ps[4 + k // 4][:, (k % 4) * P:(k % 4 + 1) * P], h2[:, k * P:(k + 1) * P], ident[:])
                last.then_inc(S["h2T_made"], 1)

            def route(t):
                pe.wait_ge(S["h2T_copied"], t + 1)
                if not (isinstance(t, int) and t == 0):
                    pe.wait_ge(S["logit_read"], t)
                for k in range(KD):
                    last = mm(ps[6][:, 0:NG + NE], h2T[:, k, :], router_w[:, k, :], start=k == 0, stop=k == KD - 1)
                last.then_inc(S["logit_made"], 1)

            pe.wait_ge(S["b_copied"], NT)
            mix(0, 0, first=True)
            mix(1, 1)
            for t in (2, 3):
                h2_transposes(t - 2)
                route(t - 2)
                mix(t, t - 2)
            with pe.Fori(2, NT // 2) as i:
                for s in range(2):
                    h2_transposes(2 * i + s - 2)
                    route(2 * i + s - 2)
                    mix(2 * i + s, s)
            for t in (NT - 2, NT - 1):
                h2_transposes(t)
                route(t)

            pe.wait_ge(S["sel_ready"], 1)
            sel = both[:].rearrange("p t e -> p (t e)")
            mm(ps[0][:, 0:NT * NE], tri[:], sel, start=True, stop=True)
            mm(ps[1][:, 0:NT * NE], ones[:], sel, start=True, stop=True).then_inc(S["ranks_made"], 1)

            def pick(j, s, start=False, stop=False):
                pe.wait_ge(S["pick_ready"], j + 1)
                return mm(ps[7][:, 0:3 * TAB], pick_r[s][:], pick_b[s][:].rearrange("p v b -> p (v b)"), start=start, stop=stop)

            pick(0, 0, start=True).then_inc(S["pick_used"], 1)
            pick(1, 1).then_inc(S["pick_used"], 1)
            with pe.Fori(1, NT - 1) as i:
                pick(2 * i, 0).then_inc(S["pick_used"], 1)
                pick(2 * i + 1, 1).then_inc(S["pick_used"], 1)
            pick(2 * NT - 2, 0)
            pick(2 * NT - 1, 1, stop=True).then_inc(S["tab_made"], 1)

            def x_transposes(i):
                pe.wait_ge(S["gathered"], 16 * (i + 1))
                if not (isinstance(i, int) and i == 0):
                    pe.wait_ge(S["xT_l_made"], i)
                for k in range(KD):
                    last = nc.tensor.transpose(ps[2 + k // 4][:, (k % 4) * P:(k % 4 + 1) * P], xg[:, k * P:(k + 1) * P], ident[:])
                last.then_inc(S["xgT_made"], 1)

            def gate_up(i, c):
                pe.wait_ge(S["chunk_l"], 6 * i + c + 1)
                if c % 2 == 0 and not (isinstance(i, int) and i == 0):
                    pe.wait_ge(S["act_ready"], 2 * i + c // 2 - 1)
                wh = ring_h[c % 3][:].rearrange("p (k n) -> p k n", k=4)
                wl = ring_l[c % 3][:].rearrange("p (k n) -> p k n", k=4)
                for k in range(4):
                    kk = 4 * (c % 2) + k
                    last = three(ps[c // 2][:], xT_h[:, kk, :], xT_l[:, kk, :], wh[:, k, :], wl[:, k, :], kk == 0, kk == KD - 1)
                return last

            def a_t(i, half):
                pe.wait_ge(S["act_ready"], 2 * i + half + 1)
                if not (isinstance(i, int) and i == 0):
                    pe.wait_ge(S["aT_l_made"], 2 * i + half)
                for k in range(2):
                    kk = 2 * half + k
                    last = nc.tensor.transpose(ps[4][:, kk * P:(kk + 1) * P], act_a[:, kk * P:(kk + 1) * P], ident[:])
                last.then_inc(S["aT_e_made"], 1)

            def down(i, c):
                pe.wait_ge(S["chunk_l"], 6 * i + c + 1)
                pe.wait_ge(S["aT_l_made"], 2 * i + c - 4 + 1)
                wh = ring_h[c % 3][:].rearrange("p (k n) -> p k n", k=2)
                wl = ring_l[c % 3][:].rearrange("p (k n) -> p k n", k=2)
                for b in range(2):
                    for k in range(2):
                        kk = 2 * (c - 4) + k
                        n = slice(512 * b, 512 * (b + 1))
                        last = three(ps[5 + b][:], aT_h[:, kk, :], aT_l[:, kk, :], wh[:, k, n], wl[:, k, n], kk == 0, kk == KE - 1)
                return last

            pe.wait_ge(S["tab_ready"], 1)
            pe.wait_ge(S["eid_ready"], 1)
            n_blocks = pe.value_load(block_n[0:1, 0:1], min_val=NE, max_val=MAXBLK)
            x_transposes(0)

            def expert_block(i, first=False):
                pe.wait_ge(S["xT_l_made"], i + 1)
                gate_up(i, 0).then_inc(S["chunk_used"], 1)
                gate_up(i, 1).then_inc(S["chunk_used"], 1)
                gate_up(i, 2).then_inc(S["chunk_used"], 1)
                a_t(i, 0)
                gate_up(i, 3).then_inc(S["chunk_used"], 1)
                x_transposes(i + 1)
                if not first:
                    pe.wait_ge(S["y_ready"], i)
                down(i, 4).then_inc(S["chunk_used"], 1)
                a_t(i, 1)
                down(i, 5).then_inc(S["chunk_used"], 1)

            expert_block(0, first=True)
            with pe.Fori(1, n_blocks) as i:
                expert_block(i)


INPUTS = ["x_prompt", "x_sample", "c_prompt", "c_sample", "w_ada", "b_ada", "w_in", "v_norm_g", "v_norm_b",
          "w_spatial", "b_spatial", "w_pool", "pool_scale", "w_out", "ln1_g", "ln1_b", "w_route_group",
          "b_route_group", "w_route_expert", "b_route_expert", "w_gate_up", "w_down", "ln2_g", "ln2_b"]
OUTPUTS = [(1, 512, D), (1, 1024, D)]


def kernel(**inputs):
    import numpy as np
    from concourse import bacc
    from concourse.bass_utils import run_bass_kernel_spmd

    nc = bacc.Bacc("TRN2", target_bir_lowering=False, num_devices=1)
    arrays, ins = {}, {}
    for name in INPUTS:
        a = np.ascontiguousarray(inputs[name])
        arrays[f"in_{name}"] = a
        ins[name] = nc.dram_tensor(f"in_{name}", a.shape, mybir.dt.from_np(a.dtype), kind="ExternalInput").ap()
    outs = [nc.dram_tensor(f"out_{i}", shape, F32, kind="ExternalOutput").ap() for i, shape in enumerate(OUTPUTS)]
    encoder(nc, ins, outs)
    r = run_bass_kernel_spmd(nc, [arrays], core_ids=[0])
    return tuple(r.results[0][f"out_{i}"] for i in range(len(outs)))
```

```python
from contextlib import ExitStack

import concourse.bass as bass
from concourse import mybir

F32 = mybir.dt.float32
F32R = mybir.dt.float32r
I32 = mybir.dt.int32
ACT = mybir.ActivationFunctionType
ALU = mybir.AluOpType
AX = mybir.AxisListType

P = 128
D = 1024
KD = D // P
SEQS = (512, 1024)
T = sum(SEQS)
NT = T // P
SEQ_TILES = ((0, SEQS[0] // P), (SEQS[0] // P, NT))
AW = D // 2
HEADS = 4
WINDOWS = (2, 4, 8, 16)
NG = 4
EPG = 8
NE = NG * EPG
DE = D // 2
KE = DE // P
NMOD = 6
EPS = 1e-5
ALPHA = 2.0 ** 0.25
PAIRS = 2 * T
MAXBLK = (PAIRS + NE * P) // P
TAB = MAXBLK + 2
NO_ROW = 4096.0
FAR = 1e30
ADA_N = 512
CH = 4
GU_SLOTS = 7
DN_SLOTS = 4
N_ADA = NMOD * D // ADA_N


class Steps:

    def __init__(self, eng, sem, carrier):
        self.eng, self.sem, self.carrier, self.base, self.n = eng, sem, carrier, 0, 0

    def done(self, ins):
        ins.then_inc(self.sem, 1)
        self.n += 1

    def sync(self):
        self.eng.wait_ge(self.sem, self.base + self.n)

    def sync_apart(self):
        self.sync()
        self.eng.sem_inc(self.carrier, 1)

    def enter(self, i, per):
        self.start = self.base + self.n
        self.per = per
        self.base, self.n = self.start + i * per, 0

    def leave(self, count):
        assert self.n == self.per, (self.n, self.per)
        self.base, self.n = self.start + count * self.per, 0


def encoder(nc, ins, outs):
    ctx = ExitStack()
    with ctx:
        names = []

        def sem(name):
            names.append(name)
            return ctx.enter_context(nc.semaphore(name))

        base = (nc.sbuf_base + 63) // 64 * 64
        top = nc.sbuf_usable_end

        class Region:
            def __init__(self, start):
                self.at = start

            def take(self, name, shape, dt=F32):
                n = 4
                for s in shape[1:]:
                    n *= s
                t = nc.alloc_sbuf_tensor_at(name, list(shape), dt, offset=self.at)
                self.at += (n + 31) // 32 * 32
                assert self.at <= top, (name, self.at - top)
                return t

        KB = 1024
        W0 = base
        Z0 = W0 + 96 * KB
        C0 = Z0 + 48 * KB

        r = Region(W0)
        win_h = r.take("win_h", [P, KD, 3 * AW], F32R)
        win_l = r.take("win_l", [P, KD, 3 * AW], F32R)
        r = Region(W0)
        wout_h = r.take("wout_h", [P, KD, D], F32R)
        wout_l = r.take("wout_l", [P, KD, D], F32R)
        wout_raw = [r.take(f"wout_raw{s}", [P, D]) for s in range(4)]
        r = Region(W0)
        gu_raw = r.take("gu_raw", [P, GU_SLOTS, 2, D])
        gu_h = r.take("gu_h", [P, GU_SLOTS, 2, D], F32R)
        dn_raw = r.take("dn_raw", [P, DN_SLOTS, 2, D])
        assert r.at <= C0
        gu_l = Region(W0).take("gu_l", [P, GU_SLOTS, 2, D], F32R)
        dn_l = Region(W0 + 2 * GU_SLOTS * 2 * D * 4).take("dn_l", [P, DN_SLOTS, 2, D], F32R)

        r = Region(Z0)
        ada = [r.take(f"ada{s}", [P, CH, ADA_N]) for s in range(3)]
        b_ada_sb = r.take("b_ada_sb", [2, NMOD * D])
        r = Region(Z0)
        z2T = r.take("z2T", [P, NT, KD, P])
        r = Region(Z0)
        x1 = r.take("x1", [P, NT, D])

        r = Region(C0)
        router_w = r.take("router_w", [P, KD, NG + NE])
        router_b = r.take("router_b", [P, NG + NE])
        C1 = r.at
        TOP0 = top // 32 * 32 - 3744
        r = Region(TOP0)
        logits = r.take("logits", [P, NT, NG + NE])
        table = r.take("table", [P, 3, TAB])
        table_i = r.take("table_i", [P, 2, TAB], I32)
        block_e = r.take("block_e", [1, TAB], I32)
        block_n = r.take("block_n", [1, 2], I32)
        KEPT0 = r.at
        ident = r.take("ident", [P, P])
        half_neg = r.take("half_neg", [P, 1])
        r = Region(C1)
        bands = r.take("bands", [P, 3, len(WINDOWS), P])
        band_prev = r.take("band_prev", [P, len(WINDOWS), P])
        band_next = r.take("band_next", [P, len(WINDOWS), P])
        w_spT = r.take("w_spT", [P, HEADS, P])
        b_sp = r.take("b_sp", [P, HEADS])
        w_pool = r.take("w_pool", [P, len(WINDOWS), P])
        pool_s = r.take("pool_s", [P, len(WINDOWS)])
        vg = r.take("vg", [P, AW])
        vb = r.take("vb", [P, AW])
        B0 = r.at
        sc1 = r.take("sc1", [P, D])
        sh1 = r.take("sh1", [P, D])
        xs = r.take("xs", [P, D])
        hT_h = [r.take(f"hT_h{s}", [P, KD, P], F32R) for s in range(2)]
        hT_l = [r.take(f"hT_l{s}", [P, KD, P], F32R) for s in range(2)]
        u_sb = r.take("u_sb", [P, AW])
        v_sb = r.take("v_sb", [P, AW])
        a_sb = r.take("a_sb", [P, AW])
        p_sb = [r.take(f"p_sb{s}", [P, AW]) for s in range(2)]
        p_old = r.take("p_old", [P, AW])
        pooledT = r.take("pooledT", [P, len(WINDOWS), P])
        v_stat = r.take("v_stat", [P, 6])
        v_mv = r.take("v_mv", [P, 2])
        v_rstd = r.take("v_rstd", [P, 1])
        assert r.at <= KEPT0
        r = Region(B0)
        mod = r.take("mod", [2, NMOD * D])
        win_raw = [r.take(f"win_raw{s}", [P, 3 * AW]) for s in range(2)]
        c_in = r.take("c_in", [2 * KD, P])
        c_act = r.take("c_act", [2 * KD, P])
        cT = r.take("cT", [P, 2 * KD])
        r = Region(C1)
        z2_h = [r.take(f"z2_h{s}", [P, KD, P], F32R) for s in range(2)]
        z2_l = [r.take(f"z2_l{s}", [P, KD, P], F32R) for s in range(2)]
        xr = r.take("xr", [P, D])
        res = r.take("res", [P, D])
        h2 = r.take("h2", [P, D])
        h2T = r.take("h2T", [P, KD, P])
        g1b = r.take("g1b", [P, D])
        sc2b = r.take("sc2b", [P, D])
        sh2b = r.take("sh2b", [P, D])
        ln_g = r.take("ln_g", [P, D])
        ln_b = r.take("ln_b", [P, D])
        stat = r.take("stat", [P, 2, 6])
        mv = r.take("mv", [P, 2])
        rstd = r.take("rstd", [P, 1])
        nmr = r.take("nmr", [P, 1])
        r = Region(C1)
        tri = r.take("tri", [P, P])
        ones = r.take("ones", [P, P])
        iota_p = r.take("iota_p", [P, 1])
        iota_r = r.take("iota_r", [P, P])
        rev = r.take("rev", [P, NE])
        tok = r.take("tok", [P, 2, NT])
        gmax = r.take("gmax", [P, NT])
        gw = r.take("gw", [P, NT])
        g_a = r.take("g_a", [P, NT, NG])
        g_b = r.take("g_b", [P, NT, NG])
        gm = r.take("gm", [P, NT])
        e2 = r.take("e2", [P, NT, NE])
        e_t = r.take("e_t", [P, NT, NE])
        oh = [r.take(f"oh{k}", [P, NT, NE]) for k in range(2)]
        both = r.take("both", [P, NT, NE])
        v1 = r.take("v1", [P, NT])
        v2 = r.take("v2", [P, NT])
        em = r.take("em", [P, NT])
        ex = r.take("ex", [P, NT])
        den = r.take("den", [P, NT])
        vals = r.take("vals", [P, 3, 2, NT])
        before = r.take("before", [P, NT + 1, NE])
        pos = r.take("pos", [P, NT, NE])
        cmp = r.take("cmp", [P, NE, NT])
        nblk = r.take("nblk", [P, NE])
        cum = [r.take(f"cum{k}", [P, NE]) for k in range(2)]
        cmp_e = r.take("cmp_e", [1, TAB, NE])
        eid_f = r.take("eid_f", [1, TAB])
        slot_f = r.take("slot_f", [P, 2, NT])
        slot_i = r.take("slot_i", [P, 2, NT], I32)
        blk_i = r.take("blk_i", [P, 2, NT], I32)
        in_i = r.take("in_i", [P, 2, NT], I32)
        blk_f = r.take("blk_f", [P, 2, NT])
        in_f = r.take("in_f", [P, 2, NT])
        pick_r = [r.take(f"pick_r{s}", [P, P]) for s in range(2)]
        pick_b = [r.take(f"pick_b{s}", [P, 3, TAB]) for s in range(2)]
        r = Region(C0)
        dn_h = r.take("dn_h", [P, DN_SLOTS, 2, D], F32R)
        xg = r.take("xg", [P, D])
        xT_h = r.take("xT_h", [P, KD, P], F32R)
        xT_l = r.take("xT_l", [P, KD, P], F32R)
        act_s = r.take("act_s", [P, DE])
        act_a = r.take("act_a", [P, DE])
        aT_h = r.take("aT_h", [P, KE, P], F32R)
        aT_l = r.take("aT_l", [P, KE, P], F32R)
        y_sb = r.take("y_sb", [P, D])
        g_idx = r.take("g_idx", [P, 1], I32)
        s_idx = r.take("s_idx", [P, 1], I32)
        s_w = r.take("s_w", [P, 1])
        assert r.at <= TOP0
        r = Region(W0)
        y0 = [r.take(f"y0_{s}", [P, D]) for s in range(2)]
        y1 = [r.take(f"y1_{s}", [P, D]) for s in range(2)]
        x1t = [r.take(f"x1t{s}", [P, D]) for s in range(2)]
        r2 = [r.take(f"r2_{s}", [P, D]) for s in range(2)]
        fin = [r.take(f"fin{s}", [P, D]) for s in range(2)]
        g2b = [r.take(f"g2b{q}", [P, D]) for q in range(2)]
        ln2_g = r.take("ln2_gb", [P, D])
        ln2_b = r.take("ln2_bb", [P, D])
        stat2 = r.take("stat2", [P, 2, 6])
        mv2 = [r.take(f"mv2_{s}", [P, 2]) for s in range(2)]
        rstd2 = [r.take(f"rstd2_{s}", [P, 1]) for s in range(2)]
        nmr2 = [r.take(f"nmr2_{s}", [P, 1]) for s in range(2)]

        ps = [ctx.enter_context(nc.psum_tensor(f"bank{b}", [P, 512], F32)) for b in range(8)]

        mod_d = nc.dram_tensor("mod_rows", (2, NMOD * D), F32).ap()
        h2_d = nc.dram_tensor("h2_rows", (T, D), F32).ap()
        x1_d = nc.dram_tensor("x1_rows", (T, D), F32).ap()
        y_d = nc.dram_tensor("y_rows", (PAIRS, D), F32).ap()

        x_in = (ins["x_prompt"][0], ins["x_sample"][0])
        y_out = (outs[0][0], outs[1][0])

        def x_rows(q, t):
            return x_in[q][bass.ds((t - SEQ_TILES[q][0]) * P, P), :]

        def bcast(row, n):
            return row.to_broadcast([P, n])

        w_ada = ins["w_ada"][0].rearrange("(k p) n -> p k n", p=P)
        w_in = ins["w_in"][0].rearrange("(k p) n -> p k n", p=P)
        w_out = ins["w_out"][0].rearrange("(k p) n -> p k n", p=P)
        w_gu = ins["w_gate_up"][0].rearrange("e (k p) n -> e p k n", p=P)
        w_dn = ins["w_down"][0].rearrange("e (k p) n -> e p k n", p=P)

        S = {n: sem(n) for n in (
            "c_loaded small_loaded ada_bias c_silu cT_made cT_copied ident_made ident_zero"
            " consts_made mod_row mod_stored wsp_loaded wspT_made wspT_copied band_edge"
            " band_made bands_ready win_h_made win_l_made"
            " mod1_loaded x_loaded h_ready xT_made hT_h_made hT_l_made v_made v_gelu v_stats v_rs"
            " v_normed u_made u_gelu p_made p_kept p_copied s_made a_ready aT_made aT_copied pooled"
            " pooled_copied b_made b_copied"
            " mod2_loaded xr_loaded wout_h_made wout_l_made z2_h_made z2_l_made mix_made res_normed"
            " res_ready var_ready rstd_ready shift_ready x1_ready x1_stored h2_ready h2_stored h2T_made h2T_copied"
            " logit_made logit_read mod2_used"
            " rt_consts g_shifted g_exp top_diff top_exp sel_ready ranks_made pick_ready pick_used"
            " tab_made tab_ready eid_ready"
            " idx_ready gathered xgT_made xT_h_made xT_l_made gu_split_h gu_split_l dn_split_h"
            " dn_split_l gu_used dn_used silu_made act_ready aT_e_made aT_h_made aT_l_made y_ready"
            " y_idx y_scattered"
            " last_loaded y_loaded_0 y_loaded_1 x1_loaded_0 x1_loaded_1 y_summed f_taken f_var f_rstd f_shift f_gained f_ready"
            " f_stored_0 f_stored_1"
            " f_scaled dve_steps pool_steps dve_carrier pool_carrier sp_carrier"
        ).split()}
        ada_loaded = [sem(f"ada_loaded{s}") for s in range(3)]
        ada_used = sem("ada_used")
        win_loaded = [sem(f"win_loaded{k}") for k in range(KD)]
        wout_loaded = [sem(f"wout_loaded{k}") for k in range(KD)]
        gu_loaded = [sem(f"gu_loaded{c}") for c in range(4)]
        dn_loaded = [sem(f"dn_loaded{c}") for c in range(2)]

        def gu_slot(buf, e, c):
            n = (4 * e + c) % GU_SLOTS
            return buf[:, n, :, :] if isinstance(n, int) else buf[:, bass.ds(n, 1), :, :].rearrange("p a k n -> p (a k) n")

        def dn_slot(buf, e, c):
            n = (2 * e + c) % DN_SLOTS
            return buf[:, n, :, :] if isinstance(n, int) else buf[:, bass.ds(n, 1), :, :].rearrange("p a k n -> p (a k) n")

        block = ctx.enter_context(nc.Block())

        @block.sync
        def _(sp):
            sp.dma_start(c_in[0:KD, :], ins["c_prompt"].rearrange("a (k p) -> (a k) p", p=P)).then_inc(S["c_loaded"], 16)
            sp.dma_start(c_in[KD:2 * KD, :], ins["c_sample"].rearrange("a (k p) -> (a k) p", p=P)).then_inc(S["c_loaded"], 16)
            sp.dma_start(b_ada_sb[:], ins["b_ada"].to_broadcast([2, NMOD * D])).then_inc(S["ada_bias"], 16)
            n = 0
            for j in range(N_ADA):
                for kk in range(KD // CH):
                    if n >= 3:
                        sp.wait_ge(ada_used, n - 2)
                    sp.dma_start(ada[n % 3][:], w_ada[:, kk * CH:(kk + 1) * CH, j * ADA_N:(j + 1) * ADA_N]).then_inc(ada_loaded[n % 3], 16)
                    n += 1
                if j == 0:
                    for dst, src in ((vg[:], bcast(ins["v_norm_g"], AW)), (vb[:], bcast(ins["v_norm_b"], AW)),
                                     (w_pool[:], ins["w_pool"][0].rearrange("g c d -> c g d")),
                                     (router_w[:, :, 0:NG], ins["w_route_group"][0].rearrange("(k p) n -> p k n", p=P)),
                                     (router_w[:, :, NG:NG + NE], ins["w_route_expert"][0].rearrange("(k p) n -> p k n", p=P)),
                                     (router_b[:, 0:NG], bcast(ins["b_route_group"], NG)),
                                     (router_b[:, NG:NG + NE], bcast(ins["b_route_expert"].rearrange("a g e -> a (g e)"), NE))):
                        sp.dma_start(dst, src).then_inc(S["small_loaded"], 16)
                    with nc.allow_non_contiguous_dma(reason="1024 words in all"):
                        sp.dma_start(b_sp[:], ins["b_spatial"][0].rearrange("h q -> q h")).then_inc(S["small_loaded"], 16)
                        sp.dma_start(pool_s[:], ins["pool_scale"][0].rearrange("(g c) -> c g", c=P)).then_inc(S["small_loaded"], 16)
                    sp.dma_start(w_spT[:], ins["w_spatial"][0].rearrange("h q p -> q h p")).then_inc(S["wsp_loaded"], 16)
            for k in range(KD):
                if k >= 2:
                    sp.wait_ge(S["win_l_made"], k - 1)
                sp.dma_start(win_raw[k % 2][:], w_in[:, k, :]).then_inc(win_loaded[k], 16)
            sp.wait_ge(S["mod_row"], N_ADA)
            sp.dma_start(mod_d, mod[:]).then_inc(S["mod_stored"], 16)
            sp.wait_ge(S["mod_stored"], 16)

            def load_mod1(q):
                sp.dma_start(sc1[:], bcast(mod_d[q:q + 1, D:2 * D], D)).then_inc(S["mod1_loaded"], 16)
                sp.dma_start(sh1[:], bcast(mod_d[q:q + 1, 0:D], D)).then_inc(S["mod1_loaded"], 16)

            def load_x(t, q):
                sp.wait_ge(S["xT_made"], t)
                sp.dma_start(xs[:], x_rows(q, t)).then_inc(S["x_loaded"], 16)

            load_mod1(0)
            sp.dma_start(xs[:], x_rows(0, 0)).then_inc(S["x_loaded"], 16)
            for t in range(1, 4):
                load_x(t, 0)
            sp.wait_ge(S["h_ready"], 4)
            load_mod1(1)
            with sp.Fori(4, NT) as t:
                load_x(t, 1)
            for k in range(KD):
                if k >= 4:
                    sp.wait_ge(S["wout_l_made"], k - 3)
                elif k == 0:
                    sp.wait_ge(S["p_made"], NT)
                sp.dma_start(wout_raw[k % 4][:], w_out[:, k, :]).then_inc(wout_loaded[k], 16)
            sp.wait_ge(S["b_copied"], NT)
            sp.wait_ge(S["aT_copied"], NT)

            def load_mod2(q):
                for dst, m in ((g1b, 2), (sc2b, 4), (sh2b, 3)):
                    sp.dma_start(dst[:], bcast(mod_d[q:q + 1, m * D:(m + 1) * D], D)).then_inc(S["mod2_loaded"], 16)

            sp.dma_start(ln_g[:], bcast(ins["ln1_g"], D)).then_inc(S["mod2_loaded"], 16)
            sp.dma_start(ln_b[:], bcast(ins["ln1_b"], D)).then_inc(S["mod2_loaded"], 16)
            load_mod2(0)

            def second(t, q, first=False):
                if not first:
                    sp.wait_ge(S["res_ready"], t)
                sp.dma_start(xr[:], x_rows(q, t)).then_inc(S["xr_loaded"], 16)

            def store_h2(t):
                sp.wait_ge(S["h2_ready"], t + 1)
                sp.dma_start(h2_d[bass.ds(t * P, P), :], h2[:]).then_inc(S["h2_stored"], 16)
                xt = x1[:, t, :] if isinstance(t, int) else x1[:, bass.ds(t, 1), :].rearrange("p a n -> p (a n)")
                sp.dma_start(x1_d[bass.ds(t * P, P), :], xt).then_inc(S["x1_stored"], 16)

            second(0, 0, first=True)
            with sp.Fori(1, 4) as t:
                second(t, 0)
                store_h2(t - 1)
            store_h2(3)
            load_mod2(1)
            second(4, 1)
            with sp.Fori(5, NT) as t:
                second(t, 1)
                store_h2(t - 1)
            store_h2(NT - 1)

            def load_gu(e, c):
                if not (isinstance(e, int) and e == 0):
                    sp.wait_ge(gu_loaded[c], 16 * e)
                if not isinstance(e, int):
                    sp.sem_inc(S["sp_carrier"], 1)
                src = w_gu[e, :, 2 * c:2 * c + 2, :] if isinstance(e, int) else w_gu[bass.ds(e, 1), :, 2 * c:2 * c + 2, :].rearrange("a p k n -> p (a k) n")
                sp.dma_start(gu_slot(gu_raw, e, c), src).then_inc(gu_loaded[c], 16)

            def load_dn(e, c):
                if not (isinstance(e, int) and e == 0):
                    sp.wait_ge(dn_loaded[c], 16 * e)
                if not isinstance(e, int):
                    sp.sem_inc(S["sp_carrier"], 1)
                src = w_dn[e, :, 2 * c:2 * c + 2, :] if isinstance(e, int) else w_dn[bass.ds(e, 1), :, 2 * c:2 * c + 2, :].rearrange("a p k n -> p (a k) n")
                sp.dma_start(dn_slot(dn_raw, e, c), src).then_inc(dn_loaded[c], 16)

            sp.wait_ge(S["mix_made"], NT)
            sp.wait_ge(S["x1_stored"], 16 * NT)
            for n in range(GU_SLOTS):
                load_gu(n // 4, n % 4)
            for n in range(DN_SLOTS):
                load_dn(n // 2, n % 2)

            sp.wait_ge(S["eid_ready"], 1)
            n_blocks = sp.value_load(block_n[0:1, 0:1], min_val=NE, max_val=MAXBLK)

            def expert_of(i):
                return sp.value_load(block_e[0:1, bass.ds(i, 1)], min_val=0, max_val=NE - 1)

            def refill(i, first=False):
                e, e_next = expert_of(i), expert_of(i + 1)
                with sp.If(e < e_next):
                    sp.wait_ge(S["gu_used"], 4 * i + 1)
                    sp.sem_inc(S["sp_carrier"], 1)
                    load_gu(e_next, 3)
                    with sp.If(e_next < NE - 1):
                        for c in range(3):
                            sp.wait_ge(S["gu_used"], 4 * i + c + 2)
                            sp.sem_inc(S["sp_carrier"], 1)
                            load_gu((e_next + 1).with_bounds(min_val=0, max_val=NE - 1), c)
                if not first:
                    with sp.If(expert_of(i - 1) < e):
                        with sp.If(e < NE - 1):
                            for c in range(2):
                                sp.wait_ge(S["dn_used"], 2 * i + c - 1)
                                sp.sem_inc(S["sp_carrier"], 1)
                                load_dn((e + 1).with_bounds(min_val=0, max_val=NE - 1), c)

            refill(0, first=True)
            with sp.Fori(1, n_blocks) as i:
                refill(i)

            sp.wait_ge(S["y_ready"], n_blocks + 1)
            for dst, src in ((g2b[0], mod_d[0:1, 5 * D:6 * D]), (g2b[1], mod_d[1:2, 5 * D:6 * D]),
                             (ln2_g, ins["ln2_g"]), (ln2_b, ins["ln2_b"])):
                sp.dma_start(dst[:], bcast(src, D)).then_inc(S["last_loaded"], 16)

            def load_x1(t, s):
                sp.dma_start(x1t[s][:], x1_d[bass.ds(t * P, P), :]).then_inc(S[f"x1_loaded_{s}"], 16)

            def load_y(t, s):
                sp.dma_start(y0[s][:], y_d[bass.ds(t * P, P), :]).then_inc(S[f"y_loaded_{s}"], 16)
                sp.dma_start(y1[s][:], y_d[bass.ds(T + t * P, P), :]).then_inc(S[f"y_loaded_{s}"], 16)

            load_x1(0, 0)
            load_x1(1, 1)
            sp.wait_ge(S["y_scattered"], n_blocks * 16)
            load_y(0, 0)
            load_y(1, 1)
            with sp.Fori(1, NT // 2) as i:
                for s in range(2):
                    sp.wait_ge(S["y_summed"], 2 * i + s - 1)
                    load_y(2 * i + s, s)
                    sp.wait_ge(S["f_taken"], 2 * i + s - 1)
                    load_x1(2 * i + s, s)

        @block.gpsimd
        def _(pool):
            st = Steps(pool, S["pool_steps"], S["pool_carrier"])
            st.done(pool.memset(ident[:], 0.0))
            st.sync()
            nc.gpsimd.affine_select(out=ident[:], in_=ident[:], compare_op=ALU.not_equal, fill=1.0, base=0,
                                    pattern=[[-1, P]], channel_multiplier=1).then_inc(S["ident_made"], 1)
            st.done(pool.memset(half_neg[:], -0.5))
            nc.gpsimd.iota(band_prev[:, 0, :], pattern=[[1, P]], base=0, channel_multiplier=0,
                           allow_small_or_imprecise_dtypes=True).then_inc(S["consts_made"], 1)
            pool.wait_ge(S["band_edge"], 1)
            for g, w in enumerate(WINDOWS):
                h = w // 2
                for b, shift in [(bands[:, v, g, :], 0) for v in range(3)] + [(band_prev[:, g, :], -P), (band_next[:, g, :], P)]:
                    st.done(nc.gpsimd.affine_select(out=b, in_=b, compare_op=ALU.is_ge, fill=0.0, base=shift + h,
                                                    pattern=[[-1, P]], channel_multiplier=1))
                    st.sync()
                    nc.gpsimd.affine_select(out=b, in_=b, compare_op=ALU.is_gt, fill=0.0, base=h - shift,
                                            pattern=[[1, P]], channel_multiplier=-1).then_inc(S["band_made"], 1)

            def modulate(t):
                if isinstance(t, int) and t == 0:
                    pool.wait_ge(S["mod1_loaded"], 32)
                    st.done(nc.gpsimd.tensor_scalar(sc1[:], sc1[:], 1.0, None, ALU.add))
                    st.sync()
                if isinstance(t, int) and t == 4:
                    pool.wait_ge(S["mod1_loaded"], 64)
                    st.done(nc.gpsimd.tensor_scalar(sc1[:], sc1[:], 1.0, None, ALU.add))
                    st.sync()
                pool.wait_ge(S["x_loaded"], 16 * (t + 1))
                st.done(nc.gpsimd.tensor_tensor(xs[:], xs[:], sc1[:], ALU.mult))
                st.sync()
                nc.gpsimd.tensor_tensor(xs[:], xs[:], sh1[:], ALU.add).then_inc(S["h_ready"], 1)

            def v_power(t):
                pool.wait_ge(S["v_stats"], t + 1)
                nc.gpsimd.tensor_tensor(v_rstd[:], v_mv[:, 1:2], half_neg[:], ALU.pow).then_inc(S["v_rs"], 1)

            modulate(0)
            modulate(1)
            for t in (0, 1, 2):
                v_power(t)
                modulate(t + 2)
            with pool.Fori(3, NT - 2) as t:
                st.enter(t - 3, 1)
                v_power(t)
                modulate(t + 2)
            st.leave(NT - 5)
            v_power(NT - 2)
            v_power(NT - 1)

            def second(t):
                pool.wait_ge(S["var_ready"], t + 1)
                nc.gpsimd.tensor_tensor(rstd[:], mv[:, 1:2], half_neg[:], ALU.pow).then_inc(S["rstd_ready"], 1)
                pool.wait_ge(S["x1_ready"], t + 1)
                if not (isinstance(t, int) and t == 0):
                    pool.wait_ge(S["h2_stored"], 16 * t)
                    pool.wait_ge(S["h2T_made"], t)
                st.done(nc.gpsimd.tensor_tensor(h2[:], x1[:, t, :] if isinstance(t, int) else x1[:, bass.ds(t, 1), :].rearrange("p a n -> p (a n)"), sc2b[:], ALU.mult))
                st.sync()
                nc.gpsimd.tensor_tensor(h2[:], h2[:], sh2b[:], ALU.add).then_inc(S["h2_ready"], 1)

            def plus_one(n):
                pool.wait_ge(S["mod2_loaded"], 16 * n)
                st.done(nc.gpsimd.tensor_scalar(sc2b[:], sc2b[:], 1.0, None, ALU.add))
                st.sync()

            plus_one(5)
            second(0)
            with pool.Fori(1, 4) as t:
                st.enter(t - 1, 1)
                second(t)
            st.leave(3)
            plus_one(8)
            with pool.Fori(4, NT) as t:
                st.enter(t - 4, 1)
                second(t)
            st.leave(NT - 4)

            pool.wait_ge(S["logit_read"], NT)
            pool.wait_ge(S["h2_stored"], 16 * NT)
            st.done(pool.memset(ones[:], 1.0))
            st.done(pool.memset(tri[:], 1.0))
            st.sync()
            nc.gpsimd.affine_select(out=tri[:], in_=tri[:], compare_op=ALU.is_gt, fill=0.0, base=0,
                                    pattern=[[1, P]], channel_multiplier=-1).then_inc(S["rt_consts"], 1)
            nc.gpsimd.iota(iota_r[:], pattern=[[1, P]], base=0, channel_multiplier=0,
                           allow_small_or_imprecise_dtypes=True).then_inc(S["rt_consts"], 1)
            nc.gpsimd.iota(rev[:], pattern=[[-1, NE]], base=NE, channel_multiplier=0,
                           allow_small_or_imprecise_dtypes=True).then_inc(S["rt_consts"], 1)
            nc.gpsimd.iota(tok[:], pattern=[[T, 2], [P, NT]], base=0, channel_multiplier=1,
                           allow_small_or_imprecise_dtypes=True).then_inc(S["rt_consts"], 1)
            nc.gpsimd.iota(cmp_e[:], pattern=[[1, TAB], [0, NE]], base=0, channel_multiplier=0,
                           allow_small_or_imprecise_dtypes=True).then_inc(S["rt_consts"], 1)
            nc.gpsimd.iota(cmp[:], pattern=[[0, NE], [P, NT]], base=0, channel_multiplier=0,
                           allow_small_or_imprecise_dtypes=True).then_inc(S["rt_consts"], 1)

            pool.wait_ge(S["tab_ready"], 1)
            pool.wait_ge(S["eid_ready"], 1)
            n_blocks = pool.value_load(block_n[0:1, 0:1], min_val=NE, max_val=MAXBLK)
            last_block = pool.value_load(block_n[0:1, 1:2], min_val=NE - 1, max_val=MAXBLK - 1)

            def gather(i, first=False):
                if not first:
                    pool.wait_ge(S["gathered"], 16 * i)
                    pool.wait_ge(S["xgT_made"], i)
                nc.gpsimd.tensor_copy(g_idx[:], table_i[:, 0, bass.ds(i, 1)]).then_inc(S["idx_ready"], 1)
                pool.wait_ge(S["idx_ready"], i + 1)
                pool.sem_inc(S["pool_carrier"], 1)
                nc.gpsimd.indirect_dma_start(out=xg[:], out_offset=None, in_=h2_d,
                                             in_offset=bass.IndirectOffsetOnAxis(ap=g_idx[:, 0:1], axis=0)).then_inc(S["gathered"], 16)

            def scatter(i):
                if not (isinstance(i, int) and i == 0):
                    pool.wait_ge(S["y_scattered"], 16 * i)
                nc.gpsimd.tensor_copy(s_idx[:], table_i[:, 1, bass.ds(i, 1)]).then_inc(S["y_idx"], 1)
                nc.gpsimd.tensor_copy(s_w[:], table[:, 2, bass.ds(i, 1)]).then_inc(S["y_idx"], 1)
                pool.wait_ge(S["y_idx"], 2 * i + 2)
                pool.wait_ge(S["y_ready"], i + 2)
                pool.sem_inc(S["pool_carrier"], 1)
                nc.gpsimd.indirect_dma_start(out=y_d, out_offset=bass.IndirectOffsetOnAxis(ap=s_idx[:, 0:1], axis=0),
                                             in_=y_sb[:], in_offset=None, bounds_check=PAIRS - 1,
                                             oob_is_err=False).then_inc(S["y_scattered"], 16)

            gather(0, first=True)
            gather(1)
            gather(2)
            scatter(0)
            with pool.Fori(2, n_blocks) as i:
                gather(i + 1)
                scatter(i - 1)
            scatter(last_block)
            pool.wait_ge(S["gathered"], 16 * (n_blocks + 1))
            pool.sem_inc(S["pool_carrier"], 1)

            def f_power(t, s):
                pool.wait_ge(S["f_var"], t + 1)
                nc.gpsimd.tensor_tensor(rstd2[s][:], mv2[s][:, 1:2], half_neg[:], ALU.pow).then_inc(S["f_rstd"], 1)

            def f_add(i, s):
                pool.wait_ge(S["f_gained"], 2 * i + s + 1)
                if not isinstance(i, int):
                    pool.wait_ge(S[f"f_stored_{s}"], 16 * i)
                nc.gpsimd.tensor_tensor(fin[s][:], r2[s][:], ln2_b[:], ALU.add).then_inc(S["f_ready"], 1)

            f_power(0, 0)
            f_power(1, 1)
            f_add(0, 0)
            f_power(2, 0)
            f_add(0, 1)
            f_power(3, 1)
            with pool.Fori(1, NT // 2 - 1) as i:
                for s in range(2):
                    f_add(i, s)
                    f_power(2 * i + s + 2, s)
            for s in range(2):
                pool.wait_ge(S["f_gained"], NT - 1 + s)
                pool.wait_ge(S[f"f_stored_{s}"], 16 * (NT // 2 - 1))
                nc.gpsimd.tensor_tensor(fin[s][:], r2[s][:], ln2_b[:], ALU.add).then_inc(S["f_ready"], 1)

        @block.scalar
        def _(act):
            act.wait_ge(S["c_loaded"], 32)
            nc.scalar.activation(c_act[:], c_in[:], ACT.Silu).then_inc(S["c_silu"], 1)
            act.wait_ge(S["cT_made"], 1)
            nc.scalar.activation(cT[:], ps[0][:, 0:2 * KD], ACT.Copy).then_inc(S["cT_copied"], 1)
            act.wait_ge(S["wspT_made"], 1)
            nc.scalar.activation(w_spT[:], ps[1][:].rearrange("p (h q) -> p h q", h=HEADS), ACT.Copy).then_inc(S["wspT_copied"], 1)
            for k in range(KD):
                act.wait_ge(win_loaded[k], 16)
                nc.scalar.activation(win_h[:, k, :], win_raw[k % 2][:], ACT.Copy).then_inc(S["win_h_made"], 1)

            def high_x(t, s):
                act.wait_ge(S["xT_made"], t + 1)
                if not (isinstance(t, int) and t < 2):
                    act.wait_ge(S["p_made"], t - 1)
                for b in range(2):
                    last = nc.scalar.activation(hT_h[s][:, 4 * b:4 * b + 4, :], ps[b][:].rearrange("p (k m) -> p k m", k=4), ACT.Copy)
                last.then_inc(S["hT_h_made"], 1)

            def z_tile(t, s, nxt, prev):
                act.wait_ge(S["v_made"], t + 1)
                if not (isinstance(t, int) and t == 0):
                    act.wait_ge(S["s_made"], t)
                nc.scalar.activation(v_sb[:], ps[2][:], ACT.Gelu_apprx_tanh).then_inc(S["v_gelu"], 1)
                if nxt:
                    high_x(t + 1, 1 - s)
                act.wait_ge(S["u_made"], t + 1)
                if not (isinstance(t, int) and t == 0):
                    act.wait_ge(S["a_ready"], t)
                nc.scalar.activation(u_sb[:], ps[3][:], ACT.Gelu_apprx_tanh).then_inc(S["u_gelu"], 1)
                if prev:
                    copy_aT(t - 1)
                act.wait_ge(S["p_made"], t + 1)
                if not (isinstance(t, int) and t < 2):
                    act.wait_ge(S["p_kept"], t - 1)
                nc.scalar.activation(p_sb[s][:], ps[4][:], ACT.Copy).then_inc(S["p_copied"], 1)

            def copy_aT(t):
                act.wait_ge(S["aT_made"], t + 1)
                dst = z2T[:, t, 0:4, :] if isinstance(t, int) else z2T[:, bass.ds(t, 1), 0:4, :].rearrange("p a k m -> p (a k) m")
                nc.scalar.activation(dst, ps[6][:].rearrange("p (k m) -> p k m", k=4), ACT.Copy).then_inc(S["aT_copied"], 1)

            high_x(0, 0)
            z_tile(0, 0, True, False)
            z_tile(1, 1, True, True)
            with act.Fori(1, NT // 2 - 1) as i:
                for s in range(2):
                    z_tile(2 * i + s, s, True, True)
            z_tile(NT - 2, 0, True, True)
            z_tile(NT - 1, 1, False, True)
            copy_aT(NT - 1)

            for k in range(KD):
                act.wait_ge(wout_loaded[k], 16)
                nc.scalar.activation(wout_h[:, k, :], wout_raw[k % 4][:], ACT.Copy).then_inc(S["wout_h_made"], 1)
            act.wait_ge(S["b_copied"], NT)

            def high_z(t, s):
                if not (isinstance(t, int) and t < 2):
                    act.wait_ge(S["mix_made"], t - 1)
                src = z2T[:, t, :, :] if isinstance(t, int) else z2T[:, bass.ds(t, 1), :, :].rearrange("p a k m -> p (a k) m")
                nc.scalar.activation(z2_h[s][:], src, ACT.Copy).then_inc(S["z2_h_made"], 1)

            def normalise(t):
                act.wait_ge(S["shift_ready"], t + 1)
                nc.scalar.activation(res[:], res[:], ACT.Identity, scale=rstd[:, 0:1], bias=nmr[:, 0:1]).then_inc(S["res_normed"], 1)

            def copy_h2T(t):
                act.wait_ge(S["h2T_made"], t + 1)
                if not (isinstance(t, int) and t == 0):
                    act.wait_ge(S["logit_made"], t)
                for b in range(2):
                    last = nc.scalar.activation(h2T[:, 4 * b:4 * b + 4, :], ps[4 + b][:].rearrange("p (k m) -> p k m", k=4), ACT.Copy)
                last.then_inc(S["h2T_copied"], 1)

            high_z(0, 0)
            high_z(1, 1)
            normalise(0)
            high_z(2, 0)
            normalise(1)
            high_z(3, 1)
            copy_h2T(0)
            with act.Fori(1, NT // 2 - 1) as i:
                for s in range(2):
                    normalise(2 * i + s)
                    high_z(2 * i + s + 2, s)
                    copy_h2T(2 * i + s - 1)
            for t in (NT - 2, NT - 1):
                normalise(t)
                copy_h2T(t - 1)
            copy_h2T(NT - 1)

            act.wait_ge(S["g_shifted"], 1)
            nc.scalar.activation(g_a[:], g_a[:], ACT.Exp).then_inc(S["g_exp"], 1)
            act.wait_ge(S["top_diff"], 1)
            nc.scalar.activation(ex[:], v2[:], ACT.Exp).then_inc(S["top_exp"], 1)

            def high_gu(e, c):
                act.wait_ge(gu_loaded[c], 16 * (e + 1))
                nc.scalar.activation(gu_slot(gu_h, e, c), gu_slot(gu_raw, e, c), ACT.Copy).then_inc(S["gu_split_h"], 1)

            def high_dn(e, c):
                act.wait_ge(dn_loaded[c], 16 * (e + 1))
                nc.scalar.activation(dn_slot(dn_h, e, c), dn_slot(dn_raw, e, c), ACT.Copy).then_inc(S["dn_split_h"], 1)

            def silu(i):
                act.wait_ge(S["gu_used"], 4 * i + 4)
                if not (isinstance(i, int) and i == 0):
                    act.wait_ge(S["act_ready"], i)
                nc.scalar.activation(act_s[:], ps[0][:], ACT.Silu).then_inc(S["silu_made"], 1)

            def high_aT(i):
                act.wait_ge(S["aT_e_made"], i + 1)
                nc.scalar.activation(aT_h[:], ps[4][:].rearrange("p (k m) -> p k m", k=KE), ACT.Copy).then_inc(S["aT_h_made"], 1)

            def high_xT(i):
                act.wait_ge(S["xgT_made"], i + 1)
                for b in range(2):
                    last = nc.scalar.activation(xT_h[:, 4 * b:4 * b + 4, :], ps[2 + b][:].rearrange("p (k m) -> p k m", k=4), ACT.Copy)
                last.then_inc(S["xT_h_made"], 1)

            act.sem_inc(S["y_ready"], 1)

            def weigh(i):
                act.wait_ge(S["dn_used"], 2 * i + 2)
                act.wait_ge(S["y_idx"], 2 * i + 2)
                if not (isinstance(i, int) and i == 0):
                    act.wait_ge(S["y_scattered"], 16 * i)
                for b in range(2):
                    last = nc.scalar.activation(y_sb[:, 512 * b:512 * (b + 1)], ps[5 + b][:], ACT.Copy, scale=s_w[:, 0:1])
                last.then_inc(S["y_ready"], 1)

            for c in range(4):
                high_gu(0, c)
            act.wait_ge(S["tab_ready"], 1)
            for c in range(2):
                high_dn(0, c)
            n_blocks = act.value_load(block_n[0:1, 0:1], min_val=NE, max_val=MAXBLK)
            last_block = act.value_load(block_n[0:1, 1:2], min_val=NE - 1, max_val=MAXBLK - 1)

            def expert_of(i):
                return act.value_load(block_e[0:1, bass.ds(i, 1)], min_val=0, max_val=NE - 1)

            high_xT(0)

            def expert_block(i, first=False):
                e, e_next = expert_of(i), expert_of(i + 1)
                with act.If(e < e_next):
                    for c in range(3):
                        high_gu(e_next, c)
                silu(i)
                high_xT(i + 1)
                with act.If(e < e_next):
                    high_gu(e_next, 3)
                if not first:
                    weigh(i - 1)
                    with act.If(expert_of(i - 1) < e):
                        for c in range(2):
                            high_dn(e, c)
                high_aT(i)

            expert_block(0, first=True)
            expert_block(1)
            with act.Fori(2, n_blocks) as i:
                expert_block(i)
            weigh(last_block)

            def f_norm(t, s):
                act.wait_ge(S["f_shift"], t + 1)
                nc.scalar.activation(r2[s][:], r2[s][:], ACT.Identity, scale=rstd2[s][:, 0:1], bias=nmr2[s][:, 0:1]).then_inc(S["f_scaled"], 1)

            def store_y(t, s, q):
                act.wait_ge(S["f_ready"], t + 1)
                nc.scalar.dma_start(y_out[q][bass.ds((t - SEQ_TILES[q][0]) * P, P), :], fin[s][:]).then_inc(S[f"f_stored_{s}"], 16)

            f_norm(0, 0)
            f_norm(1, 1)
            for q, (lo, hi) in enumerate(SEQ_TILES):
                last = hi if hi < NT else NT - 2
                with act.Fori(lo // 2, last // 2) as i:
                    for s in range(2):
                        store_y(2 * i + s, s, q)
                        f_norm(2 * i + s + 2, s)
            for s in range(2):
                store_y(NT - 2 + s, s, 1)
            for s in range(2):
                act.wait_ge(S[f"f_stored_{s}"], 16 * NT // 2)

        @block.vector
        def _(dve):
            st = Steps(dve, S["dve_steps"], S["dve_carrier"])
            nv = nc.vector

            dve.wait_ge(S["consts_made"], 1)
            for g, w in enumerate(WINDOWS):
                h = w // 2
                st.done(nv.tensor_scalar(bands[:, 0, g, :], band_prev[:, 0, :], float(h), float(w), ALU.add, ALU.min))
                st.done(nv.tensor_scalar(bands[:, 2, g, :], band_prev[:, 0, :], -1.0, float(P + h), ALU.mult, ALU.add))
                st.done(nv.memset(bands[:, 1, g, :], 1.0 / w))
                st.done(nv.memset(band_next[:, g, :], 1.0 / w))
                st.sync()
                st.done(nv.tensor_scalar(bands[:, 2, g, :], bands[:, 2, g, :], float(w), None, ALU.min))
                st.done(nv.reciprocal(bands[:, 0, g, :], bands[:, 0, g, :]))
                st.sync()
                st.done(nv.reciprocal(bands[:, 2, g, :], bands[:, 2, g, :]))
            st.sync()
            for g, w in enumerate(WINDOWS):
                last = nv.memset(band_prev[:, g, :], 1.0 / w)
            last.then_inc(S["band_edge"], 1)
            dve.wait_ge(S["band_made"], 5 * len(WINDOWS))
            dve.wait_ge(S["ident_made"], 1)
            last = nv.tensor_tensor(bands[:].rearrange("p v g m -> p (v g) m"), bands[:].rearrange("p v g m -> p (v g) m"),
                                    ident[:, None, :].to_broadcast([P, 12, P]), ALU.subtract)
            last.then_inc(S["bands_ready"], 1)

            dve.wait_ge(S["ada_bias"], 16)
            for j in range(N_ADA):
                dve.wait_ge(ada_used, (j + 1) * KD // CH)
                c = slice(j * ADA_N, (j + 1) * ADA_N)
                nv.tensor_tensor(mod[:, c], ps[2 + j % 2][0:2, :], b_ada_sb[:, c], ALU.add).then_inc(S["mod_row"], 1)
            for k in range(KD):
                dve.wait_ge(S["win_h_made"], k + 1)
                nv.tensor_tensor(win_l[:, k, :], win_raw[k % 2][:], win_h[:, k, :].bitcast(F32), ALU.subtract).then_inc(S["win_l_made"], 1)
            dve.wait_ge(S["small_loaded"], 16 * 9)
            dve.wait_ge(S["mod_stored"], 16)

            def low_x(t, s):
                dve.wait_ge(S["hT_h_made"], t + 1)
                for b in range(2):
                    last = nv.tensor_tensor(hT_l[s][:, 4 * b:4 * b + 4, :], ps[b][:].rearrange("p (k m) -> p k m", k=4),
                                            hT_h[s][:, 4 * b:4 * b + 4, :].bitcast(F32), ALU.subtract)
                last.then_inc(S["hT_l_made"], 1)

            def b_out(t):
                dve.wait_ge(S["b_made"], t + 1)
                dst = z2T[:, t, 4:8, :] if isinstance(t, int) else z2T[:, bass.ds(t, 1), 4:8, :].rearrange("p a k m -> p (a k) m")
                nv.tensor_tensor(dst, ps[6][:].rearrange("p (k m) -> p k m", k=4),
                                 pool_s[:, :, None].to_broadcast([P, 4, P]), ALU.mult).then_inc(S["b_copied"], 1)

            def pooled_copy(t):
                dve.wait_ge(S["pooled"], t + 1)
                if not (isinstance(t, int) and t == 0):
                    dve.wait_ge(S["b_made"], t)
                nv.tensor_copy(pooledT[:], ps[7][:].rearrange("p (g m) -> p g m", g=4)).then_inc(S["pooled_copied"], 1)

            def z_tile(t, s, nxt, b2, pl):
                if not (isinstance(t, int) and t < 2):
                    dve.wait_ge(S["pooled"], t - 1)
                    nv.tensor_copy(p_old[:], p_sb[s][:]).then_inc(S["p_kept"], 1)
                dve.wait_ge(S["v_gelu"], t + 1)
                st.done(nv.bn_stats(v_stat[:], v_sb[:]))
                st.sync_apart()
                st.done(nv.bn_aggr(v_mv[:], v_stat[:]))
                st.sync()
                nv.tensor_scalar(v_mv[:, 1:2], v_mv[:, 1:2], EPS, None, ALU.add).then_inc(S["v_stats"], 1)
                dve.wait_ge(S["v_rs"], t + 1)
                st.done(nv.tensor_scalar(v_sb[:], v_sb[:], v_mv[:, 0:1], v_rstd[:, 0:1], ALU.subtract, ALU.mult))
                st.sync()
                st.done(nv.tensor_tensor(v_sb[:], v_sb[:], vg[:], ALU.mult))
                st.sync()
                nv.tensor_tensor(v_sb[:], v_sb[:], vb[:], ALU.add).then_inc(S["v_normed"], 1)
                if nxt:
                    low_x(t + 1, 1 - s)
                if b2:
                    b_out(t - 2)
                dve.wait_ge(S["s_made"], t + 1)
                dve.wait_ge(S["u_gelu"], t + 1)
                if not (isinstance(t, int) and t == 0):
                    dve.wait_ge(S["aT_made"], t)
                for h in range(HEADS):
                    c = slice(h * P, (h + 1) * P)
                    last = nv.scalar_tensor_tensor(a_sb[:, c], ps[5][:, c], b_sp[:, h:h + 1], u_sb[:, c], ALU.add, ALU.mult)
                last.then_inc(S["a_ready"], 1)
                if pl:
                    pooled_copy(t - 1)

            low_x(0, 0)
            z_tile(0, 0, True, False, False)
            z_tile(1, 1, True, False, True)
            with dve.Fori(1, NT // 2 - 1) as i:
                st.enter(i - 1, 8)
                for s in range(2):
                    z_tile(2 * i + s, s, True, True, True)
            st.leave(NT // 2 - 2)
            z_tile(NT - 2, 0, True, True, True)
            z_tile(NT - 1, 1, False, True, True)
            b_out(NT - 2)
            pooled_copy(NT - 1)
            b_out(NT - 1)

            for k in range(KD):
                dve.wait_ge(S["wout_h_made"], k + 1)
                nv.tensor_tensor(wout_l[:, k, :], wout_raw[k % 4][:], wout_h[:, k, :].bitcast(F32), ALU.subtract).then_inc(S["wout_l_made"], 1)

            def low_z(t, s):
                dve.wait_ge(S["z2_h_made"], t + 1)
                src = z2T[:, t, :, :] if isinstance(t, int) else z2T[:, bass.ds(t, 1), :, :].rearrange("p a k m -> p (a k) m")
                nv.tensor_tensor(z2_l[s][:], src, z2_h[s][:].bitcast(F32), ALU.subtract).then_inc(S["z2_l_made"], 1)

            def second(t, s):
                dve.wait_ge(S["mix_made"], t + 1)
                if not (isinstance(t, int) and t == 0):
                    dve.wait_ge(S["x1_ready"], t)
                for b in range(2):
                    c = slice(512 * b, 512 * (b + 1))
                    st.done(nv.tensor_tensor(res[:, c], ps[2 * s + b][:], g1b[:, c], ALU.mult))
                st.sync()
                dve.wait_ge(S["xr_loaded"], 16 * (t + 1))
                nv.scalar_tensor_tensor(res[:], xr[:], ALPHA, res[:], ALU.mult, ALU.add).then_inc(S["res_ready"], 1)
                dve.wait_ge(S["res_ready"], t + 1)
                for b in range(2):
                    st.done(nv.bn_stats(stat[:, b, :], res[:, 512 * b:512 * (b + 1)]))
                st.sync_apart()
                st.done(nv.bn_aggr(mv[:], stat[:].rearrange("p a b -> p (a b)")))
                st.sync()
                nv.tensor_scalar(mv[:, 1:2], mv[:, 1:2], EPS, None, ALU.add).then_inc(S["var_ready"], 1)
                dve.wait_ge(S["rstd_ready"], t + 1)
                nv.scalar_tensor_tensor(nmr[:], mv[:, 0:1], -1.0, rstd[:], ALU.mult, ALU.mult).then_inc(S["shift_ready"], 1)

            def x1_out(t):
                dve.wait_ge(S["res_normed"], t + 1)
                st.done(nv.tensor_tensor(res[:], res[:], ln_g[:], ALU.mult))
                st.sync()
                dst = x1[:, t, :] if isinstance(t, int) else x1[:, bass.ds(t, 1), :].rearrange("p a n -> p (a n)")
                nv.tensor_tensor(dst, res[:], ln_b[:], ALU.add).then_inc(S["x1_ready"], 1)

            def logits_out(t):
                dve.wait_ge(S["logit_made"], t + 1)
                dst = logits[:, t, :] if isinstance(t, int) else logits[:, bass.ds(t, 1), :].rearrange("p a n -> p (a n)")
                nv.tensor_tensor(dst, ps[6][:, 0:NG + NE], router_b[:], ALU.add).then_inc(S["logit_read"], 1)

            low_z(0, 0)
            low_z(1, 1)
            dve.wait_ge(S["mod2_loaded"], 16 * 5)
            def norm_tile(t, s, nxt=True, prev=True):
                second(t, s)
                x1_out(t)
                if nxt:
                    low_z(t + 2, s)
                if prev:
                    logits_out(t - 2)

            norm_tile(0, 0, prev=False)
            norm_tile(1, 1, prev=False)
            norm_tile(2, 0)
            norm_tile(3, 1)
            dve.wait_ge(S["mod2_loaded"], 16 * 8)
            with dve.Fori(2, NT // 2 - 1) as i:
                st.enter(i - 2, 2 * 6)
                for s in range(2):
                    norm_tile(2 * i + s, s)
            st.leave(NT // 2 - 3)
            norm_tile(NT - 2, 0, nxt=False)
            norm_tile(NT - 1, 1, nxt=False)
            logits_out(NT - 2)
            logits_out(NT - 1)

            dve.wait_ge(S["rt_consts"], 6)
            G, E = logits[:, :, 0:NG], logits[:, :, NG:NG + NE]

            def step(ins):
                st.done(ins)
                st.sync()

            def first_max(dst, tmp, mx, src, n):
                step(nv.tensor_tensor(tmp, src, mx[:, :, None].to_broadcast([P, NT, n]), ALU.is_ge))
                step(nv.tensor_tensor(tmp, tmp, rev[:, None, 0:n].to_broadcast([P, NT, n]), ALU.mult))
                step(nv.tensor_reduce(em[:], tmp, AX.X, ALU.max))
                step(nv.tensor_tensor(dst, tmp, em[:, :, None].to_broadcast([P, NT, n]), ALU.is_equal))

            step(nv.tensor_reduce(gmax[:], G, AX.X, ALU.max))
            nv.tensor_tensor(g_a[:], G, gmax[:, :, None].to_broadcast([P, NT, NG]), ALU.subtract).then_inc(S["g_shifted"], 1)
            first_max(g_b[:], g_b[:], gmax, G, NG)
            step(nv.tensor_scalar(g_b[:], g_b[:], -1.0, FAR, ALU.add, ALU.mult))
            step(nv.tensor_tensor(e2[:].rearrange("p t (g e) -> p t g e", g=NG), E.rearrange("p t (g e) -> p t g e", g=NG),
                                  g_b[:, :, :, None].to_broadcast([P, NT, NG, EPG]), ALU.add))
            step(nv.tensor_reduce(v1[:], e2[:], AX.X, ALU.max))
            first_max(oh[0][:], e_t[:], v1, e2[:], NE)
            step(nv.scalar_tensor_tensor(e2[:], oh[0][:], -2 * FAR, e2[:], ALU.mult, ALU.add))
            step(nv.tensor_reduce(v2[:], e2[:], AX.X, ALU.max))
            first_max(oh[1][:], e_t[:], v2, e2[:], NE)
            nv.tensor_tensor(both[:], oh[0][:], oh[1][:], ALU.add).then_inc(S["sel_ready"], 1)
            nv.tensor_tensor(v2[:], v2[:], v1[:], ALU.subtract).then_inc(S["top_diff"], 1)
            dve.wait_ge(S["g_exp"], 1)
            step(nv.tensor_reduce(gw[:], g_a[:], AX.X, ALU.add))
            step(nv.reciprocal(gw[:], gw[:]))
            dve.wait_ge(S["top_exp"], 1)
            step(nv.tensor_scalar(den[:], ex[:], 1.0, None, ALU.add))
            step(nv.reciprocal(den[:], den[:]))
            step(nv.tensor_tensor(vals[:, 2, 0, :], den[:], gw[:], ALU.mult))
            step(nv.tensor_tensor(vals[:, 2, 1, :], vals[:, 2, 0, :], ex[:], ALU.mult))
            st.done(nv.tensor_copy(vals[:, 0, 0, :], tok[:, 0, :]))
            st.done(nv.tensor_copy(vals[:, 0, 1, :], tok[:, 0, :]))
            st.done(nv.tensor_scalar(vals[:, 1, :, :], tok[:], -NO_ROW, None, ALU.add))
            st.done(nv.memset(before[:, 0, :], 0.0))
            dve.wait_ge(S["ranks_made"], 1)
            for t in range(NT):
                st.sync()
                st.done(nv.tensor_tensor(before[:, t + 1, :], before[:, t, :], ps[1][:, NE * t:NE * (t + 1)], ALU.add))
            st.sync()
            step(nv.tensor_tensor(pos[:], before[:, 0:NT, :], ps[0][:, 0:NT * NE].rearrange("p (t e) -> p t e", t=NT), ALU.add))
            step(nv.tensor_tensor(cmp[:], before[:, NT, :, None].to_broadcast([P, NE, NT]), cmp[:], ALU.is_gt))
            step(nv.tensor_reduce(nblk[:], cmp[:], AX.X, ALU.add))
            step(nv.tensor_scalar(nblk[:], nblk[:], 1.0, None, ALU.max))
            step(nv.tensor_copy(cum[0][:], nblk[:]))
            k, d = 0, 1
            while d < NE:
                st.done(nv.tensor_copy(cum[1 - k][:, 0:d], cum[k][:, 0:d]))
                st.done(nv.tensor_tensor(cum[1 - k][:, d:NE], cum[k][:, d:NE], cum[k][:, 0:NE - d], ALU.add))
                st.sync()
                k, d = 1 - k, 2 * d
            end = cum[k]
            st.done(nv.tensor_copy(block_n[:, 0:1], end[0:1, NE - 1:NE]))
            st.done(nv.tensor_scalar(block_n[:, 1:2], end[0:1, NE - 1:NE], -1.0, None, ALU.add))
            step(nv.tensor_tensor(cmp_e[:], end[0:1, None, :].to_broadcast([1, TAB, NE]), cmp_e[:], ALU.is_le))
            step(nv.tensor_reduce(eid_f[:], cmp_e[:], AX.X, ALU.add))
            step(nv.tensor_scalar(eid_f[:], eid_f[:], float(NE - 1), None, ALU.min))
            nv.tensor_copy(block_e[:], eid_f[:]).then_inc(S["eid_ready"], 1)
            step(nv.tensor_tensor(cum[1 - k][:], end[:], nblk[:], ALU.subtract))
            step(nv.tensor_scalar(cum[1 - k][:], cum[1 - k][:], float(P), None, ALU.mult))
            step(nv.tensor_tensor(pos[:], pos[:], cum[1 - k][:, None, :].to_broadcast([P, NT, NE]), ALU.add))
            for c in range(2):
                step(nv.tensor_tensor(e_t[:], pos[:], oh[c][:], ALU.mult))
                step(nv.tensor_reduce(slot_f[:, c, :], e_t[:], AX.X, ALU.add))
            step(nv.tensor_copy(slot_i[:], slot_f[:]))
            st.done(nv.tensor_scalar(blk_i[:], slot_i[:], 7, None, ALU.logical_shift_right))
            step(nv.tensor_scalar(in_i[:], slot_i[:], P - 1, None, ALU.bitwise_and))
            st.done(nv.tensor_copy(blk_f[:], blk_i[:]))
            step(nv.tensor_copy(in_f[:], in_i[:]))
            blk_v, in_v = blk_f[:].rearrange("p c t -> p (c t)"), in_f[:].rearrange("p c t -> p (c t)")
            val_v = vals[:].rearrange("p v c t -> p v (c t)")

            def pick(j, s):
                if not (isinstance(j, int) and j < 2):
                    dve.wait_ge(S["pick_used"], j - 1)
                one = bass.ds(j, 1)
                nv.tensor_scalar(pick_r[s][:], iota_r[:], in_v[:, one], None, ALU.is_equal)
                for v in range(3):
                    last = nv.tensor_scalar(pick_b[s][:, v, :], iota_r[:, 0:TAB], blk_v[:, one], val_v[:, v, one], ALU.is_equal, ALU.mult)
                last.then_inc(S["pick_ready"], 1)

            pick(0, 0)
            pick(1, 1)
            with dve.Fori(1, NT) as i:
                pick(2 * i, 0)
                pick(2 * i + 1, 1)
            dve.wait_ge(S["tab_made"], 1)
            step(nv.tensor_copy(table[:], ps[7][:, 0:3 * TAB].rearrange("p (v b) -> p v b", v=3)))
            st.done(nv.tensor_copy(table_i[:, 0, :], table[:, 0, :]))
            step(nv.tensor_scalar(table[:, 1, :], table[:, 1, :], NO_ROW, None, ALU.add))
            nv.tensor_copy(table_i[:, 1, :], table[:, 1, :]).then_inc(S["tab_ready"], 1)

            def low_gu(e, c):
                dve.wait_ge(S["gu_split_h"], 4 * e + c + 1)
                nv.tensor_tensor(gu_slot(gu_l, e, c), gu_slot(gu_raw, e, c), gu_slot(gu_h, e, c).bitcast(F32), ALU.subtract).then_inc(S["gu_split_l"], 1)

            def low_dn(e, c):
                dve.wait_ge(S["dn_split_h"], 2 * e + c + 1)
                nv.tensor_tensor(dn_slot(dn_l, e, c), dn_slot(dn_raw, e, c), dn_slot(dn_h, e, c).bitcast(F32), ALU.subtract).then_inc(S["dn_split_l"], 1)

            def gate(i):
                dve.wait_ge(S["silu_made"], i + 1)
                if not (isinstance(i, int) and i == 0):
                    dve.wait_ge(S["aT_e_made"], i)
                nv.tensor_tensor(act_a[:], ps[1][:], act_s[:], ALU.mult).then_inc(S["act_ready"], 1)

            def low_aT(i):
                dve.wait_ge(S["aT_h_made"], i + 1)
                nv.tensor_tensor(aT_l[:], ps[4][:].rearrange("p (k m) -> p k m", k=KE), aT_h[:].bitcast(F32), ALU.subtract).then_inc(S["aT_l_made"], 1)

            def low_xT(i):
                dve.wait_ge(S["xT_h_made"], i + 1)
                for b in range(2):
                    last = nv.tensor_tensor(xT_l[:, 4 * b:4 * b + 4, :], ps[2 + b][:].rearrange("p (k m) -> p k m", k=4),
                                            xT_h[:, 4 * b:4 * b + 4, :].bitcast(F32), ALU.subtract)
                last.then_inc(S["xT_l_made"], 1)

            n_blocks = dve.value_load(block_n[0:1, 0:1], min_val=NE, max_val=MAXBLK)

            def expert_of(i):
                return dve.value_load(block_e[0:1, bass.ds(i, 1)], min_val=0, max_val=NE - 1)

            for c in range(4):
                low_gu(0, c)
            for c in range(2):
                low_dn(0, c)
            low_xT(0)

            def expert_block(i, first=False):
                e, e_next = expert_of(i), expert_of(i + 1)
                with dve.If(e < e_next):
                    for c in range(3):
                        low_gu(e_next, c)
                gate(i)
                low_xT(i + 1)
                with dve.If(e < e_next):
                    low_gu(e_next, 3)
                if not first:
                    with dve.If(expert_of(i - 1) < e):
                        for c in range(2):
                            low_dn(e, c)
                low_aT(i)

            expert_block(0, first=True)
            with dve.Fori(1, n_blocks) as i:
                expert_block(i)

            dve.wait_ge(S["last_loaded"], 64)

            def f_sum(i, s, q):
                t = 2 * i + s
                dve.wait_ge(S["y_summed"], t + 1)
                if not (isinstance(i, int) and i == 0):
                    dve.wait_ge(S["f_ready"], t - 1)
                for b in range(2):
                    c = slice(512 * b, 512 * (b + 1))
                    st.done(nv.tensor_tensor(r2[s][:, c], ps[2 * s + b][:], g2b[q][:, c], ALU.mult))
                st.sync()
                dve.wait_ge(S[f"x1_loaded_{s}"], 16 * (i + 1))
                nv.scalar_tensor_tensor(r2[s][:], x1t[s][:], ALPHA, r2[s][:], ALU.mult, ALU.add).then_inc(S["f_taken"], 1)
                dve.wait_ge(S["f_taken"], t + 1)
                for b in range(2):
                    st.done(nv.bn_stats(stat2[:, b, :], r2[s][:, 512 * b:512 * (b + 1)]))
                st.sync_apart()
                st.done(nv.bn_aggr(mv2[s][:], stat2[:].rearrange("p a b -> p (a b)")))
                st.sync()
                nv.tensor_scalar(mv2[s][:, 1:2], mv2[s][:, 1:2], EPS, None, ALU.add).then_inc(S["f_var"], 1)

            def f_gain(t, s):
                dve.wait_ge(S["f_scaled"], t + 1)
                nv.tensor_tensor(r2[s][:], r2[s][:], ln2_g[:], ALU.mult).then_inc(S["f_gained"], 1)

            def f_offset(t, s):
                dve.wait_ge(S["f_rstd"], t + 1)
                nv.scalar_tensor_tensor(nmr2[s][:], mv2[s][:, 0:1], -1.0, rstd2[s][:], ALU.mult, ALU.mult).then_inc(S["f_shift"], 1)

            f_sum(0, 0, 0)
            f_offset(0, 0)
            f_sum(0, 1, 0)
            f_gain(0, 0)
            f_offset(1, 1)
            for q, (lo, hi) in enumerate(((1, SEQ_TILES[0][1] // 2), (SEQ_TILES[1][0] // 2, NT // 2))):
                with dve.Fori(lo, hi) as i:
                    st.enter(i - lo, 10)
                    for s in range(2):
                        f_sum(i, s, q)
                        f_gain(2 * i + s - 1, 1 - s)
                        f_offset(2 * i + s, s)
                st.leave(hi - lo)
            f_gain(NT - 1, 1)

        @block.tensor
        def _(pe):
            mm = nc.tensor.matmul

            def three(out, lh, ll, rh, rl, start, stop):
                mm(out, lh, rh, start=start, stop=False)
                mm(out, lh, rl, start=False, stop=False)
                return mm(out, ll, rh, start=False, stop=stop)

            pe.wait_ge(S["ident_made"], 1)
            pe.wait_ge(S["c_silu"], 1)
            nc.tensor.transpose(ps[0][:, 0:2 * KD], c_act[:], ident[0:2 * KD, 0:2 * KD]).then_inc(S["cT_made"], 1)
            pe.wait_ge(S["wsp_loaded"], 16)
            for h in range(HEADS):
                last = nc.tensor.transpose(ps[1][:, h * P:(h + 1) * P], w_spT[:, h, :], ident[:])
            last.then_inc(S["wspT_made"], 1)
            pe.wait_ge(S["cT_copied"], 1)
            c_cols = cT[:].rearrange("p (s k) -> p k s", s=2)
            n = 0
            for j in range(N_ADA):
                if j >= 2:
                    pe.wait_ge(S["mod_row"], j - 1)
                out = ps[2 + j % 2][0:2, :]
                for kk in range(KD // CH):
                    pe.wait_ge(ada_loaded[n % 3], 16 * (n // 3 + 1))
                    for k in range(kk * CH, (kk + 1) * CH):
                        last = mm(out, c_cols[:, k, :], ada[n % 3][:, k % CH, :], start=k == 0, stop=k == KD - 1)
                    last.then_inc(ada_used, 1)
                    n += 1

            def transposes(t):
                pe.wait_ge(S["h_ready"], t + 1)
                if not (isinstance(t, int) and t == 0):
                    pe.wait_ge(S["hT_l_made"], t)
                for k in range(KD):
                    last = nc.tensor.transpose(ps[k // 4][:, (k % 4) * P:(k % 4 + 1) * P], xs[:, k * P:(k + 1) * P], ident[:])
                last.then_inc(S["xT_made"], 1)

            def z_part(out, s, part):
                c = slice(part * AW, (part + 1) * AW)
                for k in range(KD):
                    last = three(out, hT_h[s][:, k, :], hT_l[s][:, k, :], win_h[:, k, c], win_l[:, k, c], k == 0, k == KD - 1)
                return last

            def w_pool_mm(t):
                pe.wait_ge(S["pooled_copied"], t + 1)
                if not (isinstance(t, int) and t == 0):
                    pe.wait_ge(S["aT_copied"], t + 1)
                for g in range(4):
                    last = mm(ps[6][:, g * P:(g + 1) * P], w_pool[:, g, :], pooledT[:, g, :], start=True, stop=True)
                last.then_inc(S["b_made"], 1)

            def a_transposes(t):
                pe.wait_ge(S["a_ready"], t + 1)
                if not (isinstance(t, int) and t == 0):
                    pe.wait_ge(S["b_copied"], t)
                for h in range(HEADS):
                    last = nc.tensor.transpose(ps[6][:, h * P:(h + 1) * P], a_sb[:, h * P:(h + 1) * P], ident[:])
                last.then_inc(S["aT_made"], 1)

            def pool_mm(t, s, kind, prev, nxt, prev_src=p_old):
                if nxt:
                    pe.wait_ge(S["p_copied"], t + 2)
                else:
                    pe.wait_ge(S["p_copied"], t + 1)
                if prev and prev_src is p_old:
                    pe.wait_ge(S["p_kept"], t)
                if not (isinstance(t, int) and t == 0):
                    pe.wait_ge(S["pooled_copied"], t)
                for g in range(4):
                    c = slice(g * P, (g + 1) * P)
                    last = mm(ps[7][:, c], p_sb[s][:, c], bands[:, kind, g, :], start=True, stop=not (prev or nxt))
                    if prev:
                        last = mm(ps[7][:, c], prev_src[:, c], band_prev[:, g, :], start=False, stop=not nxt)
                    if nxt:
                        last = mm(ps[7][:, c], p_sb[1 - s][:, c], band_next[:, g, :], start=False, stop=True)
                last.then_inc(S["pooled"], 1)

            def z_tile(t, s, nxt, b2, prev, edge=(1, True, True)):
                pe.wait_ge(S["hT_l_made"], t + 1)
                if not (isinstance(t, int) and t == 0):
                    pe.wait_ge(S["v_gelu"], t)
                z_part(ps[2][:], s, 1).then_inc(S["v_made"], 1)
                if nxt:
                    transposes(t + 1)
                if b2:
                    w_pool_mm(t - 2)
                if not (isinstance(t, int) and t == 0):
                    pe.wait_ge(S["u_gelu"], t)
                z_part(ps[3][:], s, 0).then_inc(S["u_made"], 1)
                if prev:
                    a_transposes(t - 1)
                if not (isinstance(t, int) and t == 0):
                    pe.wait_ge(S["p_copied"], t)
                z_part(ps[4][:], s, 2).then_inc(S["p_made"], 1)
                pe.wait_ge(S["v_normed"], t + 1)
                if not (isinstance(t, int) and t == 0):
                    pe.wait_ge(S["a_ready"], t)
                for h in range(HEADS):
                    last = mm(ps[5][:, h * P:(h + 1) * P], w_spT[:, h, :], v_sb[:, h * P:(h + 1) * P], start=True, stop=True)
                last.then_inc(S["s_made"], 1)
                if prev:
                    pool_mm(t - 1, 1 - s, *edge)

            pe.wait_ge(S["wspT_copied"], 1)
            pe.wait_ge(S["bands_ready"], 1)
            transposes(0)
            pe.wait_ge(S["win_l_made"], KD)
            pe.wait_ge(S["small_loaded"], 16 * 9)
            first_t, last_t = (0, False, True), (2, True, False)
            z_tile(0, 0, True, False, False)
            z_tile(1, 1, True, False, True, first_t)
            z_tile(2, 0, True, True, True)
            z_tile(3, 1, True, True, True)
            z_tile(4, 0, True, True, True, last_t)
            z_tile(5, 1, True, True, True, first_t)
            with pe.Fori(3, NT // 2 - 1) as i:
                for s in range(2):
                    z_tile(2 * i + s, s, True, True, True)
            z_tile(NT - 2, 0, True, True, True)
            z_tile(NT - 1, 1, False, True, True)
            w_pool_mm(NT - 2)
            a_transposes(NT - 1)
            pool_mm(NT - 1, 1, *last_t, prev_src=p_sb[0])
            w_pool_mm(NT - 1)

            def h2_transposes(t):
                pe.wait_ge(S["h2_ready"], t + 1)
                if not (isinstance(t, int) and t == 0):
                    pe.wait_ge(S["h2T_copied"], t)
                for k in range(KD):
                    last = nc.tensor.transpose(ps[4 + k // 4][:, (k % 4) * P:(k % 4 + 1) * P], h2[:, k * P:(k + 1) * P], ident[:])
                last.then_inc(S["h2T_made"], 1)

            def mix(t, s, first=False, back=False):
                pe.wait_ge(S["z2_l_made"], t + 1)
                if not (isinstance(t, int) and t < 2):
                    pe.wait_ge(S["res_ready"], t - 1)
                if first:
                    for k in range(KD):
                        pe.wait_ge(S["wout_l_made"], k + 1)
                        for b in range(2):
                            c = slice(512 * b, 512 * (b + 1))
                            last = three(ps[2 * s + b][:], z2_h[s][:, k, :], z2_l[s][:, k, :], wout_h[:, k, c], wout_l[:, k, c], k == 0, k == KD - 1)
                else:
                    for b in range(2):
                        if back and b == 1:
                            h2_transposes(t - 2)
                        c = slice(512 * b, 512 * (b + 1))
                        for k in range(KD):
                            last = three(ps[2 * s + b][:], z2_h[s][:, k, :], z2_l[s][:, k, :], wout_h[:, k, c], wout_l[:, k, c], k == 0, k == KD - 1)
                last.then_inc(S["mix_made"], 1)

            def route(t):
                pe.wait_ge(S["h2T_copied"], t + 1)
                if not (isinstance(t, int) and t == 0):
                    pe.wait_ge(S["logit_read"], t)
                for k in range(KD):
                    last = mm(ps[6][:, 0:NG + NE], h2T[:, k, :], router_w[:, k, :], start=k == 0, stop=k == KD - 1)
                last.then_inc(S["logit_made"], 1)

            pe.wait_ge(S["b_copied"], NT)
            mix(0, 0, first=True)
            mix(1, 1)
            for t in (2, 3):
                mix(t, t - 2, back=True)
                route(t - 2)
            with pe.Fori(2, NT // 2) as i:
                for s in range(2):
                    mix(2 * i + s, s, back=True)
                    route(2 * i + s - 2)
            for t in (NT - 2, NT - 1):
                h2_transposes(t)
                route(t)

            pe.wait_ge(S["sel_ready"], 1)
            sel = both[:].rearrange("p t e -> p (t e)")
            mm(ps[0][:, 0:NT * NE], tri[:], sel, start=True, stop=True)
            mm(ps[1][:, 0:NT * NE], ones[:], sel, start=True, stop=True).then_inc(S["ranks_made"], 1)

            def pick(j, s, start=False, stop=False):
                pe.wait_ge(S["pick_ready"], j + 1)
                return mm(ps[7][:, 0:3 * TAB], pick_r[s][:], pick_b[s][:].rearrange("p v b -> p (v b)"), start=start, stop=stop)

            pick(0, 0, start=True).then_inc(S["pick_used"], 1)
            pick(1, 1).then_inc(S["pick_used"], 1)
            with pe.Fori(1, NT - 1) as i:
                pick(2 * i, 0).then_inc(S["pick_used"], 1)
                pick(2 * i + 1, 1).then_inc(S["pick_used"], 1)
            pick(2 * NT - 2, 0)
            pick(2 * NT - 1, 1, stop=True).then_inc(S["tab_made"], 1)

            def x_transposes(i):
                pe.wait_ge(S["gathered"], 16 * (i + 1))
                if not (isinstance(i, int) and i == 0):
                    pe.wait_ge(S["xT_l_made"], i)
                for k in range(KD):
                    last = nc.tensor.transpose(ps[2 + k // 4][:, (k % 4) * P:(k % 4 + 1) * P], xg[:, k * P:(k + 1) * P], ident[:])
                last.then_inc(S["xgT_made"], 1)

            def gate_up(i, e):
                pe.wait_ge(S["xT_l_made"], i + 1)
                if not (isinstance(i, int) and i == 0):
                    pe.wait_ge(S["act_ready"], i)
                for c in range(4):
                    pe.wait_ge(S["gu_split_l"], 4 * e + c + 1)
                    w_h, w_l = gu_slot(gu_h, e, c), gu_slot(gu_l, e, c)
                    for b in range(2):
                        n = slice(512 * b, 512 * (b + 1))
                        for k in range(2):
                            kk = 2 * c + k
                            last = three(ps[b][:], xT_h[:, kk, :], xT_l[:, kk, :], w_h[:, k, n], w_l[:, k, n], kk == 0, kk == KD - 1)
                    last.then_inc(S["gu_used"], 1)

            def a_transposes_e(i):
                pe.wait_ge(S["act_ready"], i + 1)
                if not (isinstance(i, int) and i == 0):
                    pe.wait_ge(S["aT_l_made"], i)
                for k in range(KE):
                    last = nc.tensor.transpose(ps[4][:, k * P:(k + 1) * P], act_a[:, k * P:(k + 1) * P], ident[:])
                last.then_inc(S["aT_e_made"], 1)

            def down(i, e):
                pe.wait_ge(S["aT_l_made"], i + 1)
                pe.wait_ge(S["y_ready"], i + 1)
                for c in range(2):
                    pe.wait_ge(S["dn_split_l"], 2 * e + c + 1)
                    w_h, w_l = dn_slot(dn_h, e, c), dn_slot(dn_l, e, c)
                    for b in range(2):
                        n = slice(512 * b, 512 * (b + 1))
                        for k in range(2):
                            kk = 2 * c + k
                            last = three(ps[5 + b][:], aT_h[:, kk, :], aT_l[:, kk, :], w_h[:, k, n], w_l[:, k, n], kk == 0, kk == KE - 1)
                    last.then_inc(S["dn_used"], 1)

            pe.wait_ge(S["tab_ready"], 1)
            pe.wait_ge(S["eid_ready"], 1)
            n_blocks = pe.value_load(block_n[0:1, 0:1], min_val=NE, max_val=MAXBLK)
            last_block = pe.value_load(block_n[0:1, 1:2], min_val=NE - 1, max_val=MAXBLK - 1)

            def expert_of(i):
                return pe.value_load(block_e[0:1, bass.ds(i, 1)], min_val=0, max_val=NE - 1)

            x_transposes(0)
            gate_up(0, 0)
            x_transposes(1)
            a_transposes_e(0)
            with pe.Fori(1, n_blocks) as i:
                e_before, e = expert_of(i - 1), expert_of(i)
                gate_up(i, e)
                x_transposes(i + 1)
                down(i - 1, e_before)
                a_transposes_e(i)
            down(last_block, NE - 1)

            yl = [S["y_loaded_0"], S["y_loaded_1"]]

            def y_sum(i, s):
                t = 2 * i + s
                pe.wait_ge(yl[s], 32 * (i + 1))
                if not (isinstance(i, int) and i == 0):
                    pe.wait_ge(S["f_taken"], t - 1)
                for b in range(2):
                    n = slice(512 * b, 512 * (b + 1))
                    mm(ps[2 * s + b][:], ident[:], y0[s][:, n], start=True, stop=False)
                    last = mm(ps[2 * s + b][:], ident[:], y1[s][:, n], start=False, stop=True)
                last.then_inc(S["y_summed"], 1)

            y_sum(0, 0)
            y_sum(0, 1)
            with pe.Fori(1, NT // 2) as i:
                for s in range(2):
                    y_sum(i, s)


INPUTS = ["x_prompt", "x_sample", "c_prompt", "c_sample", "w_ada", "b_ada", "w_in", "v_norm_g", "v_norm_b",
          "w_spatial", "b_spatial", "w_pool", "pool_scale", "w_out", "ln1_g", "ln1_b", "w_route_group",
          "b_route_group", "w_route_expert", "b_route_expert", "w_gate_up", "w_down", "ln2_g", "ln2_b"]
OUTPUTS = [(1, 512, D), (1, 1024, D)]


def kernel(**inputs):
    import numpy as np
    from concourse import bacc
    from concourse.bass_utils import run_bass_kernel_spmd

    nc = bacc.Bacc("TRN2", target_bir_lowering=False, num_devices=1)
    arrays, ins = {}, {}
    for name in INPUTS:
        a = np.ascontiguousarray(inputs[name])
        arrays[f"in_{name}"] = a
        ins[name] = nc.dram_tensor(f"in_{name}", a.shape, mybir.dt.from_np(a.dtype), kind="ExternalInput").ap()
    outs = [nc.dram_tensor(f"out_{i}", shape, F32, kind="ExternalOutput").ap() for i, shape in enumerate(OUTPUTS)]
    encoder(nc, ins, outs)
    r = run_bass_kernel_spmd(nc, [arrays], core_ids=[0])
    return tuple(r.results[0][f"out_{i}"] for i in range(len(outs)))
```

```python
from contextlib import ExitStack

import concourse.bass as bass
from concourse import mybir

F32 = mybir.dt.float32
F32R = mybir.dt.float32r
I32 = mybir.dt.int32
ACT = mybir.ActivationFunctionType
ALU = mybir.AluOpType
AX = mybir.AxisListType

P = 128
D = 1024
KD = D // P
SEQS = (512, 1024)
T = sum(SEQS)
NT = T // P
SEQ_TILES = ((0, SEQS[0] // P), (SEQS[0] // P, NT))
AW = D // 2
HEADS = 4
WINDOWS = (2, 4, 8, 16)
NG = 4
EPG = 8
NE = NG * EPG
DE = D // 2
KE = DE // P
NMOD = 6
EPS = 1e-5
ALPHA = 2.0 ** 0.25
PAIRS = 2 * T
MAXBLK = (PAIRS + NE * P) // P
TAB = MAXBLK + 2
NO_ROW = 4096.0
FAR = 1e30
F_SLOTS = 4
GU_SLOTS = 7
DN_SLOTS = 4
ADA_N = 256
N_ADA = NMOD * D // ADA_N
N_ADA1 = N_ADA // 2
ADA_TILES = (N_ADA - N_ADA1) // 2
CB = NMOD * KD
ADA_SLOTS = 5
WIN_SLOTS = 4


class Steps:

    def __init__(self, eng, sem, carrier):
        self.eng, self.sem, self.carrier, self.base, self.n = eng, sem, carrier, 0, 0

    def done(self, ins):
        ins.then_inc(self.sem, 1)
        self.n += 1

    def sync(self):
        self.eng.wait_ge(self.sem, self.base + self.n)

    def sync_apart(self):
        self.sync()
        self.eng.sem_inc(self.carrier, 1)

    def enter(self, i, per):
        self.start = self.base + self.n
        self.per = per
        self.base, self.n = self.start + i * per, 0

    def leave(self, count):
        assert self.n == self.per, (self.n, self.per)
        self.base, self.n = self.start + count * self.per, 0


def encoder(nc, ins, outs):
    ctx = ExitStack()
    with ctx:
        names = []

        def sem(name):
            names.append(name)
            return ctx.enter_context(nc.semaphore(name))

        base = (nc.sbuf_base + 63) // 64 * 64
        top = nc.sbuf_usable_end

        class Region:
            def __init__(self, start):
                self.at = start

            def take(self, name, shape, dt=F32):
                n = 4
                for s in shape[1:]:
                    n *= s
                t = nc.alloc_sbuf_tensor_at(name, list(shape), dt, offset=self.at)
                self.at += (n + 31) // 32 * 32
                assert self.at <= top, (name, self.at - top)
                return t

        KB = 1024
        W0 = base
        Z0 = W0 + 96 * KB
        C0 = Z0 + 48 * KB

        r = Region(W0)
        win_h = r.take("win_h", [P, KD, 3 * AW], F32R)
        win_l = r.take("win_l", [P, KD, 3 * AW], F32R)
        r = Region(W0)
        wout_h = r.take("wout_h", [P, KD, D], F32R)
        wout_l = r.take("wout_l", [P, KD, D], F32R)
        wout_raw = [r.take(f"wout_raw{s}", [P, D]) for s in range(4)]
        r = Region(W0)
        gu_raw = r.take("gu_raw", [P, GU_SLOTS, 2, D])
        gu_h = r.take("gu_h", [P, GU_SLOTS, 2, D], F32R)
        dn_raw = r.take("dn_raw", [P, DN_SLOTS, 2, D])
        assert r.at <= C0
        gu_l = Region(W0).take("gu_l", [P, GU_SLOTS, 2, D], F32R)
        dn_l = Region(W0 + 2 * GU_SLOTS * 2 * D * 4).take("dn_l", [P, DN_SLOTS, 2, D], F32R)

        r = Region(Z0)
        ada_raw, ada_h, ada_l = [], [], []
        for s in range(ADA_SLOTS):
            r = Region(Z0 + 16 * KB * s if s < 3 else W0 + 64 * KB + 16 * KB * (s - 3))
            ada_l.append(Region(r.at).take(f"ada_l{s}", [P, KD, ADA_N], F32R))
            ada_raw.append(r.take(f"ada_raw{s}", [P, KD, ADA_N]))
            ada_h.append(r.take(f"ada_h{s}", [P, KD, ADA_N], F32R))
        r = Region(Z0)
        z2T = r.take("z2T", [P, NT, KD, P])
        r = Region(Z0)
        x1 = r.take("x1", [P, NT, D])

        r = Region(C0)
        router_w = r.take("router_w", [P, KD, NG + NE])
        router_b = r.take("router_b", [P, NG + NE])
        C1 = r.at
        TOP0 = top // 32 * 32 - 3744
        r = Region(TOP0)
        logits = r.take("logits", [P, NT, NG + NE])
        table = r.take("table", [P, 3, TAB])
        table_i = r.take("table_i", [P, 2, TAB], I32)
        block_e = r.take("block_e", [1, TAB], I32)
        block_n = r.take("block_n", [1, 2], I32)
        KEPT0 = r.at
        ident = r.take("ident", [P, P])
        half_neg = r.take("half_neg", [P, 1])
        r = Region(C1)
        bands = r.take("bands", [P, 3, len(WINDOWS), P])
        band_prev = r.take("band_prev", [P, len(WINDOWS), P])
        band_next = r.take("band_next", [P, len(WINDOWS), P])
        w_spT = r.take("w_spT", [P, HEADS, P])
        b_sp = r.take("b_sp", [P, HEADS])
        w_pool = r.take("w_pool", [P, len(WINDOWS), P])
        pool_s = r.take("pool_s", [P, len(WINDOWS)])
        vg = r.take("vg", [P, AW])
        vb = r.take("vb", [P, AW])
        B0 = r.at
        c_in = r.take("c_in", [2 * KD, P])
        c_act = r.take("c_act", [2 * KD, P])
        c_hl = r.take("c_hl", [P, KD, 4], F32R)
        pair_sum = r.take("pair_sum", [4, 2])
        mod_hl = [r.take(f"mod_hl{s}", [4, ADA_N]) for s in range(2)]
        bias_rows = r.take("bias_rows", [CB, P])
        bias = r.take("bias", [P, CB])
        mod = r.take("mod", [P, 2, CB])
        gain1 = r.take("gain1", [P, 2, KD])
        mod_rows = r.take("mod_rows", [2 * CB, P])
        xs = r.take("xs", [P, D])
        hT = r.take("hT", [P, KD, P])
        hT_h = [r.take("hT_h0", [P, KD, P], F32R)]
        hT_l = [r.take("hT_l0", [P, KD, P], F32R)]
        B1 = r.at
        hT_h.append(r.take("hT_h1", [P, KD, P], F32R))
        hT_l.append(r.take("hT_l1", [P, KD, P], F32R))
        u_sb = r.take("u_sb", [P, AW])
        v_sb = r.take("v_sb", [P, AW])
        a_sb = r.take("a_sb", [P, AW])
        p_sb = [r.take(f"p_sb{s}", [P, AW]) for s in range(2)]
        p_old = r.take("p_old", [P, AW])
        pooledT = r.take("pooledT", [P, len(WINDOWS), P])
        v_stat = r.take("v_stat", [P, 6])
        v_mv = r.take("v_mv", [P, 2])
        v_rstd = r.take("v_rstd", [P, 1])
        assert r.at <= KEPT0
        r = Region(B1)
        win_raw = [r.take(f"win_raw{s}", [P, 3 * AW]) for s in range(WIN_SLOTS - 1)]
        win_raw.append(Region(Z0).take("win_raw3", [P, 3 * AW]))
        assert r.at <= KEPT0
        r = Region(C1)
        z2_h = [r.take(f"z2_h{s}", [P, KD, P], F32R) for s in range(2)]
        z2_l = [r.take(f"z2_l{s}", [P, KD, P], F32R) for s in range(2)]
        xr = r.take("xr", [P, D])
        res = r.take("res", [P, D])
        h2 = r.take("h2", [P, D])
        h2T = r.take("h2T", [P, KD, P])
        g1b = r.take("g1b", [P, D])
        sc2b = r.take("sc2b", [P, D])
        sh2b = r.take("sh2b", [P, D])
        ln_g = r.take("ln_g", [P, D])
        ln_b = r.take("ln_b", [P, D])
        stat = r.take("stat", [P, 2, 6])
        mv = r.take("mv", [P, 2])
        rstd = r.take("rstd", [P, 1])
        nmr = r.take("nmr", [P, 1])
        r = Region(C1)
        tri = r.take("tri", [P, P])
        ones = r.take("ones", [P, P])
        iota_p = r.take("iota_p", [P, 1])
        iota_r = r.take("iota_r", [P, P])
        rev = r.take("rev", [P, NE])
        tok = r.take("tok", [P, 2, NT])
        gmax = r.take("gmax", [P, NT])
        gw = r.take("gw", [P, NT])
        g_a = r.take("g_a", [P, NT, NG])
        g_b = r.take("g_b", [P, NT, NG])
        gm = r.take("gm", [P, NT])
        e2 = r.take("e2", [P, NT, NE])
        e_t = r.take("e_t", [P, NT, NE])
        oh = [r.take(f"oh{k}", [P, NT, NE]) for k in range(2)]
        both = r.take("both", [P, NT, NE])
        v1 = r.take("v1", [P, NT])
        v2 = r.take("v2", [P, NT])
        em = r.take("em", [P, NT])
        ex = r.take("ex", [P, NT])
        den = r.take("den", [P, NT])
        vals = r.take("vals", [P, 3, 2, NT])
        before = r.take("before", [P, NT + 1, NE])
        pos = r.take("pos", [P, NT, NE])
        cmp = r.take("cmp", [P, NE, NT])
        nblk = r.take("nblk", [P, NE])
        cum = [r.take(f"cum{k}", [P, NE]) for k in range(2)]
        cmp_e = r.take("cmp_e", [1, TAB, NE])
        eid_f = r.take("eid_f", [1, TAB])
        slot_f = r.take("slot_f", [P, 2, NT])
        slot_i = r.take("slot_i", [P, 2, NT], I32)
        blk_i = r.take("blk_i", [P, 2, NT], I32)
        in_i = r.take("in_i", [P, 2, NT], I32)
        blk_f = r.take("blk_f", [P, 2, NT])
        in_f = r.take("in_f", [P, 2, NT])
        pick_in = r.take("pick_in", [P, 2, NT, P])
        pick_blk = r.take("pick_blk", [P, 2, NT, TAB])
        pick_v = r.take("pick_v", [P, 2, NT, 3, TAB])
        r = Region(C0)
        dn_h = r.take("dn_h", [P, DN_SLOTS, 2, D], F32R)
        xg = r.take("xg", [P, D])
        xT_h = r.take("xT_h", [P, KD, P], F32R)
        xT_l = r.take("xT_l", [P, KD, P], F32R)
        act_s = r.take("act_s", [P, DE])
        act_a = r.take("act_a", [P, DE])
        aT_h = r.take("aT_h", [P, KE, P], F32R)
        aT_l = r.take("aT_l", [P, KE, P], F32R)
        y_sb = r.take("y_sb", [P, D])
        g_idx = r.take("g_idx", [P, 1], I32)
        s_idx = r.take("s_idx", [P, 1], I32)
        s_w = r.take("s_w", [P, 1])
        assert r.at <= TOP0
        r = Region(W0)
        y0 = [r.take(f"y0_{s}", [P, D]) for s in range(F_SLOTS)]
        y1 = [r.take(f"y1_{s}", [P, D]) for s in range(F_SLOTS)]
        x1t = [r.take(f"x1t{s}", [P, D]) for s in range(F_SLOTS)]
        r2 = [r.take(f"r2_{s}", [P, D]) for s in range(2)]
        fin = [r.take(f"fin{s}", [P, D]) for s in range(2)]
        g2b = [r.take(f"g2b{q}", [P, D]) for q in range(2)]
        ln2_g = r.take("ln2_gb", [P, D])
        ln2_b = r.take("ln2_bb", [P, D])
        stat2 = r.take("stat2", [P, 2, 6])
        mv2 = [r.take(f"mv2_{s}", [P, 2]) for s in range(2)]
        rstd2 = [r.take(f"rstd2_{s}", [P, 1]) for s in range(2)]
        nmr2 = [r.take(f"nmr2_{s}", [P, 1]) for s in range(2)]
        assert r.at <= W0 + 2 * GU_SLOTS * 2 * D * 4

        ps = [ctx.enter_context(nc.psum_tensor(f"bank{b}", [P, 512], F32)) for b in range(8)]

        mod_d = nc.dram_tensor("mod_rows", (2, NMOD * D), F32).ap()
        h2_d = nc.dram_tensor("h2_rows", (T, D), F32).ap()
        x1_d = nc.dram_tensor("x1_rows", (T, D), F32).ap()
        y_d = nc.dram_tensor("y_rows", (PAIRS, D), F32).ap()

        x_in = (ins["x_prompt"][0], ins["x_sample"][0])
        y_out = (outs[0][0], outs[1][0])

        def x_rows(q, t):
            return x_in[q][bass.ds((t - SEQ_TILES[q][0]) * P, P), :]

        def bcast(row, n):
            return row.to_broadcast([P, n])

        w_ada = ins["w_ada"][0].rearrange("(k p) n -> p k n", p=P)
        w_in = ins["w_in"][0].rearrange("(k p) n -> p k n", p=P)
        w_out = ins["w_out"][0].rearrange("(k p) n -> p k n", p=P)
        w_gu = ins["w_gate_up"][0].rearrange("e (k p) n -> e p k n", p=P)
        w_dn = ins["w_down"][0].rearrange("e (k p) n -> e p k n", p=P)

        S = {n: sem(n) for n in (
            "c_loaded small_loaded ada_bias c_silu cT_made biasT_made cT_high cT_low bias_copied pair_sum_made ada_split_h ada_split_l mod_hl_made mod_cols mod_made modT_made ident_made ident_zero"
            " consts_made mod_row mod_stored wsp_loaded wspT_made wspT_copied band_edge"
            " band_made bands_ready win_h_made win_l_made"
            " mod1_loaded x_loaded h_ready xT_made hT_h_made hT_l_made v_made v_gelu v_stats v_rs"
            " v_normed u_made u_gelu p_made p_kept p_copied s_made a_ready aT_made aT_copied pooled"
            " pooled_copied b_made b_copied"
            " mod2_loaded xr_loaded wout_h_made wout_l_made z2_h_made z2_l_made mix_made res_normed"
            " res_ready var_ready rstd_ready shift_ready x1_ready x1_stored h2_ready h2_stored h2T_made h2T_copied"
            " logit_made logit_read mod2_used"
            " rt_consts g_shifted g_exp top_diff top_exp sel_ready ranks_made pick_ready"
            " tab_made tab_ready eid_ready"
            " idx_ready gathered xgT_made xT_h_made xT_l_made gu_split_h gu_split_l dn_split_h"
            " dn_split_l gu_used dn_used silu_made act_ready aT_e_made aT_h_made aT_l_made y_ready"
            " y_idx y_scattered"
            " last_loaded y_summed f_taken f_var f_rstd f_shift f_gained f_ready"
            " f_stored_0 f_stored_1"
            " f_scaled dve_steps pool_steps dve_carrier pool_carrier sp_carrier"
        ).split()}
        ada_loaded = [sem(f"ada_loaded{s}") for s in range(ADA_SLOTS)]
        ada_used = sem("ada_used")
        win_loaded = [sem(f"win_loaded{k}") for k in range(KD)]
        wout_loaded = [sem(f"wout_loaded{k}") for k in range(KD)]
        gu_loaded = [sem(f"gu_loaded{c}") for c in range(4)]
        y_loaded = [sem(f"y_loaded{s}") for s in range(F_SLOTS)]
        x1_loaded = [sem(f"x1_loaded{s}") for s in range(F_SLOTS)]
        dn_loaded = [sem(f"dn_loaded{c}") for c in range(2)]

        def gu_slot(buf, e, c):
            n = (4 * e + c) % GU_SLOTS
            return buf[:, n, :, :] if isinstance(n, int) else buf[:, bass.ds(n, 1), :, :].rearrange("p a k n -> p (a k) n")

        def dn_slot(buf, e, c):
            n = (2 * e + c) % DN_SLOTS
            return buf[:, n, :, :] if isinstance(n, int) else buf[:, bass.ds(n, 1), :, :].rearrange("p a k n -> p (a k) n")

        def ada_slot(n):
            if n < N_ADA1:
                return n % ADA_SLOTS, n // ADA_SLOTS + 1
            return 2, len(range(2, N_ADA1, ADA_SLOTS)) + n - N_ADA1 + 1

        block = ctx.enter_context(nc.Block())

        @block.sync
        def _(sp):
            sp.dma_start(c_in[0:KD, :], ins["c_prompt"].rearrange("a (k p) -> (a k) p", p=P)).then_inc(S["c_loaded"], 16)
            sp.dma_start(c_in[KD:2 * KD, :], ins["c_sample"].rearrange("a (k p) -> (a k) p", p=P)).then_inc(S["c_loaded"], 16)
            sp.dma_start(bias_rows[:], ins["b_ada"].rearrange("a (c p) -> (a c) p", p=P)).then_inc(S["ada_bias"], 16)

            def load_ada(n):
                slot = ada_slot(n)[0]
                if n >= N_ADA1:
                    sp.wait_ge(ada_used, n)
                elif n >= ADA_SLOTS:
                    sp.wait_ge(ada_used, n - ADA_SLOTS + 1)
                sp.dma_start(ada_raw[slot][:], w_ada[:, :, n * ADA_N:(n + 1) * ADA_N]).then_inc(ada_loaded[slot], 16)

            def load_x(t, q):
                if not (isinstance(t, int) and t == 0):
                    sp.wait_ge(S["xT_made"], t)
                sp.dma_start(xs[:], x_rows(q, t)).then_inc(S["x_loaded"], 16)

            load_ada(0)
            sp.dma_start(w_spT[:], ins["w_spatial"][0].rearrange("h q p -> q h p")).then_inc(S["wsp_loaded"], 16)
            for n in range(1, N_ADA1):
                load_ada(n)
            load_x(0, 0)
            for k in range(KD):
                if k >= WIN_SLOTS:
                    sp.wait_ge(S["win_l_made"], k - WIN_SLOTS + 1)
                if k == WIN_SLOTS - 1:
                    sp.wait_ge(ada_used, N_ADA1)
                sp.dma_start(win_raw[k % WIN_SLOTS][:], w_in[:, k, :]).then_inc(win_loaded[k], 16)
            for dst, src in ((vg[:], bcast(ins["v_norm_g"], AW)), (vb[:], bcast(ins["v_norm_b"], AW)),
                             (w_pool[:], ins["w_pool"][0].rearrange("g c d -> c g d")),
                             (router_w[:, :, 0:NG], ins["w_route_group"][0].rearrange("(k p) n -> p k n", p=P)),
                             (router_w[:, :, NG:NG + NE], ins["w_route_expert"][0].rearrange("(k p) n -> p k n", p=P)),
                             (router_b[:, 0:NG], bcast(ins["b_route_group"], NG)),
                             (router_b[:, NG:NG + NE], bcast(ins["b_route_expert"].rearrange("a g e -> a (g e)"), NE))):
                sp.dma_start(dst, src).then_inc(S["small_loaded"], 16)
            with nc.allow_non_contiguous_dma(reason="1024 words in all"):
                sp.dma_start(b_sp[:], ins["b_spatial"][0].rearrange("h q -> q h")).then_inc(S["small_loaded"], 16)
                sp.dma_start(pool_s[:], ins["pool_scale"][0].rearrange("(g c) -> c g", c=P)).then_inc(S["small_loaded"], 16)

            load_ada(N_ADA1)
            load_x(1, 0)
            for t in range(ADA_TILES):
                load_x(t + 2, 0 if t + 2 < SEQ_TILES[0][1] else 1)
                load_ada(N_ADA1 + 2 * t + 1)
                if t < ADA_TILES - 1:
                    load_ada(N_ADA1 + 2 * t + 2)
            sp.wait_ge(S["mod_row"], 1)
            sp.dma_start(mod_d.rearrange("s (c j) -> (s c) j", j=P), mod_rows[:]).then_inc(S["mod_stored"], 16)
            with sp.Fori(ADA_TILES + 2, NT) as t:
                load_x(t, 1)
            sp.wait_ge(S["mod_stored"], 16)
            for k in range(KD):
                if k >= 4:
                    sp.wait_ge(S["wout_l_made"], k - 3)
                elif k == 0:
                    sp.wait_ge(S["p_made"], NT)
                sp.dma_start(wout_raw[k % 4][:], w_out[:, k, :]).then_inc(wout_loaded[k], 16)
            sp.wait_ge(S["b_copied"], NT)
            sp.wait_ge(S["aT_copied"], NT)

            def load_mod2(q):
                for dst, m in ((g1b, 2), (sc2b, 4), (sh2b, 3)):
                    sp.dma_start(dst[:], bcast(mod_d[q:q + 1, m * D:(m + 1) * D], D)).then_inc(S["mod2_loaded"], 16)

            sp.dma_start(ln_g[:], bcast(ins["ln1_g"], D)).then_inc(S["mod2_loaded"], 16)
            sp.dma_start(ln_b[:], bcast(ins["ln1_b"], D)).then_inc(S["mod2_loaded"], 16)
            load_mod2(0)

            def second(t, q, first=False):
                if not first:
                    sp.wait_ge(S["res_ready"], t)
                sp.dma_start(xr[:], x_rows(q, t)).then_inc(S["xr_loaded"], 16)

            def store_h2(t):
                sp.wait_ge(S["h2_ready"], t + 1)
                sp.dma_start(h2_d[bass.ds(t * P, P), :], h2[:]).then_inc(S["h2_stored"], 16)
                xt = x1[:, t, :] if isinstance(t, int) else x1[:, bass.ds(t, 1), :].rearrange("p a n -> p (a n)")
                sp.dma_start(x1_d[bass.ds(t * P, P), :], xt).then_inc(S["x1_stored"], 16)

            second(0, 0, first=True)
            with sp.Fori(1, 4) as t:
                second(t, 0)
                store_h2(t - 1)
            store_h2(3)
            load_mod2(1)
            second(4, 1)
            with sp.Fori(5, NT) as t:
                second(t, 1)
                store_h2(t - 1)
            store_h2(NT - 1)

            def load_gu(e, c):
                if not (isinstance(e, int) and e == 0):
                    sp.wait_ge(gu_loaded[c], 16 * e)
                if not isinstance(e, int):
                    sp.sem_inc(S["sp_carrier"], 1)
                src = w_gu[e, :, 2 * c:2 * c + 2, :] if isinstance(e, int) else w_gu[bass.ds(e, 1), :, 2 * c:2 * c + 2, :].rearrange("a p k n -> p (a k) n")
                sp.dma_start(gu_slot(gu_raw, e, c), src).then_inc(gu_loaded[c], 16)

            def load_dn(e, c):
                if not (isinstance(e, int) and e == 0):
                    sp.wait_ge(dn_loaded[c], 16 * e)
                if not isinstance(e, int):
                    sp.sem_inc(S["sp_carrier"], 1)
                src = w_dn[e, :, 2 * c:2 * c + 2, :] if isinstance(e, int) else w_dn[bass.ds(e, 1), :, 2 * c:2 * c + 2, :].rearrange("a p k n -> p (a k) n")
                sp.dma_start(dn_slot(dn_raw, e, c), src).then_inc(dn_loaded[c], 16)

            sp.wait_ge(S["mix_made"], NT)
            sp.wait_ge(S["x1_stored"], 16 * NT)
            for n in range(GU_SLOTS):
                load_gu(n // 4, n % 4)
            for n in range(DN_SLOTS):
                load_dn(n // 2, n % 2)

            sp.wait_ge(S["eid_ready"], 1)
            n_blocks = sp.value_load(block_n[0:1, 0:1], min_val=NE, max_val=MAXBLK)

            def expert_of(i):
                return sp.value_load(block_e[0:1, bass.ds(i, 1)], min_val=0, max_val=NE - 1)

            def refill(i, first=False):
                e, e_next = expert_of(i), expert_of(i + 1)
                with sp.If(e < e_next):
                    sp.wait_ge(S["gu_used"], 4 * i + 1)
                    sp.sem_inc(S["sp_carrier"], 1)
                    load_gu(e_next, 3)
                    with sp.If(e_next < NE - 1):
                        for c in range(3):
                            sp.wait_ge(S["gu_used"], 4 * i + c + 2)
                            sp.sem_inc(S["sp_carrier"], 1)
                            load_gu((e_next + 1).with_bounds(min_val=0, max_val=NE - 1), c)
                if not first:
                    with sp.If(expert_of(i - 1) < e):
                        with sp.If(e < NE - 1):
                            for c in range(2):
                                sp.wait_ge(S["dn_used"], 2 * i + c - 1)
                                sp.sem_inc(S["sp_carrier"], 1)
                                load_dn((e + 1).with_bounds(min_val=0, max_val=NE - 1), c)

            refill(0, first=True)
            with sp.Fori(1, n_blocks) as i:
                refill(i)

            sp.wait_ge(S["gu_used"], 4 * n_blocks)
            for dst, src in ((g2b[0], mod_d[0:1, 5 * D:6 * D]), (g2b[1], mod_d[1:2, 5 * D:6 * D]),
                             (ln2_g, ins["ln2_g"]), (ln2_b, ins["ln2_b"])):
                sp.dma_start(dst[:], bcast(src, D)).then_inc(S["last_loaded"], 16)

            def load_x1(t, s):
                sp.dma_start(x1t[s][:], x1_d[bass.ds(t * P, P), :]).then_inc(x1_loaded[s], 16)

            def load_y(t, s):
                sp.dma_start(y0[s][:], y_d[bass.ds(t * P, P), :]).then_inc(y_loaded[s], 16)
                sp.dma_start(y1[s][:], y_d[bass.ds(T + t * P, P), :]).then_inc(y_loaded[s], 16)

            for s in range(F_SLOTS):
                load_x1(s, s)
            sp.wait_ge(S["y_scattered"], n_blocks * 16)
            for s in range(F_SLOTS):
                load_y(s, s)
            with sp.Fori(1, NT // F_SLOTS) as i:
                for s in range(F_SLOTS):
                    t = F_SLOTS * i + s
                    sp.wait_ge(S["y_summed"], t - F_SLOTS + 1)
                    load_y(t, s)
                    sp.wait_ge(S["f_taken"], t - F_SLOTS + 1)
                    load_x1(t, s)

        @block.gpsimd
        def _(pool):
            st = Steps(pool, S["pool_steps"], S["pool_carrier"])
            st.done(pool.memset(ident[:], 0.0))
            st.sync()
            nc.gpsimd.affine_select(out=ident[:], in_=ident[:], compare_op=ALU.not_equal, fill=1.0, base=0,
                                    pattern=[[-1, P]], channel_multiplier=1).then_inc(S["ident_made"], 1)
            st.done(pool.memset(half_neg[:], -0.5))
            nc.gpsimd.iota(band_prev[:, 0, :], pattern=[[1, P]], base=0, channel_multiplier=0,
                           allow_small_or_imprecise_dtypes=True).then_inc(S["consts_made"], 1)
            pool.wait_ge(S["band_edge"], 1)
            for g, w in enumerate(WINDOWS):
                h = w // 2
                for b, shift in [(bands[:, v, g, :], 0) for v in range(3)] + [(band_prev[:, g, :], -P), (band_next[:, g, :], P)]:
                    st.done(nc.gpsimd.affine_select(out=b, in_=b, compare_op=ALU.is_ge, fill=0.0, base=shift + h,
                                                    pattern=[[-1, P]], channel_multiplier=1))
                    st.sync()
                    nc.gpsimd.affine_select(out=b, in_=b, compare_op=ALU.is_gt, fill=0.0, base=h - shift,
                                            pattern=[[1, P]], channel_multiplier=-1).then_inc(S["band_made"], 1)

            with pool.Fori(0, NT) as t:
                pool.wait_ge(S["v_stats"], t + 1)
                nc.gpsimd.tensor_tensor(v_rstd[:], v_mv[:, 1:2], half_neg[:], ALU.pow).then_inc(S["v_rs"], 1)

            def second(t):
                pool.wait_ge(S["var_ready"], t + 1)
                nc.gpsimd.tensor_tensor(rstd[:], mv[:, 1:2], half_neg[:], ALU.pow).then_inc(S["rstd_ready"], 1)
                pool.wait_ge(S["x1_ready"], t + 1)
                if not (isinstance(t, int) and t == 0):
                    pool.wait_ge(S["h2_stored"], 16 * t)
                    pool.wait_ge(S["h2T_made"], t)
                st.done(nc.gpsimd.tensor_tensor(h2[:], x1[:, t, :] if isinstance(t, int) else x1[:, bass.ds(t, 1), :].rearrange("p a n -> p (a n)"), sc2b[:], ALU.mult))
                st.sync()
                nc.gpsimd.tensor_tensor(h2[:], h2[:], sh2b[:], ALU.add).then_inc(S["h2_ready"], 1)

            def plus_one(n):
                pool.wait_ge(S["mod2_loaded"], 16 * n)
                st.done(nc.gpsimd.tensor_scalar(sc2b[:], sc2b[:], 1.0, None, ALU.add))
                st.sync()

            plus_one(5)
            second(0)
            with pool.Fori(1, 4) as t:
                st.enter(t - 1, 1)
                second(t)
            st.leave(3)
            plus_one(8)
            with pool.Fori(4, NT) as t:
                st.enter(t - 4, 1)
                second(t)
            st.leave(NT - 4)

            pool.wait_ge(S["logit_read"], NT)
            pool.wait_ge(S["h2_stored"], 16 * NT)
            st.done(pool.memset(ones[:], 1.0))
            st.done(pool.memset(tri[:], 1.0))
            st.sync()
            nc.gpsimd.affine_select(out=tri[:], in_=tri[:], compare_op=ALU.is_gt, fill=0.0, base=0,
                                    pattern=[[1, P]], channel_multiplier=-1).then_inc(S["rt_consts"], 1)
            nc.gpsimd.iota(iota_r[:], pattern=[[1, P]], base=0, channel_multiplier=0,
                           allow_small_or_imprecise_dtypes=True).then_inc(S["rt_consts"], 1)
            nc.gpsimd.iota(rev[:], pattern=[[-1, NE]], base=NE, channel_multiplier=0,
                           allow_small_or_imprecise_dtypes=True).then_inc(S["rt_consts"], 1)
            nc.gpsimd.iota(tok[:], pattern=[[T, 2], [P, NT]], base=0, channel_multiplier=1,
                           allow_small_or_imprecise_dtypes=True).then_inc(S["rt_consts"], 1)
            nc.gpsimd.iota(cmp[:], pattern=[[0, NE], [P, NT]], base=0, channel_multiplier=0,
                           allow_small_or_imprecise_dtypes=True).then_inc(S["rt_consts"], 1)

            nc.gpsimd.iota(cmp_e[:], pattern=[[1, TAB], [0, NE]], base=0, channel_multiplier=0,
                           allow_small_or_imprecise_dtypes=True).then_inc(S["rt_consts"], 1)
            for c in range(4):
                pool.wait_ge(S["gu_split_h"], c + 1)
                nc.gpsimd.tensor_tensor(gu_slot(gu_l, 0, c), gu_slot(gu_raw, 0, c), gu_slot(gu_h, 0, c).bitcast(F32), ALU.subtract).then_inc(S["gu_split_l"], 1)

            pool.wait_ge(S["tab_ready"], 1)
            pool.wait_ge(S["eid_ready"], 1)
            n_blocks = pool.value_load(block_n[0:1, 0:1], min_val=NE, max_val=MAXBLK)
            last_block = pool.value_load(block_n[0:1, 1:2], min_val=NE - 1, max_val=MAXBLK - 1)

            def gather(i, first=False):
                if not first:
                    pool.wait_ge(S["gathered"], 16 * i)
                    pool.wait_ge(S["xgT_made"], i)
                nc.gpsimd.tensor_copy(g_idx[:], table_i[:, 0, bass.ds(i, 1)]).then_inc(S["idx_ready"], 1)
                pool.wait_ge(S["idx_ready"], i + 1)
                pool.sem_inc(S["pool_carrier"], 1)
                nc.gpsimd.indirect_dma_start(out=xg[:], out_offset=None, in_=h2_d,
                                             in_offset=bass.IndirectOffsetOnAxis(ap=g_idx[:, 0:1], axis=0)).then_inc(S["gathered"], 16)

            def scatter(i):
                if not (isinstance(i, int) and i == 0):
                    pool.wait_ge(S["y_scattered"], 16 * i)
                nc.gpsimd.tensor_copy(s_idx[:], table_i[:, 1, bass.ds(i, 1)]).then_inc(S["y_idx"], 1)
                nc.gpsimd.tensor_copy(s_w[:], table[:, 2, bass.ds(i, 1)]).then_inc(S["y_idx"], 1)
                pool.wait_ge(S["y_idx"], 2 * i + 2)
                pool.wait_ge(S["y_ready"], i + 2)
                pool.sem_inc(S["pool_carrier"], 1)
                nc.gpsimd.indirect_dma_start(out=y_d, out_offset=bass.IndirectOffsetOnAxis(ap=s_idx[:, 0:1], axis=0),
                                             in_=y_sb[:], in_offset=None, bounds_check=PAIRS - 1,
                                             oob_is_err=False).then_inc(S["y_scattered"], 16)

            gather(0, first=True)
            gather(1)
            gather(2)
            scatter(0)
            with pool.Fori(2, n_blocks) as i:
                gather(i + 1)
                scatter(i - 1)
            scatter(last_block)
            pool.wait_ge(S["gathered"], 16 * (n_blocks + 1))
            pool.sem_inc(S["pool_carrier"], 1)

            def f_power(t, s):
                pool.wait_ge(S["f_var"], t + 1)
                nc.gpsimd.tensor_tensor(rstd2[s][:], mv2[s][:, 1:2], half_neg[:], ALU.pow).then_inc(S["f_rstd"], 1)

            def f_add(i, s):
                pool.wait_ge(S["f_gained"], 2 * i + s + 1)
                nc.gpsimd.tensor_tensor(fin[s][:], fin[s][:], ln2_b[:], ALU.add).then_inc(S["f_ready"], 1)

            f_power(0, 0)
            f_power(1, 1)
            f_add(0, 0)
            f_power(2, 0)
            f_add(0, 1)
            f_power(3, 1)
            with pool.Fori(1, NT // 2 - 1) as i:
                for s in range(2):
                    f_add(i, s)
                    f_power(2 * i + s + 2, s)
            for s in range(2):
                pool.wait_ge(S["f_gained"], NT - 1 + s)
                nc.gpsimd.tensor_tensor(fin[s][:], fin[s][:], ln2_b[:], ALU.add).then_inc(S["f_ready"], 1)

        @block.scalar
        def _(act):
            act.wait_ge(S["c_loaded"], 32)
            nc.scalar.activation(c_act[:], c_in[:], ACT.Silu).then_inc(S["c_silu"], 1)
            act.wait_ge(S["cT_made"], 1)
            c_cols = ps[0][:, 0:2 * KD].rearrange("p (s k) -> p k s", s=2)
            nc.scalar.activation(c_hl[:, :, 0:2], c_cols, ACT.Copy).then_inc(S["cT_high"], 1)
            act.wait_ge(S["biasT_made"], 1)
            nc.scalar.activation(bias[:], ps[3][:, 0:CB], ACT.Copy).then_inc(S["bias_copied"], 1)
            act.wait_ge(S["wspT_made"], 1)
            nc.scalar.activation(w_spT[:], ps[1][:].rearrange("p (h q) -> p h q", h=HEADS), ACT.Copy).then_inc(S["wspT_copied"], 1)

            def high_ada(n):
                slot, count = ada_slot(n)
                act.wait_ge(ada_loaded[slot], 16 * count)
                nc.scalar.activation(ada_h[slot][:], ada_raw[slot][:], ACT.Copy).then_inc(S["ada_split_h"], 1)

            def mod_hl_out(n, bank):
                act.wait_ge(ada_used, n + 1)
                if n >= 2:
                    act.wait_ge(S["mod_cols"], n - 1)
                nc.scalar.activation(mod_hl[n % 2][:], ps[bank][0:4, 0:ADA_N], ACT.Copy).then_inc(S["mod_hl_made"], 1)

            for n in range(N_ADA1):
                high_ada(n)
                if n >= 1:
                    mod_hl_out(n - 1, 5 + (n - 1) % 2)
            mod_hl_out(N_ADA1 - 1, 5 + (N_ADA1 - 1) % 2)
            def high_x(t, s):
                act.wait_ge(S["h_ready"], t + 1)
                if not (isinstance(t, int) and t < 2):
                    act.wait_ge(S["p_made"], t - 1)
                nc.scalar.activation(hT_h[s][:], hT[:], ACT.Copy).then_inc(S["hT_h_made"], 1)

            for k in range(KD):
                if k == KD // 2:
                    high_x(0, 0)
                act.wait_ge(win_loaded[k], 16)
                nc.scalar.activation(win_h[:, k, :], win_raw[k % WIN_SLOTS][:], ACT.Copy).then_inc(S["win_h_made"], 1)

            def z_tile(t, s, nxt, prev, n=None):
                if n:
                    high_ada(n)
                act.wait_ge(S["v_made"], t + 1)
                if not (isinstance(t, int) and t == 0):
                    act.wait_ge(S["s_made"], t)
                nc.scalar.activation(v_sb[:], ps[2][:], ACT.Gelu_apprx_tanh).then_inc(S["v_gelu"], 1)
                if nxt:
                    high_x(t + 1, 1 - s)
                if n:
                    mod_hl_out(n, 7)
                act.wait_ge(S["u_made"], t + 1)
                if not (isinstance(t, int) and t == 0):
                    act.wait_ge(S["a_ready"], t)
                nc.scalar.activation(u_sb[:], ps[3][:], ACT.Gelu_apprx_tanh).then_inc(S["u_gelu"], 1)
                if n:
                    high_ada(n + 1)
                if prev:
                    copy_aT(t - 1)
                act.wait_ge(S["p_made"], t + 1)
                if not (isinstance(t, int) and t < 2):
                    act.wait_ge(S["p_kept"], t - 1)
                nc.scalar.activation(p_sb[s][:], ps[4][:], ACT.Copy).then_inc(S["p_copied"], 1)
                if n:
                    mod_hl_out(n + 1, 7)

            def copy_aT(t):
                act.wait_ge(S["aT_made"], t + 1)
                dst = z2T[:, t, 0:4, :] if isinstance(t, int) else z2T[:, bass.ds(t, 1), 0:4, :].rearrange("p a k m -> p (a k) m")
                nc.scalar.activation(dst, ps[6][:].rearrange("p (k m) -> p k m", k=4), ACT.Copy).then_inc(S["aT_copied"], 1)

            for t in range(ADA_TILES):
                z_tile(t, t % 2, True, t >= 1, N_ADA1 + 2 * t)
            with act.Fori(ADA_TILES // 2, NT // 2 - 1) as i:
                for s in range(2):
                    z_tile(2 * i + s, s, True, True)
            z_tile(NT - 2, 0, True, True)
            z_tile(NT - 1, 1, False, True)
            copy_aT(NT - 1)

            for k in range(KD):
                act.wait_ge(wout_loaded[k], 16)
                nc.scalar.activation(wout_h[:, k, :], wout_raw[k % 4][:], ACT.Copy).then_inc(S["wout_h_made"], 1)
            act.wait_ge(S["mod_stored"], 16)
            act.wait_ge(S["b_copied"], NT)

            def high_z(t, s):
                if not (isinstance(t, int) and t < 2):
                    act.wait_ge(S["mix_made"], t - 1)
                src = z2T[:, t, :, :] if isinstance(t, int) else z2T[:, bass.ds(t, 1), :, :].rearrange("p a k m -> p (a k) m")
                nc.scalar.activation(z2_h[s][:], src, ACT.Copy).then_inc(S["z2_h_made"], 1)

            def normalise(t):
                act.wait_ge(S["shift_ready"], t + 1)
                nc.scalar.activation(res[:], res[:], ACT.Identity, scale=rstd[:, 0:1], bias=nmr[:, 0:1]).then_inc(S["res_normed"], 1)

            def copy_h2T(t):
                act.wait_ge(S["h2T_made"], t + 1)
                if not (isinstance(t, int) and t == 0):
                    act.wait_ge(S["logit_made"], t)
                for b in range(2):
                    last = nc.scalar.activation(h2T[:, 4 * b:4 * b + 4, :], ps[4 + b][:].rearrange("p (k m) -> p k m", k=4), ACT.Copy)
                last.then_inc(S["h2T_copied"], 1)

            high_z(0, 0)
            high_z(1, 1)
            normalise(0)
            high_z(2, 0)
            normalise(1)
            high_z(3, 1)
            copy_h2T(0)
            with act.Fori(1, NT // 2 - 1) as i:
                for s in range(2):
                    normalise(2 * i + s)
                    high_z(2 * i + s + 2, s)
                    copy_h2T(2 * i + s - 1)
            for t in (NT - 2, NT - 1):
                normalise(t)
                copy_h2T(t - 1)
            copy_h2T(NT - 1)

            act.wait_ge(S["g_shifted"], 1)
            nc.scalar.activation(g_a[:], g_a[:], ACT.Exp).then_inc(S["g_exp"], 1)
            act.wait_ge(S["top_diff"], 1)
            nc.scalar.activation(ex[:], v2[:], ACT.Exp).then_inc(S["top_exp"], 1)

            def high_gu(e, c):
                act.wait_ge(gu_loaded[c], 16 * (e + 1))
                nc.scalar.activation(gu_slot(gu_h, e, c), gu_slot(gu_raw, e, c), ACT.Copy).then_inc(S["gu_split_h"], 1)

            def high_dn(e, c):
                act.wait_ge(dn_loaded[c], 16 * (e + 1))
                nc.scalar.activation(dn_slot(dn_h, e, c), dn_slot(dn_raw, e, c), ACT.Copy).then_inc(S["dn_split_h"], 1)

            def silu(i):
                act.wait_ge(S["gu_used"], 4 * i + 4)
                if not (isinstance(i, int) and i == 0):
                    act.wait_ge(S["act_ready"], i)
                nc.scalar.activation(act_s[:], ps[0][:], ACT.Silu).then_inc(S["silu_made"], 1)

            def high_aT(i):
                act.wait_ge(S["aT_e_made"], i + 1)
                nc.scalar.activation(aT_h[:], ps[4][:].rearrange("p (k m) -> p k m", k=KE), ACT.Copy).then_inc(S["aT_h_made"], 1)

            def high_xT(i):
                act.wait_ge(S["xgT_made"], i + 1)
                for b in range(2):
                    last = nc.scalar.activation(xT_h[:, 4 * b:4 * b + 4, :], ps[2 + b][:].rearrange("p (k m) -> p k m", k=4), ACT.Copy)
                last.then_inc(S["xT_h_made"], 1)

            act.sem_inc(S["y_ready"], 1)

            def weigh(i):
                act.wait_ge(S["dn_used"], 2 * i + 2)
                act.wait_ge(S["y_idx"], 2 * i + 2)
                if not (isinstance(i, int) and i == 0):
                    act.wait_ge(S["y_scattered"], 16 * i)
                for b in range(2):
                    last = nc.scalar.activation(y_sb[:, 512 * b:512 * (b + 1)], ps[5 + b][:], ACT.Copy, scale=s_w[:, 0:1])
                last.then_inc(S["y_ready"], 1)

            for c in range(4):
                high_gu(0, c)
            act.wait_ge(S["tab_ready"], 1)
            for c in range(2):
                high_dn(0, c)
            n_blocks = act.value_load(block_n[0:1, 0:1], min_val=NE, max_val=MAXBLK)
            last_block = act.value_load(block_n[0:1, 1:2], min_val=NE - 1, max_val=MAXBLK - 1)

            def expert_of(i):
                return act.value_load(block_e[0:1, bass.ds(i, 1)], min_val=0, max_val=NE - 1)

            high_xT(0)

            def expert_block(i, first=False):
                e, e_next = expert_of(i), expert_of(i + 1)
                with act.If(e < e_next):
                    for c in range(3):
                        high_gu(e_next, c)
                silu(i)
                high_xT(i + 1)
                with act.If(e < e_next):
                    high_gu(e_next, 3)
                if not first:
                    weigh(i - 1)
                    with act.If(expert_of(i - 1) < e):
                        for c in range(2):
                            high_dn(e, c)
                high_aT(i)

            expert_block(0, first=True)
            expert_block(1)
            with act.Fori(2, n_blocks) as i:
                expert_block(i)
            weigh(last_block)

            def f_norm(t, s):
                act.wait_ge(S["f_shift"], t + 1)
                nc.scalar.activation(r2[s][:], r2[s][:], ACT.Identity, scale=rstd2[s][:, 0:1], bias=nmr2[s][:, 0:1]).then_inc(S["f_scaled"], 1)

            def store_y(t, s, q):
                act.wait_ge(S["f_ready"], t + 1)
                nc.scalar.dma_start(y_out[q][bass.ds((t - SEQ_TILES[q][0]) * P, P), :], fin[s][:]).then_inc(S[f"f_stored_{s}"], 16)

            f_norm(0, 0)
            f_norm(1, 1)
            for q, (lo, hi) in enumerate(SEQ_TILES):
                last = hi if hi < NT else NT - 2
                with act.Fori(lo // 2, last // 2) as i:
                    for s in range(2):
                        store_y(2 * i + s, s, q)
                        f_norm(2 * i + s + 2, s)
            for s in range(2):
                store_y(NT - 2 + s, s, 1)
            for s in range(2):
                act.wait_ge(S[f"f_stored_{s}"], 16 * NT // 2)

        @block.vector
        def _(dve):
            st = Steps(dve, S["dve_steps"], S["dve_carrier"])
            nv = nc.vector

            def step(ins):
                st.done(ins)
                st.sync()

            dve.wait_ge(S["consts_made"], 1)
            for g, w in enumerate(WINDOWS):
                h = w // 2
                st.done(nv.tensor_scalar(bands[:, 0, g, :], band_prev[:, 0, :], float(h), float(w), ALU.add, ALU.min))
                st.done(nv.tensor_scalar(bands[:, 2, g, :], band_prev[:, 0, :], -1.0, float(P + h), ALU.mult, ALU.add))
                st.done(nv.memset(bands[:, 1, g, :], 1.0 / w))
                st.done(nv.memset(band_next[:, g, :], 1.0 / w))
                st.sync()
                st.done(nv.tensor_scalar(bands[:, 2, g, :], bands[:, 2, g, :], float(w), None, ALU.min))
                st.done(nv.reciprocal(bands[:, 0, g, :], bands[:, 0, g, :]))
                st.sync()
                st.done(nv.reciprocal(bands[:, 2, g, :], bands[:, 2, g, :]))
            st.sync()
            for g, w in enumerate(WINDOWS):
                last = nv.memset(band_prev[:, g, :], 1.0 / w)
            last.then_inc(S["band_edge"], 1)
            dve.wait_ge(S["cT_high"], 1)
            nv.tensor_tensor(c_hl[:, :, 2:4], ps[0][:, 0:2 * KD].rearrange("p (s k) -> p k s", s=2),
                             c_hl[:, :, 0:2].bitcast(F32), ALU.subtract).then_inc(S["cT_low"], 1)
            dve.wait_ge(S["ident_made"], 1)
            nv.tensor_tensor(pair_sum[:], ident[0:4, 0:2], ident[0:4, 2:4], ALU.add).then_inc(S["pair_sum_made"], 1)

            def low_ada(n):
                slot = ada_slot(n)[0]
                dve.wait_ge(S["ada_split_h"], n + 1)
                nv.tensor_tensor(ada_l[slot][:], ada_raw[slot][:], ada_h[slot][:].bitcast(F32), ALU.subtract).then_inc(S["ada_split_l"], 1)

            def mod_out(bank, lo, hi):
                dve.wait_ge(S["mod_cols"], hi)
                cols = slice(2 * lo, 2 * hi)
                nv.tensor_tensor(mod[:, :, cols], ps[bank][:, 0:4 * (hi - lo)].rearrange("p (c s) -> p s c", s=2),
                                 bias[:, None, cols].to_broadcast([P, 2, 2 * (hi - lo)]), ALU.add).then_inc(S["mod_made"], 1)

            for n in range(N_ADA1):
                low_ada(n)
            dve.wait_ge(S["bias_copied"], 1)
            mod_out(4, 0, N_ADA1)
            dve.wait_ge(S["mod_made"], 1)
            step(nv.tensor_scalar(gain1[:], mod[:, :, KD:2 * KD], 1.0, None, ALU.add))
            def low_x(t, s):
                dve.wait_ge(S["hT_h_made"], t + 1)
                nv.tensor_tensor(hT_l[s][:], hT[:], hT_h[s][:].bitcast(F32), ALU.subtract).then_inc(S["hT_l_made"], 1)

            def modulate(t, q):
                dve.wait_ge(S["xT_made"], t + 1)
                for k in range(KD):
                    last = nv.tensor_scalar(hT[:, k, :], ps[k // 4][:, (k % 4) * P:(k % 4 + 1) * P],
                                            gain1[:, q, k:k + 1], mod[:, q, k:k + 1], ALU.mult, ALU.add)
                last.then_inc(S["h_ready"], 1)

            modulate(0, 0)
            for k in range(KD):
                if k == KD // 2 + 1:
                    low_x(0, 0)
                if k == 2:
                    dve.wait_ge(ada_used, N_ADA1)
                dve.wait_ge(S["win_h_made"], k + 1)
                nv.tensor_tensor(win_l[:, k, :], win_raw[k % WIN_SLOTS][:], win_h[:, k, :].bitcast(F32), ALU.subtract).then_inc(S["win_l_made"], 1)
            dve.wait_ge(S["band_made"], 5 * len(WINDOWS))
            last = nv.tensor_tensor(bands[:].rearrange("p v g m -> p (v g) m"), bands[:].rearrange("p v g m -> p (v g) m"),
                                    ident[:, None, :].to_broadcast([P, 12, P]), ALU.subtract)
            last.then_inc(S["bands_ready"], 1)
            dve.wait_ge(S["small_loaded"], 16 * 9)

            def b_out(t):
                dve.wait_ge(S["b_made"], t + 1)
                dst = z2T[:, t, 4:8, :] if isinstance(t, int) else z2T[:, bass.ds(t, 1), 4:8, :].rearrange("p a k m -> p (a k) m")
                nv.tensor_tensor(dst, ps[6][:].rearrange("p (k m) -> p k m", k=4),
                                 pool_s[:, :, None].to_broadcast([P, 4, P]), ALU.mult).then_inc(S["b_copied"], 1)

            def pooled_copy(t):
                dve.wait_ge(S["pooled"], t + 1)
                if not (isinstance(t, int) and t == 0):
                    dve.wait_ge(S["b_made"], t)
                nv.tensor_copy(pooledT[:], ps[7][:].rearrange("p (g m) -> p g m", g=4)).then_inc(S["pooled_copied"], 1)

            def z_tile(t, s, nxt, b2, pl, q=1, n=None):
                if n:
                    low_ada(n)
                if not (isinstance(t, int) and t < 2):
                    dve.wait_ge(S["pooled"], t - 1)
                    nv.tensor_copy(p_old[:], p_sb[s][:]).then_inc(S["p_kept"], 1)
                dve.wait_ge(S["v_gelu"], t + 1)
                st.done(nv.bn_stats(v_stat[:], v_sb[:]))
                st.sync_apart()
                st.done(nv.bn_aggr(v_mv[:], v_stat[:]))
                st.sync()
                nv.tensor_scalar(v_mv[:, 1:2], v_mv[:, 1:2], EPS, None, ALU.add).then_inc(S["v_stats"], 1)
                if nxt:
                    modulate(t + 1, q)
                dve.wait_ge(S["v_rs"], t + 1)
                st.done(nv.tensor_scalar(v_sb[:], v_sb[:], v_mv[:, 0:1], v_rstd[:, 0:1], ALU.subtract, ALU.mult))
                st.sync()
                st.done(nv.tensor_tensor(v_sb[:], v_sb[:], vg[:], ALU.mult))
                st.sync()
                nv.tensor_tensor(v_sb[:], v_sb[:], vb[:], ALU.add).then_inc(S["v_normed"], 1)
                if nxt:
                    low_x(t + 1, 1 - s)
                if b2:
                    b_out(t - 2)
                if n:
                    mod_out(7, max(n - 1, N_ADA1), n + 1)
                    low_ada(n + 1)
                dve.wait_ge(S["s_made"], t + 1)
                dve.wait_ge(S["u_gelu"], t + 1)
                if not (isinstance(t, int) and t == 0):
                    dve.wait_ge(S["aT_made"], t)
                for h in range(HEADS):
                    c = slice(h * P, (h + 1) * P)
                    last = nv.scalar_tensor_tensor(a_sb[:, c], ps[5][:, c], b_sp[:, h:h + 1], u_sb[:, c], ALU.add, ALU.mult)
                last.then_inc(S["a_ready"], 1)
                if n == N_ADA - 2:
                    mod_out(7, N_ADA - 1, N_ADA)
                    dve.wait_ge(S["modT_made"], 1)
                    nv.tensor_copy(mod_rows[:], ps[7][0:2 * CB, 0:P]).then_inc(S["mod_row"], 1)
                if pl:
                    pooled_copy(t - 1)

            for t in range(ADA_TILES):
                z_tile(t, t % 2, True, t >= 2, t >= 1, 0 if t + 1 < SEQ_TILES[0][1] else 1, N_ADA1 + 2 * t)
            with dve.Fori(ADA_TILES // 2, NT // 2 - 1) as i:
                st.enter(i - ADA_TILES // 2, 8)
                for s in range(2):
                    z_tile(2 * i + s, s, True, True, True)
            st.leave(NT // 2 - 1 - ADA_TILES // 2)
            z_tile(NT - 2, 0, True, True, True)
            z_tile(NT - 1, 1, False, True, True)
            b_out(NT - 2)
            pooled_copy(NT - 1)
            b_out(NT - 1)

            for k in range(KD):
                dve.wait_ge(S["wout_h_made"], k + 1)
                nv.tensor_tensor(wout_l[:, k, :], wout_raw[k % 4][:], wout_h[:, k, :].bitcast(F32), ALU.subtract).then_inc(S["wout_l_made"], 1)

            def low_z(t, s):
                dve.wait_ge(S["z2_h_made"], t + 1)
                src = z2T[:, t, :, :] if isinstance(t, int) else z2T[:, bass.ds(t, 1), :, :].rearrange("p a k m -> p (a k) m")
                nv.tensor_tensor(z2_l[s][:], src, z2_h[s][:].bitcast(F32), ALU.subtract).then_inc(S["z2_l_made"], 1)

            def second(t, s):
                dve.wait_ge(S["mix_made"], t + 1)
                if not (isinstance(t, int) and t == 0):
                    dve.wait_ge(S["x1_ready"], t)
                for b in range(2):
                    c = slice(512 * b, 512 * (b + 1))
                    st.done(nv.tensor_tensor(res[:, c], ps[2 * s + b][:], g1b[:, c], ALU.mult))
                st.sync()
                dve.wait_ge(S["xr_loaded"], 16 * (t + 1))
                nv.scalar_tensor_tensor(res[:], xr[:], ALPHA, res[:], ALU.mult, ALU.add).then_inc(S["res_ready"], 1)
                dve.wait_ge(S["res_ready"], t + 1)
                for b in range(2):
                    st.done(nv.bn_stats(stat[:, b, :], res[:, 512 * b:512 * (b + 1)]))
                st.sync_apart()
                st.done(nv.bn_aggr(mv[:], stat[:].rearrange("p a b -> p (a b)")))
                st.sync()
                nv.tensor_scalar(mv[:, 1:2], mv[:, 1:2], EPS, None, ALU.add).then_inc(S["var_ready"], 1)
                dve.wait_ge(S["rstd_ready"], t + 1)
                nv.scalar_tensor_tensor(nmr[:], mv[:, 0:1], -1.0, rstd[:], ALU.mult, ALU.mult).then_inc(S["shift_ready"], 1)

            def x1_out(t):
                dve.wait_ge(S["res_normed"], t + 1)
                st.done(nv.tensor_tensor(res[:], res[:], ln_g[:], ALU.mult))
                st.sync()
                dst = x1[:, t, :] if isinstance(t, int) else x1[:, bass.ds(t, 1), :].rearrange("p a n -> p (a n)")
                nv.tensor_tensor(dst, res[:], ln_b[:], ALU.add).then_inc(S["x1_ready"], 1)

            def logits_out(t):
                dve.wait_ge(S["logit_made"], t + 1)
                dst = logits[:, t, :] if isinstance(t, int) else logits[:, bass.ds(t, 1), :].rearrange("p a n -> p (a n)")
                nv.tensor_tensor(dst, ps[6][:, 0:NG + NE], router_b[:], ALU.add).then_inc(S["logit_read"], 1)

            low_z(0, 0)
            low_z(1, 1)
            dve.wait_ge(S["mod2_loaded"], 16 * 5)
            def norm_tile(t, s, nxt=True, prev=True):
                second(t, s)
                x1_out(t)
                if nxt:
                    low_z(t + 2, s)
                if prev:
                    logits_out(t - 2)

            norm_tile(0, 0, prev=False)
            norm_tile(1, 1, prev=False)
            norm_tile(2, 0)
            norm_tile(3, 1)
            dve.wait_ge(S["mod2_loaded"], 16 * 8)
            with dve.Fori(2, NT // 2 - 1) as i:
                st.enter(i - 2, 2 * 6)
                for s in range(2):
                    norm_tile(2 * i + s, s)
            st.leave(NT // 2 - 3)
            norm_tile(NT - 2, 0, nxt=False)
            norm_tile(NT - 1, 1, nxt=False)
            logits_out(NT - 2)
            logits_out(NT - 1)

            dve.wait_ge(S["rt_consts"], 4)
            G, E = logits[:, :, 0:NG], logits[:, :, NG:NG + NE]

            def first_max(dst, tmp, mx, src, n):
                step(nv.tensor_tensor(tmp, src, mx[:, :, None].to_broadcast([P, NT, n]), ALU.is_ge))
                step(nv.tensor_tensor(tmp, tmp, rev[:, None, 0:n].to_broadcast([P, NT, n]), ALU.mult))
                step(nv.tensor_reduce(em[:], tmp, AX.X, ALU.max))
                step(nv.tensor_tensor(dst, tmp, em[:, :, None].to_broadcast([P, NT, n]), ALU.is_equal))

            step(nv.tensor_reduce(gmax[:], G, AX.X, ALU.max))
            nv.tensor_tensor(g_a[:], G, gmax[:, :, None].to_broadcast([P, NT, NG]), ALU.subtract).then_inc(S["g_shifted"], 1)
            first_max(g_b[:], g_b[:], gmax, G, NG)
            step(nv.tensor_scalar(g_b[:], g_b[:], -1.0, FAR, ALU.add, ALU.mult))
            step(nv.tensor_tensor(e2[:].rearrange("p t (g e) -> p t g e", g=NG), E.rearrange("p t (g e) -> p t g e", g=NG),
                                  g_b[:, :, :, None].to_broadcast([P, NT, NG, EPG]), ALU.add))
            step(nv.tensor_reduce(v1[:], e2[:], AX.X, ALU.max))
            first_max(oh[0][:], e_t[:], v1, e2[:], NE)
            step(nv.scalar_tensor_tensor(e2[:], oh[0][:], -2 * FAR, e2[:], ALU.mult, ALU.add))
            step(nv.tensor_reduce(v2[:], e2[:], AX.X, ALU.max))
            first_max(oh[1][:], e_t[:], v2, e2[:], NE)
            nv.tensor_tensor(both[:], oh[0][:], oh[1][:], ALU.add).then_inc(S["sel_ready"], 1)
            nv.tensor_tensor(v2[:], v2[:], v1[:], ALU.subtract).then_inc(S["top_diff"], 1)
            dve.wait_ge(S["g_exp"], 1)
            step(nv.tensor_reduce(gw[:], g_a[:], AX.X, ALU.add))
            step(nv.reciprocal(gw[:], gw[:]))
            dve.wait_ge(S["top_exp"], 1)
            step(nv.tensor_scalar(den[:], ex[:], 1.0, None, ALU.add))
            step(nv.reciprocal(den[:], den[:]))
            step(nv.tensor_tensor(vals[:, 2, 0, :], den[:], gw[:], ALU.mult))
            step(nv.tensor_tensor(vals[:, 2, 1, :], vals[:, 2, 0, :], ex[:], ALU.mult))
            st.done(nv.tensor_copy(vals[:, 0, 0, :], tok[:, 0, :]))
            st.done(nv.tensor_copy(vals[:, 0, 1, :], tok[:, 0, :]))
            st.done(nv.tensor_scalar(vals[:, 1, :, :], tok[:], -NO_ROW, None, ALU.add))
            st.done(nv.memset(before[:, 0, :], 0.0))
            dve.wait_ge(S["ranks_made"], 1)
            for t in range(NT):
                st.sync()
                st.done(nv.tensor_tensor(before[:, t + 1, :], before[:, t, :], ps[1][:, NE * t:NE * (t + 1)], ALU.add))
            st.sync()
            step(nv.tensor_tensor(pos[:], before[:, 0:NT, :], ps[0][:, 0:NT * NE].rearrange("p (t e) -> p t e", t=NT), ALU.add))
            dve.wait_ge(S["rt_consts"], 6)
            step(nv.tensor_tensor(cmp[:], before[:, NT, :, None].to_broadcast([P, NE, NT]), cmp[:], ALU.is_gt))
            step(nv.tensor_reduce(nblk[:], cmp[:], AX.X, ALU.add))
            step(nv.tensor_scalar(nblk[:], nblk[:], 1.0, None, ALU.max))
            step(nv.tensor_copy(cum[0][:], nblk[:]))
            k, d = 0, 1
            while d < NE:
                st.done(nv.tensor_copy(cum[1 - k][:, 0:d], cum[k][:, 0:d]))
                st.done(nv.tensor_tensor(cum[1 - k][:, d:NE], cum[k][:, d:NE], cum[k][:, 0:NE - d], ALU.add))
                st.sync()
                k, d = 1 - k, 2 * d
            end = cum[k]
            st.done(nv.tensor_copy(block_n[:, 0:1], end[0:1, NE - 1:NE]))
            st.done(nv.tensor_scalar(block_n[:, 1:2], end[0:1, NE - 1:NE], -1.0, None, ALU.add))
            step(nv.tensor_tensor(cum[1 - k][:], end[:], nblk[:], ALU.subtract))
            step(nv.tensor_scalar(cum[1 - k][:], cum[1 - k][:], float(P), None, ALU.mult))
            step(nv.tensor_tensor(pos[:], pos[:], cum[1 - k][:, None, :].to_broadcast([P, NT, NE]), ALU.add))
            for c in range(2):
                step(nv.tensor_tensor(e_t[:], pos[:], oh[c][:], ALU.mult))
                step(nv.tensor_reduce(slot_f[:, c, :], e_t[:], AX.X, ALU.add))
            step(nv.tensor_copy(slot_i[:], slot_f[:]))
            st.done(nv.tensor_scalar(blk_i[:], slot_i[:], 7, None, ALU.logical_shift_right))
            step(nv.tensor_scalar(in_i[:], slot_i[:], P - 1, None, ALU.bitwise_and))
            st.done(nv.tensor_copy(blk_f[:], blk_i[:]))
            step(nv.tensor_copy(in_f[:], in_i[:]))
            for c in range(2):
                st.done(nv.tensor_tensor(pick_blk[:, c], iota_r[:, None, 0:TAB].to_broadcast([P, NT, TAB]),
                                         blk_f[:, c, :, None].to_broadcast([P, NT, TAB]), ALU.is_equal))
                step(nv.tensor_tensor(pick_in[:, c], iota_r[:, None, :].to_broadcast([P, NT, P]),
                                      in_f[:, c, :, None].to_broadcast([P, NT, P]), ALU.is_equal))
                for v in range(3):
                    last = nv.tensor_tensor(pick_v[:, c, :, v, :], pick_blk[:, c], vals[:, v, c, :, None].to_broadcast([P, NT, TAB]), ALU.mult)
                last.then_inc(S["pick_ready"], 1)
            step(nv.tensor_tensor(cmp_e[:], end[0:1, None, :].to_broadcast([1, TAB, NE]), cmp_e[:], ALU.is_le))
            step(nv.tensor_reduce(eid_f[:], cmp_e[:], AX.X, ALU.add))
            step(nv.tensor_scalar(eid_f[:], eid_f[:], float(NE - 1), None, ALU.min))
            nv.tensor_copy(block_e[:], eid_f[:]).then_inc(S["eid_ready"], 1)
            dve.wait_ge(S["tab_made"], 1)
            step(nv.tensor_copy(table[:], ps[7][:, 0:3 * TAB].rearrange("p (v b) -> p v b", v=3)))
            st.done(nv.tensor_copy(table_i[:, 0, :], table[:, 0, :]))
            step(nv.tensor_scalar(table[:, 1, :], table[:, 1, :], NO_ROW, None, ALU.add))
            nv.tensor_copy(table_i[:, 1, :], table[:, 1, :]).then_inc(S["tab_ready"], 1)

            def low_gu(e, c):
                dve.wait_ge(S["gu_split_h"], 4 * e + c + 1)
                nv.tensor_tensor(gu_slot(gu_l, e, c), gu_slot(gu_raw, e, c), gu_slot(gu_h, e, c).bitcast(F32), ALU.subtract).then_inc(S["gu_split_l"], 1)

            def low_dn(e, c):
                dve.wait_ge(S["dn_split_h"], 2 * e + c + 1)
                nv.tensor_tensor(dn_slot(dn_l, e, c), dn_slot(dn_raw, e, c), dn_slot(dn_h, e, c).bitcast(F32), ALU.subtract).then_inc(S["dn_split_l"], 1)

            def gate(i):
                dve.wait_ge(S["silu_made"], i + 1)
                if not (isinstance(i, int) and i == 0):
                    dve.wait_ge(S["aT_e_made"], i)
                nv.tensor_tensor(act_a[:], ps[1][:], act_s[:], ALU.mult).then_inc(S["act_ready"], 1)

            def low_aT(i):
                dve.wait_ge(S["aT_h_made"], i + 1)
                nv.tensor_tensor(aT_l[:], ps[4][:].rearrange("p (k m) -> p k m", k=KE), aT_h[:].bitcast(F32), ALU.subtract).then_inc(S["aT_l_made"], 1)

            def low_xT(i):
                dve.wait_ge(S["xT_h_made"], i + 1)
                for b in range(2):
                    last = nv.tensor_tensor(xT_l[:, 4 * b:4 * b + 4, :], ps[2 + b][:].rearrange("p (k m) -> p k m", k=4),
                                            xT_h[:, 4 * b:4 * b + 4, :].bitcast(F32), ALU.subtract)
                last.then_inc(S["xT_l_made"], 1)

            n_blocks = dve.value_load(block_n[0:1, 0:1], min_val=NE, max_val=MAXBLK)

            def expert_of(i):
                return dve.value_load(block_e[0:1, bass.ds(i, 1)], min_val=0, max_val=NE - 1)

            low_xT(0)
            for c in range(2):
                low_dn(0, c)
            dve.wait_ge(S["gu_split_l"], 4)

            def expert_block(i, first=False):
                e, e_next = expert_of(i), expert_of(i + 1)
                with dve.If(e < e_next):
                    for c in range(3):
                        low_gu(e_next, c)
                gate(i)
                low_xT(i + 1)
                with dve.If(e < e_next):
                    low_gu(e_next, 3)
                if not first:
                    with dve.If(expert_of(i - 1) < e):
                        for c in range(2):
                            low_dn(e, c)
                low_aT(i)

            expert_block(0, first=True)
            with dve.Fori(1, n_blocks) as i:
                expert_block(i)

            dve.wait_ge(S["last_loaded"], 64)

            def f_sum(i, slot, q):
                t, s = F_SLOTS * i + slot, slot % 2
                dve.wait_ge(S["y_summed"], t + 1)
                if not (isinstance(t, int) and t < 2):
                    dve.wait_ge(S["f_gained"], t - 1)
                for b in range(2):
                    c = slice(512 * b, 512 * (b + 1))
                    st.done(nv.tensor_tensor(r2[s][:, c], ps[2 * s + b][:], g2b[q][:, c], ALU.mult))
                st.sync()
                dve.wait_ge(x1_loaded[slot], 16 * (i + 1))
                nv.scalar_tensor_tensor(r2[s][:], x1t[slot][:], ALPHA, r2[s][:], ALU.mult, ALU.add).then_inc(S["f_taken"], 1)
                dve.wait_ge(S["f_taken"], t + 1)
                for b in range(2):
                    st.done(nv.bn_stats(stat2[:, b, :], r2[s][:, 512 * b:512 * (b + 1)]))
                st.sync_apart()
                st.done(nv.bn_aggr(mv2[s][:], stat2[:].rearrange("p a b -> p (a b)")))
                st.sync()
                nv.tensor_scalar(mv2[s][:, 1:2], mv2[s][:, 1:2], EPS, None, ALU.add).then_inc(S["f_var"], 1)

            def f_gain(t, s, pairs):
                dve.wait_ge(S["f_scaled"], t + 1)
                if not (isinstance(pairs, int) and pairs == 0):
                    dve.wait_ge(S[f"f_stored_{s}"], 16 * pairs)
                nv.tensor_tensor(fin[s][:], r2[s][:], ln2_g[:], ALU.mult).then_inc(S["f_gained"], 1)

            def f_offset(t, s):
                dve.wait_ge(S["f_rstd"], t + 1)
                nv.scalar_tensor_tensor(nmr2[s][:], mv2[s][:, 0:1], -1.0, rstd2[s][:], ALU.mult, ALU.mult).then_inc(S["f_shift"], 1)

            f_sum(0, 0, 0)
            f_offset(0, 0)
            for t in range(1, F_SLOTS):
                f_sum(0, t, 0)
                f_gain(t - 1, 1 - t % 2, (t - 1) // 2)
                f_offset(t, t % 2)
            assert F_SLOTS == SEQ_TILES[1][0]
            with dve.Fori(1, NT // F_SLOTS) as i:
                st.enter(i - 1, 5 * F_SLOTS)
                for s in range(F_SLOTS):
                    f_sum(i, s, 1)
                    f_gain(F_SLOTS * i + s - 1, 1 - s % 2, F_SLOTS // 2 * i + (s - 1) // 2)
                    f_offset(F_SLOTS * i + s, s % 2)
            st.leave(NT // F_SLOTS - 1)
            f_gain(NT - 1, 1, NT // 2 - 1)

        @block.tensor
        def _(pe):
            mm = nc.tensor.matmul

            def three(out, lh, ll, rh, rl, start, stop):
                mm(out, lh, rh, start=start, stop=False)
                mm(out, lh, rl, start=False, stop=False)
                return mm(out, ll, rh, start=False, stop=stop)

            pe.wait_ge(S["ident_made"], 1)
            pe.wait_ge(S["c_silu"], 1)
            nc.tensor.transpose(ps[0][:, 0:2 * KD], c_act[:], ident[0:2 * KD, 0:2 * KD]).then_inc(S["cT_made"], 1)
            pe.wait_ge(S["ada_bias"], 16)
            nc.tensor.transpose(ps[3][:, 0:CB], bias_rows[:], ident[0:CB, 0:CB]).then_inc(S["biasT_made"], 1)
            pe.wait_ge(S["wsp_loaded"], 16)
            for h in range(HEADS):
                last = nc.tensor.transpose(ps[1][:, h * P:(h + 1) * P], w_spT[:, h, :], ident[:])
            last.then_inc(S["wspT_made"], 1)
            pe.wait_ge(S["cT_low"], 1)
            pe.wait_ge(S["pair_sum_made"], 1)

            def ada_mm(bank, n):
                slot = ada_slot(n)[0]
                pe.wait_ge(S["ada_split_l"], n + 1)
                for k in range(KD):
                    mm(ps[bank][0:4, 0:ADA_N], c_hl[:, k, :], ada_h[slot][:, k, :], start=k == 0, stop=False)
                    last = mm(ps[bank][0:4, 0:ADA_N], c_hl[:, k, :], ada_l[slot][:, k, :], start=False, stop=k == KD - 1)
                last.then_inc(ada_used, 1)

            def mod_columns(out, n):
                pe.wait_ge(S["mod_hl_made"], n + 1)
                for c in range(ADA_N // P):
                    last = mm(out[:, 2 * c:2 * c + 2], mod_hl[n % 2][:, c * P:(c + 1) * P], pair_sum[:], start=True, stop=True)
                last.then_inc(S["mod_cols"], 1)

            for n in range(N_ADA1):
                if n >= 2:
                    pe.wait_ge(S["mod_hl_made"], n - 1)
                ada_mm(5 + n % 2, n)
                if n >= 1:
                    mod_columns(ps[4][:, 4 * n - 4:4 * n], n - 1)
            mod_columns(ps[4][:, 4 * N_ADA1 - 4:4 * N_ADA1], N_ADA1 - 1)

            def transposes(t):
                pe.wait_ge(S["x_loaded"], 16 * (t + 1))
                if not (isinstance(t, int) and t == 0):
                    pe.wait_ge(S["h_ready"], t)
                for k in range(KD):
                    last = nc.tensor.transpose(ps[k // 4][:, (k % 4) * P:(k % 4 + 1) * P], xs[:, k * P:(k + 1) * P], ident[:])
                last.then_inc(S["xT_made"], 1)

            def z_part(out, s, part, first=False):
                c = slice(part * AW, (part + 1) * AW)
                for k in range(KD):
                    if first:
                        pe.wait_ge(S["win_l_made"], k + 1)
                    last = three(out, hT_h[s][:, k, :], hT_l[s][:, k, :], win_h[:, k, c], win_l[:, k, c], k == 0, k == KD - 1)
                return last

            def w_pool_mm(t):
                pe.wait_ge(S["pooled_copied"], t + 1)
                if not (isinstance(t, int) and t == 0):
                    pe.wait_ge(S["aT_copied"], t + 1)
                for g in range(4):
                    last = mm(ps[6][:, g * P:(g + 1) * P], w_pool[:, g, :], pooledT[:, g, :], start=True, stop=True)
                last.then_inc(S["b_made"], 1)

            def a_transposes(t):
                pe.wait_ge(S["a_ready"], t + 1)
                if not (isinstance(t, int) and t == 0):
                    pe.wait_ge(S["b_copied"], t)
                for h in range(HEADS):
                    last = nc.tensor.transpose(ps[6][:, h * P:(h + 1) * P], a_sb[:, h * P:(h + 1) * P], ident[:])
                last.then_inc(S["aT_made"], 1)

            def pool_mm(t, s, kind, prev, nxt, prev_src=p_old):
                if nxt:
                    pe.wait_ge(S["p_copied"], t + 2)
                else:
                    pe.wait_ge(S["p_copied"], t + 1)
                if prev and prev_src is p_old:
                    pe.wait_ge(S["p_kept"], t)
                if not (isinstance(t, int) and t == 0):
                    pe.wait_ge(S["pooled_copied"], t)
                for g in range(4):
                    c = slice(g * P, (g + 1) * P)
                    last = mm(ps[7][:, c], p_sb[s][:, c], bands[:, kind, g, :], start=True, stop=not (prev or nxt))
                    if prev:
                        last = mm(ps[7][:, c], prev_src[:, c], band_prev[:, g, :], start=False, stop=not nxt)
                    if nxt:
                        last = mm(ps[7][:, c], p_sb[1 - s][:, c], band_next[:, g, :], start=False, stop=True)
                last.then_inc(S["pooled"], 1)

            def z_tile(t, s, nxt, b2, prev, edge=(1, True, True), n=None):
                pe.wait_ge(S["hT_l_made"], t + 1)
                if not (isinstance(t, int) and t == 0):
                    pe.wait_ge(S["v_gelu"], t)
                z_part(ps[2][:], s, 1, first=isinstance(t, int) and t == 0).then_inc(S["v_made"], 1)
                if nxt:
                    transposes(t + 1)
                if b2:
                    w_pool_mm(t - 2)
                if n:
                    if t == 1:
                        pe.wait_ge(S["mod_hl_made"], n)
                    ada_mm(7, n)
                if not (isinstance(t, int) and t == 0):
                    pe.wait_ge(S["u_gelu"], t)
                z_part(ps[3][:], s, 0).then_inc(S["u_made"], 1)
                if n:
                    pe.wait_ge(S["mod_hl_made"], n + 1)
                    chunks = range(max(n - 1, N_ADA1), n + 1)
                    for j, m in enumerate(chunks):
                        mod_columns(ps[7][:, 4 * j:4 * j + 4], m)
                if prev:
                    a_transposes(t - 1)
                if not (isinstance(t, int) and t == 0):
                    pe.wait_ge(S["p_copied"], t)
                z_part(ps[4][:], s, 2).then_inc(S["p_made"], 1)
                if n:
                    pe.wait_ge(S["mod_made"], t + 2)
                    ada_mm(7, n + 1)
                pe.wait_ge(S["v_normed"], t + 1)
                if not (isinstance(t, int) and t == 0):
                    pe.wait_ge(S["a_ready"], t)
                for h in range(HEADS):
                    last = mm(ps[5][:, h * P:(h + 1) * P], w_spT[:, h, :], v_sb[:, h * P:(h + 1) * P], start=True, stop=True)
                last.then_inc(S["s_made"], 1)
                if n:
                    pe.wait_ge(S["mod_hl_made"], n + 2)
                if n == N_ADA - 2:
                    mod_columns(ps[7][:, 0:4], n + 1)
                    pe.wait_ge(S["mod_made"], ADA_TILES + 2)
                    nc.tensor.transpose(ps[7][0:2 * CB, 0:P], mod[:].rearrange("p s c -> p (s c)"), ident[:]).then_inc(S["modT_made"], 1)
                    pe.wait_ge(S["mod_row"], 1)
                if isinstance(t, int) and t == 1:
                    pe.wait_ge(S["bands_ready"], 1)
                if prev:
                    pool_mm(t - 1, 1 - s, *edge)

            pe.wait_ge(S["wspT_copied"], 1)
            pe.wait_ge(S["bias_copied"], 1)
            pe.wait_ge(S["mod_made"], 1)
            transposes(0)
            pe.wait_ge(S["small_loaded"], 16 * 9)
            first_t, last_t = (0, False, True), (2, True, False)
            inner = (1, True, True)
            for t in range(ADA_TILES):
                edge = {1: first_t, SEQ_TILES[1][0]: last_t, SEQ_TILES[1][0] + 1: first_t}.get(t, inner)
                z_tile(t, t % 2, True, t >= 2, t >= 1, edge, n=N_ADA1 + 2 * t)
            with pe.Fori(3, NT // 2 - 1) as i:
                for s in range(2):
                    z_tile(2 * i + s, s, True, True, True)
            z_tile(NT - 2, 0, True, True, True)
            z_tile(NT - 1, 1, False, True, True)
            w_pool_mm(NT - 2)
            a_transposes(NT - 1)
            pool_mm(NT - 1, 1, *last_t, prev_src=p_sb[0])
            w_pool_mm(NT - 1)

            def h2_transposes(t):
                pe.wait_ge(S["h2_ready"], t + 1)
                if not (isinstance(t, int) and t == 0):
                    pe.wait_ge(S["h2T_copied"], t)
                for k in range(KD):
                    last = nc.tensor.transpose(ps[4 + k // 4][:, (k % 4) * P:(k % 4 + 1) * P], h2[:, k * P:(k + 1) * P], ident[:])
                last.then_inc(S["h2T_made"], 1)

            def mix(t, s, first=False, back=False):
                pe.wait_ge(S["z2_l_made"], t + 1)
                if not (isinstance(t, int) and t < 2):
                    pe.wait_ge(S["res_ready"], t - 1)
                if first:
                    for k in range(KD):
                        pe.wait_ge(S["wout_l_made"], k + 1)
                        for b in range(2):
                            c = slice(512 * b, 512 * (b + 1))
                            last = three(ps[2 * s + b][:], z2_h[s][:, k, :], z2_l[s][:, k, :], wout_h[:, k, c], wout_l[:, k, c], k == 0, k == KD - 1)
                else:
                    for b in range(2):
                        if back and b == 1:
                            h2_transposes(t - 2)
                        c = slice(512 * b, 512 * (b + 1))
                        for k in range(KD):
                            last = three(ps[2 * s + b][:], z2_h[s][:, k, :], z2_l[s][:, k, :], wout_h[:, k, c], wout_l[:, k, c], k == 0, k == KD - 1)
                last.then_inc(S["mix_made"], 1)

            def route(t):
                pe.wait_ge(S["h2T_copied"], t + 1)
                if not (isinstance(t, int) and t == 0):
                    pe.wait_ge(S["logit_read"], t)
                for k in range(KD):
                    last = mm(ps[6][:, 0:NG + NE], h2T[:, k, :], router_w[:, k, :], start=k == 0, stop=k == KD - 1)
                last.then_inc(S["logit_made"], 1)

            pe.wait_ge(S["b_copied"], NT)
            mix(0, 0, first=True)
            mix(1, 1)
            for t in (2, 3):
                mix(t, t - 2, back=True)
                route(t - 2)
            with pe.Fori(2, NT // 2) as i:
                for s in range(2):
                    mix(2 * i + s, s, back=True)
                    route(2 * i + s - 2)
            for t in (NT - 2, NT - 1):
                h2_transposes(t)
                route(t)

            pe.wait_ge(S["sel_ready"], 1)
            sel = both[:].rearrange("p t e -> p (t e)")
            mm(ps[0][:, 0:NT * NE], tri[:], sel, start=True, stop=True)
            mm(ps[1][:, 0:NT * NE], ones[:], sel, start=True, stop=True).then_inc(S["ranks_made"], 1)

            for c in range(2):
                pe.wait_ge(S["pick_ready"], c + 1)
                for t in range(NT):
                    last = mm(ps[7][:, 0:3 * TAB], pick_in[:, c, t, :], pick_v[:, c, t].rearrange("p v b -> p (v b)"),
                              start=c + t == 0, stop=c == 1 and t == NT - 1)
            last.then_inc(S["tab_made"], 1)

            def x_transposes(i):
                pe.wait_ge(S["gathered"], 16 * (i + 1))
                if not (isinstance(i, int) and i == 0):
                    pe.wait_ge(S["xT_l_made"], i)
                for k in range(KD):
                    last = nc.tensor.transpose(ps[2 + k // 4][:, (k % 4) * P:(k % 4 + 1) * P], xg[:, k * P:(k + 1) * P], ident[:])
                last.then_inc(S["xgT_made"], 1)

            def gate_up(i, e):
                pe.wait_ge(S["xT_l_made"], i + 1)
                if not (isinstance(i, int) and i == 0):
                    pe.wait_ge(S["act_ready"], i)
                for c in range(4):
                    pe.wait_ge(S["gu_split_l"], 4 * e + c + 1)
                    w_h, w_l = gu_slot(gu_h, e, c), gu_slot(gu_l, e, c)
                    for b in range(2):
                        n = slice(512 * b, 512 * (b + 1))
                        for k in range(2):
                            kk = 2 * c + k
                            last = three(ps[b][:], xT_h[:, kk, :], xT_l[:, kk, :], w_h[:, k, n], w_l[:, k, n], kk == 0, kk == KD - 1)
                    last.then_inc(S["gu_used"], 1)

            def a_transposes_e(i):
                pe.wait_ge(S["act_ready"], i + 1)
                if not (isinstance(i, int) and i == 0):
                    pe.wait_ge(S["aT_l_made"], i)
                for k in range(KE):
                    last = nc.tensor.transpose(ps[4][:, k * P:(k + 1) * P], act_a[:, k * P:(k + 1) * P], ident[:])
                last.then_inc(S["aT_e_made"], 1)

            def down(i, e):
                pe.wait_ge(S["aT_l_made"], i + 1)
                pe.wait_ge(S["y_ready"], i + 1)
                for c in range(2):
                    pe.wait_ge(S["dn_split_l"], 2 * e + c + 1)
                    w_h, w_l = dn_slot(dn_h, e, c), dn_slot(dn_l, e, c)
                    for b in range(2):
                        n = slice(512 * b, 512 * (b + 1))
                        for k in range(2):
                            kk = 2 * c + k
                            last = three(ps[5 + b][:], aT_h[:, kk, :], aT_l[:, kk, :], w_h[:, k, n], w_l[:, k, n], kk == 0, kk == KE - 1)
                    last.then_inc(S["dn_used"], 1)

            pe.wait_ge(S["tab_ready"], 1)
            pe.wait_ge(S["eid_ready"], 1)
            n_blocks = pe.value_load(block_n[0:1, 0:1], min_val=NE, max_val=MAXBLK)
            last_block = pe.value_load(block_n[0:1, 1:2], min_val=NE - 1, max_val=MAXBLK - 1)

            def expert_of(i):
                return pe.value_load(block_e[0:1, bass.ds(i, 1)], min_val=0, max_val=NE - 1)

            x_transposes(0)
            gate_up(0, 0)
            x_transposes(1)
            a_transposes_e(0)
            with pe.Fori(1, n_blocks) as i:
                e_before, e = expert_of(i - 1), expert_of(i)
                gate_up(i, e)
                x_transposes(i + 1)
                down(i - 1, e_before)
                a_transposes_e(i)
            down(last_block, NE - 1)

            def y_sum(i, slot):
                t, s = F_SLOTS * i + slot, slot % 2
                pe.wait_ge(y_loaded[slot], 32 * (i + 1))
                if not (isinstance(t, int) and t < 2):
                    pe.wait_ge(S["f_taken"], t - 1)
                for b in range(2):
                    n = slice(512 * b, 512 * (b + 1))
                    mm(ps[2 * s + b][:], ident[:], y0[slot][:, n], start=True, stop=False)
                    last = mm(ps[2 * s + b][:], ident[:], y1[slot][:, n], start=False, stop=True)
                last.then_inc(S["y_summed"], 1)

            for s in range(F_SLOTS):
                y_sum(0, s)
            with pe.Fori(1, NT // F_SLOTS) as i:
                for s in range(F_SLOTS):
                    y_sum(i, s)


INPUTS = ["x_prompt", "x_sample", "c_prompt", "c_sample", "w_ada", "b_ada", "w_in", "v_norm_g", "v_norm_b",
          "w_spatial", "b_spatial", "w_pool", "pool_scale", "w_out", "ln1_g", "ln1_b", "w_route_group",
          "b_route_group", "w_route_expert", "b_route_expert", "w_gate_up", "w_down", "ln2_g", "ln2_b"]
OUTPUTS = [(1, 512, D), (1, 1024, D)]


def kernel(**inputs):
    import numpy as np
    from concourse import bacc
    from concourse.bass_utils import run_bass_kernel_spmd

    nc = bacc.Bacc("TRN2", target_bir_lowering=False, num_devices=1)
    arrays, ins = {}, {}
    for name in INPUTS:
        a = np.ascontiguousarray(inputs[name])
        arrays[f"in_{name}"] = a
        ins[name] = nc.dram_tensor(f"in_{name}", a.shape, mybir.dt.from_np(a.dtype), kind="ExternalInput").ap()
    outs = [nc.dram_tensor(f"out_{i}", shape, F32, kind="ExternalOutput").ap() for i, shape in enumerate(OUTPUTS)]
    encoder(nc, ins, outs)
    r = run_bass_kernel_spmd(nc, [arrays], core_ids=[0])
    return tuple(r.results[0][f"out_{i}"] for i in range(len(outs)))
```
